# Optimizing a Trainium2 kernel written in Bass

```python
import jax, jax.numpy as jnp
from jax import lax
import numpy as np

D_MODEL = 1024
BATCH = 1
SEQ = 256
DEPTH = 1
DEC_BATCH = 1
DEC_SEQ = 1024
PAST_LEN = 512

GRID_W = 64
MLA_HEADS = 8
MLA_NOPE = 64
MLA_ROPE = 32
MLA_V = 64
Q_LORA = 768
KV_LORA = 256
ROPE_BASE = 10000.0
Q_BLOCK = 128
HG_HEADS = 4
HG_DK = 128
HG_DV = 128
HG_CHUNK = 32
N_EXPERTS = 16
EC_FACTOR = 2
D_EXPERT = 1024
ALPHA = (2 * DEPTH) ** 0.25
BETA = (8 * DEPTH) ** -0.25
EPS = 1e-6
IN_WIDTHS = (Q_LORA, KV_LORA, MLA_ROPE, HG_HEADS * HG_DK, HG_HEADS * HG_DK, HG_HEADS * HG_DK,
             HG_HEADS * HG_DV, HG_HEADS * HG_DV, D_MODEL, D_MODEL)
IN_W = sum(IN_WIDTHS)

kernel_name = 'hybrid_mla_hgrn2_ec_flow_step'

def rms_norm(x, g):
    xf = x.astype(jnp.float32)
    y = xf * lax.rsqrt(jnp.mean(xf * xf, axis=-1, keepdims=True) + EPS)
    return (y * g.astype(jnp.float32)).astype(x.dtype)

def layer_norm(x, g, b):
    xf = x.astype(jnp.float32)
    xc = xf - jnp.mean(xf, axis=-1, keepdims=True)
    var = jnp.mean(xc * xc, axis=-1, keepdims=True)
    y = xc * lax.rsqrt(var + EPS) * g.astype(jnp.float32) + b.astype(jnp.float32)
    return y.astype(x.dtype)

def adaln(cond, w_ada, b_ada):
    m = jax.nn.silu(cond) @ w_ada + b_ada
    return tuple(a[:, None, :] for a in jnp.split(m, 6, axis=-1))

def axial_rope(x, rows):
    n_freq = MLA_ROPE // 4
    inv = ROPE_BASE ** (-jnp.arange(n_freq, dtype=jnp.float32) / n_freq)
    t = jnp.arange(rows * GRID_W)
    r = (t // GRID_W).astype(jnp.float32)
    col = (t % GRID_W).astype(jnp.float32)
    ang = jnp.concatenate([r[:, None] * inv, col[:, None] * inv], axis=-1)
    cos = jnp.cos(ang)[None, :, None, :]
    sin = jnp.sin(ang)[None, :, None, :]
    xf = x.astype(jnp.float32)
    x1, x2 = xf[..., 0::2], xf[..., 1::2]
    out = jnp.stack([x1 * cos - x2 * sin, x1 * sin + x2 * cos], axis=-1).reshape(x.shape)
    return out.astype(x.dtype)

def forget_gate(z, lb):
    B, T, _ = z.shape
    f = lb + (1.0 - lb) * jax.nn.sigmoid(z.astype(jnp.float32))
    f = f.reshape(B, T, HG_HEADS, HG_DK)
    return jnp.log(f), 1.0 - f

def hgrn_chunk_scan(q, k, v, logf, s0):
    B, T, H, _ = q.shape
    n = T // HG_CHUNK

    def chunks(a):
        return a.reshape(B, n, HG_CHUNK, H, a.shape[-1]).astype(jnp.float32)

    qc, kc, vc, lf = chunks(q), chunks(k), chunks(v), chunks(logf)
    b = jnp.cumsum(lf, axis=2)
    b_last = b[:, :, -1]
    q_dec = qc * jnp.exp(b)
    k_dec = kc * jnp.exp(-b)
    causal = jnp.tril(jnp.ones((HG_CHUNK, HG_CHUNK), dtype=bool))
    a = jnp.where(causal, jnp.einsum('bnthk,bnshk->bnhts', q_dec, k_dec), 0.0)
    o_intra = jnp.einsum('bnhts,bnshv->bnthv', a, vc)
    k_end = kc * jnp.exp(b_last[:, :, None] - b)
    u = jnp.einsum('bnshk,bnshv->bnhkv', k_end, vc)

    def step(s, inp):
        decay, u_n = inp
        return jnp.exp(decay)[..., None] * s + u_n, s

    s_final, s_prev = lax.scan(step, s0.astype(jnp.float32), (b_last.swapaxes(0, 1), u.swapaxes(0, 1)))
    o_inter = jnp.einsum('bnthk,bnhkv->bnthv', q_dec, s_prev.swapaxes(0, 1))
    o = (o_intra + o_inter).reshape(B, T, H, v.shape[-1])
    return o.astype(q.dtype), s_final

def mla_up(c_kv, w_ukv):
    B, S, _ = c_kv.shape
    kv = (c_kv @ w_ukv).reshape(B, S, MLA_HEADS, MLA_NOPE + MLA_V)
    return kv[..., :MLA_NOPE], kv[..., MLA_NOPE:]

def mla_attend(q_nope, q_pe, k_nope, k_pe, v):
    B, T, H, _ = q_nope.shape
    nb = T // Q_BLOCK
    scale = (MLA_NOPE + MLA_ROPE) ** -0.5

    def blocks(a):
        return a.reshape(B, nb, Q_BLOCK, H, a.shape[-1]).swapaxes(0, 1)

    def one(qs):
        qn, qp = qs
        s = jnp.einsum('bqhd,bkhd->bhqk', qn, k_nope) + jnp.einsum('bqhr,bkr->bhqk', qp, k_pe)
        p = jax.nn.softmax(s.astype(jnp.float32) * scale, axis=-1).astype(v.dtype)
        return jnp.einsum('bhqk,bkhd->bqhd', p, v)

    o = lax.map(one, (blocks(q_nope), blocks(q_pe)))
    return o.swapaxes(0, 1).reshape(B, T, H * MLA_V)

def token_mixer(h, rows, ctx, lb, w_in, q_norm, w_uq, kv_norm, w_ukv, w_o_mla, hg_norm, w_o_hg, w_out):
    B, T, _ = h.shape
    offs = [int(o) for o in np.cumsum(IN_WIDTHS)[:-1]]
    cq, ckv_raw, kpe, hq, hf_fwd, hf_bwd, hi, hg, ga, gb = jnp.split(h @ w_in, offs, axis=-1)
    q = (rms_norm(cq, q_norm) @ w_uq).reshape(B, T, MLA_HEADS, MLA_NOPE + MLA_ROPE)
    q_nope, q_pe = q[..., :MLA_NOPE], q[..., MLA_NOPE:]
    c_kv = rms_norm(ckv_raw, kv_norm)
    k_nope, v = mla_up(c_kv, w_ukv)
    k_pe = kpe
    if rows is not None:
        q_pe = axial_rope(q_pe, rows)
        k_pe = axial_rope(kpe[:, :, None, :], rows)[:, :, 0, :]
    hg_q = jax.nn.silu(hq).reshape(B, T, HG_HEADS, HG_DK)
    hg_i = hi.reshape(B, T, HG_HEADS, HG_DV)
    logf_f, k_f = forget_gate(hf_fwd, lb[0])
    logf_b, k_b = forget_gate(hf_bwd, lb[1])
    if ctx is None:
        s_f0 = jnp.zeros((B, HG_HEADS, HG_DK, HG_DV), jnp.float32)
        s_b0 = s_f0
        keys_nope, keys_pe, vals = k_nope, k_pe, v
    else:
        ckv_c, kpe_c, s_f0, s_b0 = ctx
        kn_c, v_c = mla_up(ckv_c, w_ukv)
        keys_nope = jnp.concatenate([k_nope, kn_c], axis=1)
        keys_pe = jnp.concatenate([k_pe, kpe_c], axis=1)
        vals = jnp.concatenate([v, v_c], axis=1)
    o_mla = mla_attend(q_nope, q_pe, keys_nope, keys_pe, vals)
    o_f, s_f = hgrn_chunk_scan(hg_q, k_f, hg_i, logf_f, s_f0)
    o_b, s_b = hgrn_chunk_scan(jnp.flip(hg_q, axis=1), jnp.flip(k_b, axis=1), jnp.flip(hg_i, axis=1),
                               jnp.flip(logf_b, axis=1), s_b0)
    o_hg = rms_norm(o_f + jnp.flip(o_b, axis=1), hg_norm) * jax.nn.silu(hg.reshape(B, T, HG_HEADS, HG_DV))
    merged = (jax.nn.sigmoid(ga) * (o_mla @ w_o_mla)
              + jax.nn.sigmoid(gb) * (o_hg.reshape(B, T, HG_HEADS * HG_DV) @ w_o_hg))
    return merged @ w_out, (c_kv, k_pe, s_f.astype(h.dtype), s_b.astype(h.dtype))

def ec_ffn(h, w_router, w1, w3, w2):
    B, T, D = h.shape
    n = B * T
    cap = EC_FACTOR * n // N_EXPERTS
    xs = h.reshape(n, D)
    aff = jax.nn.softmax((xs @ w_router).astype(jnp.float32), axis=-1)
    gate, idx = lax.top_k(aff.T, cap)
    xe = xs[idx]
    hid = jax.nn.silu(jnp.einsum('ecd,edf->ecf', xe, w1)) * jnp.einsum('ecd,edf->ecf', xe, w3)
    ye = jnp.einsum('ecf,efd->ecd', hid, w2) * gate[..., None].astype(h.dtype)
    out = jnp.zeros_like(xs).at[idx.reshape(-1)].add(ye.reshape(-1, D))
    return out.reshape(B, T, D)

def trunk_layer(x, cond, rows, ctx, lb, w_ada, b_ada, w_in, q_norm, w_uq, kv_norm, w_ukv, w_o_mla,
                hg_norm, w_o_hg, w_out, ln1_g, ln1_b, w_router, w1, w3, w2, ln2_g, ln2_b):
    sh1, sc1, g1, sh2, sc2, g2 = adaln(cond, w_ada, b_ada)
    mix, ctx_out = token_mixer(x * (1.0 + sc1) + sh1, rows, ctx, lb, w_in, q_norm, w_uq, kv_norm, w_ukv,
                               w_o_mla, hg_norm, w_o_hg, w_out)
    x = layer_norm(ALPHA * x + g1 * mix, ln1_g, ln1_b)
    ffn = ec_ffn(x * (1.0 + sc2) + sh2, w_router, w1, w3, w2)
    x = layer_norm(ALPHA * x + g2 * ffn, ln2_g, ln2_b)
    return x, ctx_out

def setup_inputs(seed: int = 0) -> dict:
    key = jax.random.key(seed)
    ks = jax.random.split(key, 32)

    def nrm(k, shape, scale):
        return jax.random.normal(k, shape, jnp.float32) * scale

    hqk = MLA_HEADS * (MLA_NOPE + MLA_ROPE)
    hkv = MLA_HEADS * (MLA_NOPE + MLA_V)
    return {
        'x_prompt': nrm(ks[0], (BATCH, SEQ, D_MODEL), 1.0),
        'x_sample': nrm(ks[1], (DEC_BATCH, DEC_SEQ, D_MODEL), 1.0),
        'c': nrm(ks[2], (DEC_BATCH, D_MODEL), 1.0),
        'cache_ckv': nrm(ks[3], (DEC_BATCH, DEPTH, PAST_LEN, KV_LORA), 1.0),
        'cache_kpe': nrm(ks[4], (DEC_BATCH, DEPTH, PAST_LEN, MLA_ROPE), 1.0),
        'state_hgrn': nrm(ks[5], (DEC_BATCH, DEPTH, 2, HG_HEADS, HG_DK, HG_DV), 0.5),
        'c_ctx': nrm(ks[6], (D_MODEL,), 1.0),
        'w_ada': nrm(ks[7], (DEPTH, D_MODEL, 6 * D_MODEL), 0.5 * D_MODEL ** -0.5),
        'b_ada': nrm(ks[8], (DEPTH, 6 * D_MODEL), 0.01),
        'w_in': nrm(ks[9], (DEPTH, D_MODEL, IN_W), D_MODEL ** -0.5),
        'mla_q_norm': 1.0 + nrm(ks[10], (DEPTH, Q_LORA), 0.01),
        'mla_w_uq': nrm(ks[11], (DEPTH, Q_LORA, hqk), Q_LORA ** -0.5),
        'mla_kv_norm': 1.0 + nrm(ks[12], (DEPTH, KV_LORA), 0.01),
        'mla_w_ukv': nrm(ks[13], (DEPTH, KV_LORA, hkv), KV_LORA ** -0.5),
        'mla_w_o': nrm(ks[14], (DEPTH, MLA_HEADS * MLA_V, D_MODEL), (MLA_HEADS * MLA_V) ** -0.5),
        'hgrn_gamma': nrm(ks[15], (2, DEPTH + 1, HG_HEADS * HG_DK), 0.1),
        'hgrn_norm': 1.0 + nrm(ks[16], (DEPTH, HG_DV), 0.01),
        'hgrn_w_o': nrm(ks[17], (DEPTH, HG_HEADS * HG_DV, D_MODEL), (HG_HEADS * HG_DV) ** -0.5),
        'w_out': nrm(ks[18], (DEPTH, D_MODEL, D_MODEL), BETA * D_MODEL ** -0.5),
        'ln1_g': 1.0 + nrm(ks[19], (DEPTH, D_MODEL), 0.01),
        'ln1_b': nrm(ks[20], (DEPTH, D_MODEL), 0.01),
        'moe_w_router': nrm(ks[21], (DEPTH, D_MODEL, N_EXPERTS), D_MODEL ** -0.5),
        'moe_w1': nrm(ks[22], (DEPTH, N_EXPERTS, D_MODEL, D_EXPERT), D_MODEL ** -0.5),
        'moe_w3': nrm(ks[23], (DEPTH, N_EXPERTS, D_MODEL, D_EXPERT), D_MODEL ** -0.5),
        'moe_w2': nrm(ks[24], (DEPTH, N_EXPERTS, D_EXPERT, D_MODEL), BETA * D_EXPERT ** -0.5),
        'ln2_g': 1.0 + nrm(ks[25], (DEPTH, D_MODEL), 0.01),
        'ln2_b': nrm(ks[26], (DEPTH, D_MODEL), 0.01),
    }

def reference(x_prompt, x_sample, c, cache_ckv, cache_kpe, state_hgrn, c_ctx, w_ada, b_ada, w_in,
              mla_q_norm, mla_w_uq, mla_kv_norm, mla_w_ukv, mla_w_o, hgrn_gamma, hgrn_norm, hgrn_w_o,
              w_out, ln1_g, ln1_b, moe_w_router, moe_w1, moe_w3, moe_w2, ln2_g, ln2_b):
    lb_all = jnp.cumsum(jax.nn.softmax(hgrn_gamma.astype(jnp.float32), axis=1), axis=1)
    rows = x_sample.shape[1] // GRID_W
    y_prompt = x_prompt
    y_sample = x_sample
    ckv_list, kpe_list, st_list = [], [], []
    for l in range(DEPTH):
        weights = (w_ada[l], b_ada[l], w_in[l], mla_q_norm[l], mla_w_uq[l], mla_kv_norm[l], mla_w_ukv[l],
                   mla_w_o[l], hgrn_norm[l], hgrn_w_o[l], w_out[l], ln1_g[l], ln1_b[l], moe_w_router[l],
                   moe_w1[l], moe_w3[l], moe_w2[l], ln2_g[l], ln2_b[l])
        lb = lb_all[:, l]
        y_prompt, (ckv_p, kpe_p, sf_p, sb_p) = trunk_layer(y_prompt, c_ctx[None], None, None, lb, *weights)
        ckv_list.append(ckv_p)
        kpe_list.append(kpe_p)
        st_list.append(jnp.stack([sf_p, sb_p], axis=1))
        ctx = (cache_ckv[:, l], cache_kpe[:, l], state_hgrn[:, l, 0], state_hgrn[:, l, 1])
        y_sample, _ = trunk_layer(y_sample, c, rows, ctx, lb, *weights)
    new_ckv = jnp.stack(ckv_list, axis=1)
    new_kpe = jnp.stack(kpe_list, axis=1)
    new_state_hgrn = jnp.stack(st_list, axis=1)
    return (y_prompt, y_sample, new_ckv, new_kpe, new_state_hgrn)


_drawn_inputs = setup_inputs


def setup_inputs(seed=0):
    import zlib

    import numpy as np

    out = dict(_drawn_inputs(seed))
    spreads = {}
    factors = {'cache_ckv': 8.0,
     'cache_kpe': 8.0,
     'state_hgrn': 64.0,
     'b_ada': 2.732,
     'mla_q_norm': 8.0,
     'mla_w_uq': 7.076,
     'mla_kv_norm': 5.963,
     'mla_w_ukv': 2.839,
     'mla_w_o': 2.806,
     'hgrn_norm': 64.0,
     'ln1_g': 18.705,
     'ln1_b': 20.926,
     'ln2_g': 31.045,
     'ln2_b': 31.382}
    for name, (base, spread) in spreads.items():
        noise = np.random.default_rng([zlib.crc32(name.encode()), seed]).standard_normal(out[name].shape)
        drawn = base * np.exp(spread * noise) if base else spread * noise
        out[name] = __import__('jax').numpy.asarray(drawn.astype(out[name].dtype))
    for name, factor in factors.items():
        out[name] = (out[name] * factor).astype(out[name].dtype)
    return out
```

```python
import concourse.bass as bass
from concourse import mybir
from contextlib import ExitStack

P = 128
D = 1024
DK = D // P
LAT, CTX, PAST = 1024, 256, 512
TOK = LAT + CTX
KEYS = LAT + PAST + CTX
BLK = TOK // P
LBLK, PBLK = LAT // P, PAST // P
HEADS, NOPE, ROPE, VD = 8, 64, 32, 64
QKD = NOPE + ROPE
QL, KVL = 768, 256
QT_, KT_ = QL // P, KVL // P
HG, CHUNK = 4, 32
HLINKS = 2 * 4 + 2 * 20 + 2
CPB = P // CHUNK
EXPERTS = 16
CAPL, CAPC = 2 * LAT // EXPERTS, 2 * CTX // EXPERTS
CAP = CAPL + CAPC
ALPHA = 2.0 ** 0.25
EPS = 1e-6
SCALE = float(QKD) ** -0.5
GRID_W = 64
UNIT = 256
O_CQ, O_CKV, O_KPE = 0, QL, QL + KVL
O_HQ = O_KPE + ROPE
O_HF, O_HB, O_HI, O_HG = (O_HQ + n * HG * P for n in range(1, 5))
O_GA = O_HG + HG * P
O_GB = O_GA + D
TCH = [(0, 512), (512, 512), (1024, 256)]
VROWS = 89
R_BADA, R_C, R_QN, R_KVN, R_HN, R_GAM = 0, 48, 64, 70, 72, 73


class Chain:

    def __init__(self, eng, sem):
        self.eng, self.sem, self.n, self.reg, self.per = eng, sem, 0, None, 0

    def link(self, ins):
        ins.then_inc(self.sem, 1)
        self.n += 1
        self.eng.wait_ge(self.sem, self.n if self.reg is None else self.reg * self.per + self.n)

    def enter(self, reg, per, first=0):
        self.n -= first * per
        self.reg, self.per, self.at = reg, per, self.n

    def leave(self, times):
        assert self.n - self.at == self.per, (self.n - self.at, self.per)
        self.n, self.reg = self.at + times * self.per, None


def flow_step(nc, x_prompt, x_sample, c, cache_ckv, cache_kpe, state_hgrn, c_ctx, w_ada, b_ada, w_in,
              q_norm, w_uq, kv_norm, w_ukv, w_o_mla, gamma, hg_norm, w_o_hg, w_out, ln1_g, ln1_b,
              w_router, w1, w3, w2, ln2_g, ln2_b, tables, rope, y_prompt, y_sample, new_ckv, new_kpe,
              new_state):
    F32, U32 = mybir.dt.float32, mybir.dt.uint32
    ALU, ACT, AX = mybir.AluOpType, mybir.ActivationFunctionType, mybir.AxisListType

    ctx = ExitStack()
    with ctx:
        def sem(name):
            return ctx.enter_context(nc.semaphore(name))

        WORDS = 53184
        arena = ctx.enter_context(nc.sbuf_tensor("arena", [P, WORDS], F32))
        ps = ctx.enter_context(nc.psum_tensor("ps", [P, 8, 512], F32))
        mod_rows = nc.dram_tensor("mod_rows", [96, P], F32, kind="Internal").ap()
        h2_rows = nc.dram_tensor("h2_rows", [TOK, D], F32, kind="Internal").ap()
        acc_rows = nc.dram_tensor("acc_rows", [TOK, D], F32, kind="Internal").ap()

        def at(off, *dims):
            size = 1
            for d in dims:
                size *= d
            assert off + size <= WORDS, (off, dims)
            v = arena[:, off:off + size]
            if len(dims) == 2:
                v = v.rearrange("p (a b) -> p a b", b=dims[1])
            if len(dims) == 3:
                v = v.rearrange("p (a b c) -> p a b c", b=dims[1], c=dims[2])
            return v

        K0 = 50000
        ident, ones = at(K0, P), at(K0 + 128, P)
        masks = at(K0 + 256, 2, P)
        modv = at(K0 + 512, 2, 48)
        vcol = at(K0 + 608, VROWS + 7)
        scond = at(K0 + 704, DK, 2)
        lb, oml, noml = at(K0 + 720, 2, HG), at(K0 + 728, 2, HG), at(K0 + 736, 2, HG)
        eps = at(K0 + 744, 1)
        small = at(K0 + 752, 48)
        rope_t = at(K0 + 816, 2, LAT)
        assert K0 + 816 + 2 * LAT <= WORDS
        hT = at(0, DK, TOK)
        xin = [at(10240 + 1024 * s, D) for s in range(2)]
        cache_t, ckpe_t = at(12288, PBLK, KVL), at(13312, PBLK, QKD)
        kpc, nck, nkp = at(13696, CTX), at(13952, 2, KVL), at(14464, 2, QKD)
        vrow = at(14656, P)
        mrow = at(14784, P)
        o_tok = at(10240, BLK, HEADS * VD)
        cq = at(15360, QT_, TOK)
        ring = [at(23040 + 2048 * s, DK, UNIT) for s in range(4)]
        prob = [at(23040 + 1536 * s, 1536) for s in range(2)]
        probT = [at(26112 + 1536 * s, 12, P) for s in range(2)]
        ckn = at(31232, KT_, KEYS)
        val = at(34816, KEYS // P, HEADS * VD)
        wkpe = at(34816, DK, QKD)
        kT, qT = at(41984, KEYS), at(43776, TOK)
        rsk, rsq = at(43776, TOK), at(45056, TOK)
        wuq, wukk = at(46336, QT_, QKD), at(46912, KT_, NOPE)
        wukv = at(47040, KT_, HEADS, VD)
        sqr = [at(48064 + 512 * s, 512) for s in range(3)]
        rtmp = at(48064, LAT)
        om = at(15360, HG, TOK)

        att = at(K0 + 800, 16)
        hw = [at(20480 + 1024 * s, DK, P) for s in range(5)]
        hq, hgate = at(25600, TOK), at(26880, TOK)
        kd, bd, ed, ke = ([at(28160 + 5120 * d + 1280 * n, TOK) for d in range(2)] for n in range(4))
        vh, vx = at(38400, BLK, P), at(39680, BLK, CPB, P)
        sring = [at(44800 + P * n, P) for n in range(16)]
        am = [at(46848 + P * n, P) for n in range(2)]
        ket = [at(47104 + P * n, P) for n in range(2)]
        st0, fin = at(47360, 2, P), at(47616, 2, P)
        reset = at(47872, TOK)
        dec = at(49152, 2, TOK // CHUNK)
        oh = at(10240, HG * TOK)

        gw = [at(20480 + 3072 * s, 24, P) for s in range(2)]
        mt = at(26624, DK * TOK)
        wout = at(36864, DK, D)
        gate_a = [at(45056 + 1024 * s, 512) for s in range(2)]
        gate_b = [at(45568 + 1024 * s, 512) for s in range(2)]
        g1b, scb, shb = ([at(2048 * n + 1024 * g, D) for g in range(2)] for n in range(3))
        ln1gb, ln1bb = at(6144, D), at(7168, D)
        xt, zt, zn, xa, h2 = ([at(8192 + 2048 * n + 1024 * s, D) for s in range(2)] for n in range(5))
        h2T = [at(18432 + 1024 * s, DK, P) for s in range(2)]
        wrt = at(49280, DK, EXPERTS)
        affp = [at(49408 + 48 * s, 48) for s in range(2)]
        st5 = at(49504, 64)
        ex5 = at(49568, EXPERTS)
        aff = at(45056, LAT)
        topv, topi, topf = at(46080, P), at(46208, P), at(46336, P)
        gates, rowi = at(49600, 48), at(49648, 48)
        slots = [20480, 22528, 24576, 47104] + [26624 + 2048 * n for n in range(8)]
        wslot = [at(o, DK, UNIT) for o in slots]
        xl, xc, xeT = at(0, D), at(1024, D), at(2048, DK, CAP)
        hid, yt = at(3328, DK, CAP), at(4608, DK, CAP)
        slu = [at(5888 + CAP * s, CAP) for s in range(2)]
        yl, yc = at(6400, D), at(7424, D)
        idx_g, idx_s, gate_s = at(49696, 2), at(49700, 2), at(49704, 2)
        ln2gb, ln2bb = at(10240, D), at(11264, D)
        at_, zt8 = [at(12288 + 1024 * s, D) for s in range(3)], [at(15360 + 1024 * s, D) for s in range(3)]
        st8 = at(49712, 3 * 18)

        vec_in, tab_in = sem("vec_in"), sem("tab_in")
        memsets = sem("memsets")
        vrow_t, vcol_rd, scond_rd = sem("vrow_transposed"), sem("vcol_ready"), sem("scond_ready")
        ring_in = [sem(f"ring_in{s}") for s in range(4)]
        unit_used = sem("unit_used")
        mod_rd = sem("mod_ready")
        xin_in = [sem(f"xin_in{s}") for s in range(2)]
        xt_done, h_dve, h_act = sem("x_transposed"), sem("h_by_dve"), sem("h_by_act")
        dve_chain, act_chain, pool_chain = sem("dve_chain"), sem("act_chain"), sem("pool_chain")
        pr_mm, pr_dve, pr_act, ssq_mm, rs_read = (sem(n) for n in (
            "proj_matmuls", "proj_by_dve", "proj_squared", "ssq_matmuls", "ssq_read"))
        rs_rd = sem("rstd_ready")
        wkpe_in, cache_in, wukv_in = sem("wkpe_in"), sem("cache_in"), sem("wukv_in")
        ex_mm, ex_dve, v_act = sem("extra_matmuls"), sem("extra_by_dve"), sem("values_by_act")
        outs = sem("stores_done")
        mr_mm, mr_rd, mr_out = sem("mod_transposed"), sem("mod_rows_ready"), sem("mod_rows_stored")

        wq_in, qkv_mm, q_rd, k_rd = sem("wq_in"), sem("qk_proj_matmuls"), sem("q_ready"), sem("k_ready")
        s_mm, nb_rd, p_rd, t_mm = sem("score_matmuls"), sem("neg_max_ready"), sem("probs_ready"), sem("probs_transposed")
        pt_dve, pt_act, pv_mm, o_ev = sem("probsT_by_dve"), sem("probsT_by_act"), sem("pv_matmuls"), sem("o_evacuated")
        om_mm, om_dve, om_act = sem("om_transposed"), sem("om_by_dve"), sem("om_by_act")
        hw_in = [sem(f"head_weights_in{n}") for n in range(5)]
        st_in, s_init, fin_rd, fin_out = sem("state_in"), sem("state_taken"), sem("final_ready"), sem("final_stored")
        hp_mm, hp_act, ln_rd, cs_rd, e_rd, hg_rd, vx_rd = (sem(n) for n in (
            "head_proj_matmuls", "head_proj_by_act", "logf_ready", "cumsum_ready", "exp_ready",
            "decayed_ready", "vx_ready"))
        kt_mm, a_mm, u_mm, oo_mm = sem("kend_transposed"), sem("a_matmuls"), sem("u_matmuls"), sem("o_matmuls")
        ket_rd, am_rd, st_rd, u_free, of_ev, ob_ev = (sem(n) for n in (
            "ket_ready", "am_ready", "states_ready", "u_read", "o_fwd_evacuated", "o_bwd_added"))
        sq_rd, hss_mm, hs_read, tail_rd = sem("head_squares"), sem("head_ssq"), sem("head_ssq_read"), sem("head_done")

        gw_in = [sem(f"merge_weights_in{n}") for n in range(2)]
        mg_mm, mg_sig, mg_ev = sem("merge_matmuls"), sem("merge_gates"), sem("merged")
        wout_in, bc_in, x_in = sem("wout_in"), sem("broadcasts_in"), [sem(f"x_in{n}") for n in range(2)]
        wo_mm, z_rd, z_sum, var_rd, sd_rd, nm_rd, zn_rd, zg_rd, x1_rd = (sem(n) for n in (
            "out_proj_matmuls", "mix_read", "z_summed", "variance_ready", "deviation_ready", "norm_scale_ready",
            "normed", "norm_gained", "x1_ready"))
        hs_rd, h2_rd, xa_rd, pads = sem("h2_scaled"), sem("h2_ready"), sem("xa_ready"), sem("paddings")
        h2_out, acc_out = [sem(f"h2_stored{n}") for n in range(2)], [sem(f"acc_stored{n}") for n in range(2)]
        ht_mm, ht_ev, lg_mm, lmax_rd, lexp_rd, af_rd, af_mm, af_ev = (sem(n) for n in (
            "h2_transposed", "h2T_ready", "logits_matmuls", "logits_max", "logits_exp", "affinity_ready",
            "affinity_transposed", "affinity_in_rows"))
        top_rd, top_mm, top_ev = sem("top_ready"), sem("top_transposed"), sem("top_columns")
        w_slot_in = [sem(f"expert_weights_in{n}") for n in range(12)]
        ix_rd, xg_in, xe_mm, xe_ev = sem("index_ready"), sem("tokens_gathered"), sem("tokens_transposed"), sem("xeT_ready")
        up_mm, sl_rd, hid_ev, dn_mm = sem("up_matmuls"), sem("silu_ready"), sem("hidden_ready"), sem("down_matmuls")
        yt_act, yt_dve, yb_mm, gs_rd = sem("yt_by_act"), sem("yt_by_dve"), sem("y_transposed"), sem("gates_taken")
        yl_rd, yc_rd, sc_out = sem("latents_y_ready"), sem("context_y_ready"), sem("scattered")
        ln2_in, a_in, y_out = sem("ln2_in"), [sem(f"acc_in{n}") for n in range(3)], [sem(f"y_stored{n}") for n in range(3)]

        passed = sem("loop_waits_passed")

        block = ctx.enter_context(nc.Block())

        def chunk(t, n):
            return t[:, TCH[n][0]:TCH[n][0] + TCH[n][1]]

        W_IN = w_in[0].rearrange("(k p) n -> p k n", p=P)
        W_ADA = w_ada[0].rearrange("(k p) n -> p k n", p=P)
        W_UQ = w_uq[0].rearrange("(k p) n -> p k n", p=P)
        W_UKV = w_ukv[0].rearrange("(k p) n -> p k n", p=P)
        HCOLS = (O_HI, O_HF, O_HB, O_HG, O_HQ)
        W_OM = w_o_mla[0].rearrange("(k p) n -> p k n", p=P)
        W_OH = w_o_hg[0].rearrange("(k p) n -> p k n", p=P)
        NPR = 27

        def pr_free(eng, i):
            j = i - 5
            if j < 0:
                return
            if j < 24:
                eng.wait_ge(pr_act, j + 1)
            elif j < NPR:
                eng.wait_ge(pr_dve, j + 1)
            elif j < NPR + 5:
                eng.wait_ge(ex_dve, j - NPR + 1)
            else:
                eng.wait_ge(v_act, j - NPR - 5 + 1)

        QB = BLK

        def tiles_before(j):
            return 3 * j if j < LBLK else 3 * LBLK + (j - LBLK)

        TPH = tiles_before(QB) // 2

        def steps(d):
            return list(range(BLK)) if d == 0 else [*range(LBLK - 1, -1, -1), *range(BLK - 1, LBLK - 1, -1)]

        SEQ = [(d, b) for d in range(2) for b in steps(d)]
        NS = len(SEQ)

        def after_loop_wait(eng):
            eng.sem_inc(passed, 1)

        @block.sync
        def _(sp):
            for r, n, src in ((R_BADA, 48, b_ada.rearrange("a (r p) -> (a r) p", p=P)),
                              (R_C, 8, c.rearrange("a (r p) -> (a r) p", p=P)),
                              (R_C + 8, 8, c_ctx.rearrange("(r p) -> r p", p=P)),
                              (R_QN, 6, q_norm.rearrange("a (r p) -> (a r) p", p=P)),
                              (R_KVN, 2, kv_norm.rearrange("a (r p) -> (a r) p", p=P)),
                              (R_HN, 1, hg_norm),
                              (R_GAM, 16, gamma.rearrange("a b (r p) -> (a b r) p", p=P))):
                sp.dma_start(vrow[r:r + n, :], src).then_inc(vec_in, 16)
            sp.dma_start(ident, tables[:, 0:P]).then_inc(tab_in, 16)
            sp.dma_start(masks, tables[:, P:3 * P].rearrange("p (a b) -> p a b", b=P)).then_inc(tab_in, 16)
            sp.dma_start(rope_t[NOPE:QKD, :, :], rope).then_inc(tab_in, 16)
            for s in range(4):
                sp.dma_start(ring[s], W_ADA[:, :, s * UNIT:(s + 1) * UNIT]).then_inc(ring_in[s], 16)
            sp.dma_start(xin[0], x_sample[0, 0:P, :]).then_inc(xin_in[0], 16)
            sp.dma_start(xin[1], x_sample[0, P:2 * P, :]).then_inc(xin_in[1], 16)
            for s in range(4):
                sp.wait_ge(unit_used, s + 1)
                sp.dma_start(ring[s], W_ADA[:, :, (s + 4) * UNIT:(s + 5) * UNIT]).then_inc(ring_in[s], 16)
            for s in range(4):
                sp.wait_ge(unit_used, s + 5)
                sp.dma_start(ring[s], W_IN[:, :, s * UNIT:(s + 1) * UNIT]).then_inc(ring_in[s], 16)
            sp.dma_start(wkpe, W_IN[:, :, O_KPE - NOPE:O_KPE + ROPE]).then_inc(wkpe_in, 16)
            sp.dma_start(cache_t, cache_ckv[0, 0].rearrange("(b p) f -> p b f", p=P)).then_inc(cache_in, 16)
            sp.wait_ge(memsets, 4)
            sp.dma_start(ckpe_t[:, :, NOPE:QKD],
                         cache_kpe[0, 0].rearrange("(b p) f -> p b f", p=P)).then_inc(cache_in, 16)
            for k in range(KT_):
                sp.dma_start(wukv[:, k], w_ukv[0, k * P:(k + 1) * P, :]
                             .rearrange("p (h e) -> p h e", e=NOPE + VD)[:, :, NOPE:]).then_inc(wukv_in, 16)
            sp.dma_start(wuq, W_UQ[:, :, 0:QKD]).then_inc(wq_in, 16)
            sp.dma_start(wukk, W_UKV[:, :, 0:NOPE]).then_inc(wq_in, 16)
            for b in range(2, BLK):
                sp.wait_ge(xt_done, 2 * (b - 1))
                src = x_sample[0, b * P:(b + 1) * P, :] if b < LBLK else \
                    x_prompt[0, (b - LBLK) * P:(b - LBLK + 1) * P, :]
                sp.dma_start(xin[b % 2], src).then_inc(xin_in[b % 2], 16)
            with sp.Fori(0, 4) as i:
                for s in range(4):
                    sp.wait_ge(unit_used, 4 * i + s + 9)
                    sp.dma_start(ring[s], W_ADA[:, :, bass.ds((4 * i + s + 8) * UNIT, UNIT)])\
                        .then_inc(ring_in[s], 16)
            sp.wait_ge(ex_dve, 4)
            sp.dma_start(new_ckv[0, 0].rearrange("(b p) f -> p b f", p=P), nck).then_inc(outs, 16)
            sp.wait_ge(ex_dve, 5)
            sp.dma_start(new_kpe[0, 0].rearrange("(b p) f -> p b f", p=P),
                         nkp[:, :, NOPE:QKD]).then_inc(outs, 16)
            sp.wait_ge(mr_rd, 1)
            sp.dma_start(mod_rows, mrow[0:96, :]).then_inc(mr_out, 16)
            with sp.Fori(1, HEADS) as h:
                sp.wait_ge(qkv_mm, 2 * h)
                sp.dma_start(wuq, W_UQ[:, :, bass.ds(h * QKD, QKD)]).then_inc(wq_in, 16)
                sp.dma_start(wukk, W_UKV[:, :, bass.ds(h * (NOPE + VD), NOPE)]).then_inc(wq_in, 16)
            sp.sem_inc(fin_out, 16)
            sp.wait_ge(om_mm, 1)
            for n, col in enumerate(HCOLS):
                sp.dma_start(hw[n], W_IN[:, :, col:col + P]).then_inc(hw_in[n], 16)
            sp.dma_start(st0, state_hgrn[0, 0, :, 0].rearrange("d k v -> k d v")).then_inc(st_in, 16)
            with sp.Fori(1, HG) as h:
                for n, col in enumerate(HCOLS):
                    sp.wait_ge(hp_mm, 15 * h - 12 + 3 * n)
                    sp.dma_start(hw[n], W_IN[:, :, bass.ds(col + h * P, P)]).then_inc(hw_in[n], 16)
                sp.wait_ge(s_init, 2 * h)
                sp.dma_start(st0, state_hgrn[0, 0, :, bass.ds(h, 1)].rearrange("d a k v -> k d (a v)"))\
                    .then_inc(st_in, 16)
                sp.wait_ge(fin_rd, 2 * h)
                sp.dma_start(new_state[0, 0, :, bass.ds(h - 1, 1)].rearrange("d a k v -> k d (a v)"), fin)\
                    .then_inc(fin_out, 16)
            sp.wait_ge(fin_rd, 2 * HG)
            sp.dma_start(new_state[0, 0, :, HG - 1].rearrange("d k v -> k d v"), fin).then_inc(fin_out, 16)

            def merge_weights(s, col):
                sp.dma_start(gw[s][:, 0:8, :], W_IN[:, :, bass.ds(O_GA + col, P)]).then_inc(gw_in[s], 16)
                sp.dma_start(gw[s][:, 8:16, :], W_IN[:, :, bass.ds(O_GB + col, P)]).then_inc(gw_in[s], 16)
                sp.dma_start(gw[s][:, 16:20, :], W_OM[:, :, bass.ds(col, P)]).then_inc(gw_in[s], 16)
                sp.dma_start(gw[s][:, 20:24, :], W_OH[:, :, bass.ds(col, P)]).then_inc(gw_in[s], 16)

            sp.wait_ge(hg_rd, 2 * HG)
            for s in range(2):
                merge_weights(s, s * P)
            sp.wait_ge(sq_rd, HG)
            sp.dma_start(wout, w_out[0].rearrange("(k p) n -> p k n", p=P)).then_inc(wout_in, 16)
            with sp.Fori(1, DK // 2) as i:
                for s in range(2):
                    sp.wait_ge(mg_mm, 6 * i + 3 * s - 3)
                    merge_weights(s, (2 * i + s) * P)

            def mod_row(g, j):
                return mod_rows[g * 48 + j * 8:g * 48 + j * 8 + 8, :].rearrange("(o a) p -> o (a p)", o=1)\
                    .to_broadcast([P, D])

            sp.wait_ge(mg_mm, 24)
            sp.wait_ge(mr_out, 16)
            for g in range(2):
                sp.dma_start(g1b[g], mod_row(g, 2)).then_inc(bc_in, 16)
                sp.dma_start(shb[g], mod_row(g, 3)).then_inc(bc_in, 16)
                sp.dma_start(scb[g], mod_row(g, 4)).then_inc(bc_in, 16)
            sp.dma_start(ln1gb, ln1_g.to_broadcast([P, D])).then_inc(bc_in, 16)
            sp.dma_start(ln1bb, ln1_b.to_broadcast([P, D])).then_inc(bc_in, 16)
            sp.dma_start(wrt, w_router[0].rearrange("(k p) e -> p k e", p=P)).then_inc(bc_in, 16)

            def token_rows(b, lat, con):
                return lat[0, b * P:(b + 1) * P, :] if b < LBLK else con[0, (b - LBLK) * P:(b - LBLK + 1) * P, :]

            for b in range(2):
                sp.dma_start(xt[b], token_rows(b, x_sample, x_prompt)).then_inc(x_in[b], 16)
            W = [w1, w3]
            def up_src(e, u, which):
                return W[which][0, e].rearrange("(k p) n -> p k n", p=P)[:, :, u * UNIT:(u + 1) * UNIT]

            for n in range(4):
                sp.dma_start(wslot[n], up_src(0, n // 2, n % 2)).then_inc(w_slot_in[n], 16)
            for b in range(BLK):
                sp.wait_ge(x1_rd, b + 1)
                sp.wait_ge(xa_rd, b + 1)
                sp.dma_start(acc_rows[b * P:(b + 1) * P, :], xa[b % 2]).then_inc(acc_out[b % 2], 16)
                sp.wait_ge(h2_rd, b + 1)
                sp.dma_start(h2_rows[b * P:(b + 1) * P, :], h2[b % 2]).then_inc(h2_out[b % 2], 16)
                if b + 2 < BLK:
                    sp.wait_ge(z_sum, b + 1)
                    sp.dma_start(xt[b % 2], token_rows(b + 2, x_sample, x_prompt)).then_inc(x_in[b % 2], 16)
            for n in range(4, 8):
                sp.dma_start(wslot[n], up_src(0, n // 2, n % 2)).then_inc(w_slot_in[n], 16)
            for n in range(4):
                sp.dma_start(wslot[8 + n], w2[0, 0].rearrange("(k p) n -> p k n", p=P)
                             [:, :, n * UNIT:(n + 1) * UNIT]).then_inc(w_slot_in[8 + n], 16)
            sp.wait_ge(top_ev, 2)
            sp.dma_start(ln2gb, ln2_g.to_broadcast([P, D])).then_inc(ln2_in, 16)
            sp.dma_start(ln2bb, ln2_b.to_broadcast([P, D])).then_inc(ln2_in, 16)
            with sp.Fori(1, EXPERTS) as e:
                for n in range(8):
                    if n % 2 == 0:
                        sp.wait_ge(up_mm, 8 * e + n - 6)
                    src = W[n % 2][0, bass.ds(e, 1)].rearrange("a (k p) n -> p (a k) n", p=P)
                    sp.dma_start(wslot[n], src[:, :, (n // 2) * UNIT:(n // 2 + 1) * UNIT]).then_inc(w_slot_in[n], 16)
                for n in range(4):
                    sp.wait_ge(dn_mm, 8 * e + 2 * n - 6)
                    src = w2[0, bass.ds(e, 1)].rearrange("a (k p) n -> p (a k) n", p=P)
                    sp.dma_start(wslot[8 + n], src[:, :, n * UNIT:(n + 1) * UNIT]).then_inc(w_slot_in[8 + n], 16)

            sp.wait_ge(sc_out, 32 * EXPERTS)
            for b in range(BLK + 1):
                if b < BLK:
                    if b >= 3:
                        sp.wait_ge(zn_rd, BLK + b - 2)
                    sp.dma_start(at_[b % 3], acc_rows[b * P:(b + 1) * P, :]).then_inc(a_in[b % 3], 16)
                if b >= 1:
                    sp.wait_ge(x1_rd, BLK + b)
                    sp.dma_start(token_rows(b - 1, y_sample, y_prompt), zt8[(b - 1) % 3])\
                        .then_inc(y_out[(b - 1) % 3], 16)
            for n in range(3):
                sp.wait_ge(y_out[n], 16 * len(range(n, BLK, 3)))
            sp.wait_ge(outs, 32)
            sp.wait_ge(fin_out, 16 * (HG + 1))

        @block.tensor
        def _(pe):
            pe.wait_ge(vec_in, 16 * 7)
            pe.wait_ge(tab_in, 16 * 3)
            pe.transpose(ps[:, 0, 0:VROWS], vrow[0:VROWS, :], ident[0:VROWS, 0:VROWS]).then_inc(vrow_t, 1)

            def ada_unit(u, s, bank):
                for o in range(2):
                    for k in range(DK):
                        last = pe.matmul(ps[:, bank, bass.ds((u * 2 + o) * 2, 2)] if not isinstance(u, int)
                                         else ps[:, bank, (u * 2 + o) * 2:(u * 2 + o) * 2 + 2],
                                         ring[s][:, k, o * P:(o + 1) * P], scond[:, k, :],
                                         start=(k == 0), stop=(k == DK - 1))
                last.then_inc(unit_used, 1)

            pe.wait_ge(scond_rd, 1)
            for u in range(8):
                pe.wait_ge(ring_in[u % 4], 16 * (u // 4 + 1))
                ada_unit(u, u % 4, 0)

            for b in range(BLK):
                pe.wait_ge(xin_in[b % 2], 16 * (b // 2 + 1))
                for half in range(2):
                    bank = 1 + 2 * (b % 2) + half
                    if b >= 2:
                        pe.wait_ge(h_act if half else h_dve, b - 1)
                    for q in range(4):
                        k = half * 4 + q
                        last = pe.transpose(ps[:, bank, q * P:(q + 1) * P], xin[b % 2][:, k * P:(k + 1) * P],
                                            ident)
                    last.then_inc(xt_done, 1)

            pe.wait_ge(h_act, BLK)
            pe.wait_ge(h_dve, BLK)
            pe.wait_ge(memsets, 1)

            def sums(o):
                for n in range(3):
                    i = o * 3 + n
                    pe.wait_ge(pr_act, i + 1)
                    if o >= QT_:
                        pe.wait_ge(rs_read, 3)
                    pe.matmul(ps[:, 5 + n, 0:TCH[n][1]], ones, sqr[i % 3][:, 0:TCH[n][1]],
                              start=(o in (0, QT_)), stop=(o in (QT_ - 1, QT_ + KT_ - 1))).then_inc(ssq_mm, 1)

            for o in range(QT_ + KT_):
                s = o // 2
                if o % 2 == 0:
                    pe.wait_ge(ring_in[s], 48)
                for n in range(3):
                    pr_free(pe, o * 3 + n)
                    for k in range(DK):
                        last = pe.matmul(ps[:, (o * 3 + n) % 5, 0:TCH[n][1]],
                                         ring[s][:, k, (o % 2) * P:(o % 2 + 1) * P], chunk(hT[:, k], n),
                                         start=(k == 0), stop=(k == DK - 1))
                    last.then_inc(pr_mm, 1)
                if o % 2 == 1:
                    pe.wait_ge(pr_mm, o * 3 + 3)
                    pe.sem_inc(unit_used, 1)
                if o >= 1:
                    sums(o - 1)
            pe.wait_ge(wkpe_in, 16)
            for n in range(3):
                pr_free(pe, 24 + n)
                for k in range(DK):
                    last = pe.matmul(ps[0:QKD, (24 + n) % 5, 0:TCH[n][1]], wkpe[:, k, :], chunk(hT[:, k], n),
                                     start=(k == 0), stop=(k == DK - 1))
                last.then_inc(pr_mm, 1)
            sums(QT_ + KT_ - 1)

            pe.wait_ge(cache_in, 32)
            for j in range(2):
                pr_free(pe, NPR + j)
                for b in range(PBLK):
                    last = pe.transpose(ps[:, (NPR + j) % 5, b * P:(b + 1) * P],
                                        cache_t[:, b, j * P:(j + 1) * P], ident)
                last.then_inc(ex_mm, 1)
            pr_free(pe, NPR + 2)
            for b in range(PBLK):
                last = pe.transpose(ps[0:QKD, (NPR + 2) % 5, b * P:(b + 1) * P], ckpe_t[:, b, :], ident)
            last.then_inc(ex_mm, 1)

            pe.wait_ge(rs_read, 6)
            with pe.Fori(0, 4) as i:
                for s in range(4):
                    pe.wait_ge(ring_in[s], 16 * i + 64)
                    ada_unit(i * 4 + s, s, 7)

            pe.wait_ge(rs_rd, 9)
            pr_free(pe, NPR + 3)
            for b in range(2):
                for k in range(KT_):
                    last = pe.transpose(ps[:, (NPR + 3) % 5, b * KVL + k * P:b * KVL + (k + 1) * P],
                                        ckn[:, k, LAT + PAST + b * P:LAT + PAST + (b + 1) * P], ident)
            last.then_inc(ex_mm, 1)
            pr_free(pe, NPR + 4)
            for b in range(2):
                last = pe.transpose(ps[:, (NPR + 4) % 5, b * QKD:(b + 1) * QKD],
                                    kpc[0:QKD, b * P:(b + 1) * P], ident[0:QKD, 0:QKD])
            last.then_inc(ex_mm, 1)
            pe.wait_ge(wukv_in, 32)
            for b in range(KEYS // P):
                i = NPR + 5 + b
                pr_free(pe, i)
                for k in range(KT_):
                    last = pe.matmul(ps[:, i % 5, :], ckn[:, k, b * P:(b + 1) * P],
                                     wukv[:, k].rearrange("p h e -> p (h e)"),
                                     start=(k == 0), stop=(k == KT_ - 1))
                last.then_inc(ex_mm, 1)
            pe.wait_ge(mod_rd, 3)
            pe.transpose(ps[0:96, 6, 0:P], modv.rearrange("p g j -> p (g j)"), ident).then_inc(mr_mm, 1)


            pe.wait_ge(v_act, KEYS // P)
            pe.wait_ge(mr_rd, 1)
            pe.wait_ge(rs_rd, 9)
            with pe.Fori(0, HEADS) as h:
                pe.wait_ge(wq_in, 32 * h + 32)
                pe.wait_ge(o_ev, QB * h + 1)
                for n in range(3):
                    for k in range(QT_):
                        pe.matmul(ps[0:QKD, n, 0:TCH[n][1]], wuq[:, k, :], chunk(cq[:, k], n),
                                  start=(k == 0), stop=(k == QT_ - 1))
                for k in range(KT_):
                    last = pe.matmul(ps[0:NOPE, 2, 256:512], wukk[:, k, :], ckn[:, k, LAT + PAST:KEYS],
                                     start=(k == 0), stop=(k == KT_ - 1))
                last.then_inc(qkv_mm, 1)
                pe.wait_ge(o_ev, QB * h + 2)
                for n in range(3):
                    for k in range(KT_):
                        last = pe.matmul(ps[0:NOPE, 3 + n, :], wukk[:, k, :], ckn[:, k, n * 512:(n + 1) * 512],
                                         start=(k == 0), stop=(k == KT_ - 1))
                last.then_inc(qkv_mm, 1)

                def scores(j):
                    if j == 0:
                        pe.wait_ge(q_rd, h + 1)
                        pe.wait_ge(k_rd, h + 1)
                    elif j >= 2:
                        pe.wait_ge(o_ev, QB * h + j + 1)
                    s = 3 * (j % 2)
                    if j < LBLK:
                        for n in range(3):
                            last = pe.matmul(ps[:, s + n, :], qT[0:QKD, j * P:(j + 1) * P],
                                             kT[0:QKD, n * 512:(n + 1) * 512], start=True, stop=True)
                    else:
                        last = pe.matmul(ps[:, s, 0:CTX], qT[0:QKD, j * P:(j + 1) * P],
                                         kT[0:QKD, LAT + PAST:KEYS], start=True, stop=True)
                    last.then_inc(s_mm, 1)

                scores(0)
                for j in range(QB):
                    if j + 1 < QB:
                        scores(j + 1)
                    pe.wait_ge(p_rd, QB * h + j + 1)
                    nt = 4 if j < LBLK else 2
                    for c in range(3 if j < LBLK else 1):
                        t = tiles_before(j) + c
                        pe.wait_ge(pt_act if t % 2 else pt_dve, TPH * h + t // 2 + 1)
                        for q in range(nt):
                            last = pe.transpose(ps[:, 6 + t % 2, q * P:(q + 1) * P],
                                                prob[j % 2][:, (c * 4 + q) * P:(c * 4 + q + 1) * P], ident)
                        last.then_inc(t_mm, 1)
                    nk = 12 if j < LBLK else 2
                    for kb in range(nk):
                        if kb % 4 == 0:
                            t = tiles_before(j) + kb // 4
                            pe.wait_ge(pt_act if t % 2 else pt_dve, TPH * h + t // 2 + 2)
                        vb = kb if j < LBLK else 12 + kb
                        last = pe.matmul(ps[:, 3 * (j % 2), 0:VD], probT[j % 2][:, kb, :],
                                         val[:, vb, bass.ds(h * VD, VD)], start=(kb == 0), stop=(kb == nk - 1))
                    last.then_inc(pv_mm, 1)

            pe.wait_ge(o_ev, QB * HEADS + 2)
            for b in range(BLK):
                if b >= 6:
                    pe.wait_ge(om_act if b % 2 else om_dve, (b - 6) // 2 + 1)
                for q in range(4):
                    last = pe.transpose(ps[:, b % 6, q * P:(q + 1) * P], o_tok[:, b, q * P:(q + 1) * P], ident)
                last.then_inc(om_mm, 1)

            pe.wait_ge(om_act, BLK // 2)
            pe.wait_ge(om_dve, BLK // 2)
            pe.sem_inc(oo_mm, 2)
            with pe.Fori(0, HG) as h:
                pe.wait_ge(hw_in[0], 16 * h + 16)
                for n in range(3):
                    for b in range(4 * n, min(4 * n + 4, BLK)):
                        for k in range(DK):
                            last = pe.matmul(ps[:, n, (b % 4) * P:(b % 4 + 1) * P], hT[:, k, b * P:(b + 1) * P],
                                             hw[0][:, k, :], start=(k == 0), stop=(k == DK - 1))
                    last.then_inc(hp_mm, 1)
                for m in range(1, 5):
                    pe.wait_ge(hw_in[m], 16 * h + 16)
                    for n in range(3):
                        if m == 1:
                            pe.wait_ge(hs_read, 3 * h + 1 + n)
                        else:
                            pe.wait_ge(hp_act, 15 * h + 3 * (m - 2) + n + 1)
                        for k in range(DK):
                            last = pe.matmul(ps[:, 3 * (m % 2) + n, 0:TCH[n][1]], hw[m][:, k, :],
                                             chunk(hT[:, k], n), start=(k == 0), stop=(k == DK - 1))
                        last.then_inc(hp_mm, 1)

                def products(s):
                    d, b = SEQ[s]
                    blk = slice(b * P, (b + 1) * P)
                    pe.wait_ge(ket_rd, NS * h + s + 1)
                    pe.transpose(ps[:, 6 + s % 2, 0:P], ke[d][:, blk], ident).then_inc(kt_mm, 1)
                    pe.wait_ge(am_rd, NS * h + s + 1)
                    pe.matmul(ps[:, 1 + s % 2, 0:P], kd[d][:, blk], ed[d][:, blk],
                              start=True, stop=True).then_inc(a_mm, 1)

                def update(s):
                    b = SEQ[s][1]
                    pe.wait_ge(ket_rd, NS * h + s + 3)
                    pe.wait_ge(u_free, NS * h + s + 1)
                    pe.matmul(ps[:, 3 + s % 2, :], ket[s % 2], vx[:, b].rearrange("p c v -> p (c v)"),
                              start=True, stop=True).then_inc(u_mm, 1)

                pe.wait_ge(hp_act, 15 * h + 15)
                pe.wait_ge(hg_rd, 2 * h + 1)
                pe.wait_ge(vx_rd, 4 * h + 4)
                products(0)
                products(1)
                update(0)
                for s in range(NS):
                    d, b = SEQ[s]
                    if s + 2 == BLK:
                        pe.wait_ge(hg_rd, 2 * h + 2)
                    if s + 2 < NS:
                        products(s + 2)
                    if s + 1 < NS:
                        update(s + 1)
                    pe.wait_ge(am_rd, NS * h + s + 3)
                    pe.wait_ge(st_rd, NS * h + s + 1)
                    if 2 <= s < BLK + 2:
                        pe.wait_ge(of_ev, BLK * h + s - 1)
                    elif s >= BLK + 2:
                        pe.wait_ge(ob_ev, BLK * h + s - BLK - 1)
                    ob = 0 if s % 2 else 5
                    pe.matmul(ps[:, ob, 0:P], vh[:, b, :], am[s % 2], start=True, stop=False)
                    for p in range(CPB):
                        cc = p if d == 0 else CPB - 1 - p
                        last = pe.matmul(ps[:, ob, cc * CHUNK:(cc + 1) * CHUNK], sring[(4 * s + p) % 16],
                                         ed[d][:, b * P + cc * CHUNK:b * P + (cc + 1) * CHUNK],
                                         start=False, stop=(p == CPB - 1))
                    last.then_inc(oo_mm, 1)
                pe.wait_ge(sq_rd, h + 1)
                for n in range(3):
                    pe.matmul(ps[:, (6, 7, 5)[n], 0:TCH[n][1]], ones, chunk(bd[0], n),
                              start=True, stop=True).then_inc(hss_mm, 1)


            pe.wait_ge(hs_read, 3 * HG + 3)
            with pe.Fori(0, DK // 2) as i:
                for s in range(2):
                    pe.wait_ge(gw_in[s], 64 * i + 64)
                    for n in range(3):
                        u = 3 * s + n
                        bank = 4 * (u % 2)
                        w = TCH[n][1]
                        pe.wait_ge(mg_ev, 6 * i + u + 1)
                        for q in range(2):
                            for k in range(DK):
                                pe.matmul(ps[:, bank + q, 0:w], gw[s][:, 8 * q + k, :], chunk(hT[:, k], n),
                                          start=(k == 0), stop=(k == DK - 1))
                        for k in range(HG):
                            pe.matmul(ps[:, bank + 2, 0:w], gw[s][:, 16 + k, :], chunk(om[:, k], n),
                                      start=(k == 0), stop=(k == HG - 1))
                        pe.wait_ge(tail_rd, HG + 1)
                        for k in range(HG):
                            last = pe.matmul(ps[:, bank + 3, 0:w], gw[s][:, 20 + k, :],
                                             oh[:, k * TOK + TCH[n][0]:k * TOK + TCH[n][0] + w],
                                             start=(k == 0), stop=(k == HG - 1))
                        last.then_inc(mg_mm, 1)

            mtk = mt.rearrange("p (k t) -> p k t", t=TOK)
            pe.wait_ge(mg_ev, 26)
            pe.wait_ge(wout_in, 16)

            def h2_transposed(b):
                pe.wait_ge(h2_rd, b + 1)
                if b >= 1:
                    pe.wait_ge(ht_ev, b)
                for k in range(DK):
                    last = pe.transpose(ps[:, 4 + k // 4, (k % 4) * P:(k % 4 + 1) * P],
                                        h2[b % 2][:, k * P:(k + 1) * P], ident)
                last.then_inc(ht_mm, 1)

            def logits(b):
                pe.wait_ge(ht_ev, b + 1)
                if b >= 1:
                    pe.wait_ge(lexp_rd, b)
                else:
                    pe.wait_ge(bc_in, 16 * 9)
                for k in range(DK):
                    last = pe.matmul(ps[:, 6, 0:EXPERTS], h2T[b % 2][:, k, :], wrt[:, k, :],
                                     start=(k == 0), stop=(k == DK - 1))
                last.then_inc(lg_mm, 1)

            def affinities(b):
                pe.wait_ge(af_rd, b + 1)
                if b >= 1:
                    pe.wait_ge(af_ev, b)
                pe.transpose(ps[0:48, 7, 0:P], affp[b % 2], ident).then_inc(af_mm, 1)

            for b in range(BLK + 3):
                if b < BLK:
                    if b >= 2:
                        pe.wait_ge(z_rd, b - 1)
                    for half in range(2):
                        for k in range(DK):
                            last = pe.matmul(ps[:, 2 * (b % 2) + half, :], mtk[:, k, b * P:(b + 1) * P],
                                             wout[:, k, half * 512:(half + 1) * 512],
                                             start=(k == 0), stop=(k == DK - 1))
                    last.then_inc(wo_mm, 1)
                if 1 <= b <= BLK:
                    h2_transposed(b - 1)
                if 2 <= b <= BLK + 1:
                    logits(b - 2)
                if b >= 3:
                    affinities(b - 3)

            pe.wait_ge(top_rd, 1)
            pe.wait_ge(af_ev, BLK)
            pe.transpose(ps[:, 0, 0:48], topv[0:48, :], ident[0:48, 0:48]).then_inc(top_mm, 1)
            pe.transpose(ps[:, 1, 0:48], topf[0:48, :], ident[0:48, 0:48]).then_inc(top_mm, 1)

            def tokens_transposed(e):
                pe.wait_ge(xg_in, 32 * e + 32)
                for k in range(DK):
                    bank, c = 4 + k // 3, (k % 3) * CAP
                    pe.transpose(ps[:, bank, c:c + CAPL], xl[:, k * P:(k + 1) * P], ident)
                    last = pe.transpose(ps[:, bank, c + CAPL:c + CAP], xc[0:CAPC, k * P:(k + 1) * P],
                                        ident[0:CAPC, 0:CAPC])
                    if k % 3 == 2 or k == DK - 1:
                        last.then_inc(xe_mm, 1)

            def expert(e, more):
                pe.wait_ge(xe_ev, 3 * e + 3)
                pe.wait_ge(yt_act, 4 * e + 1)
                pe.wait_ge(yt_dve, 4 * e + 1)
                for f in range(DK):
                    bank, c = 2 * (f % 2), (f % 2) * P
                    if f % 2 == 0:
                        pe.wait_ge(w_slot_in[f], 16 * e + 16)
                        pe.wait_ge(w_slot_in[f + 1], 16 * e + 16)
                    pe.wait_ge(hid_ev, 8 * e + f + 1)
                    for q in range(2):
                        for k in range(DK):
                            last = pe.matmul(ps[:, bank + q, 0:CAP], wslot[f // 2 * 2 + q][:, k, c:c + P],
                                             xeT[:, k, :], start=(k == 0), stop=(k == DK - 1))
                    last.then_inc(up_mm, 1)
                pe.wait_ge(yl_rd, 2 * e + 1)
                pe.wait_ge(yc_rd, 2 * e + 1)
                if more:
                    tokens_transposed(e + 1)
                pe.wait_ge(hid_ev, 8 * e + 10)

                def back(d):
                    if d % 2:
                        pe.wait_ge(yt_dve, 4 * e + d // 2 + 2)
                    else:
                        pe.wait_ge(yt_act, 4 * e + d // 2 + 2)
                    c = (d % 4) * P
                    pe.transpose(ps[:, 4 + d // 4, c:c + P], yt[:, d, 0:CAPL], ident)
                    last = pe.transpose(ps[0:CAPC, 6 + d // 4, c:c + P], yt[:, d, CAPL:CAP], ident)
                    if d % 4 == 3:
                        last.then_inc(yb_mm, 1)

                for d in range(DK):
                    if d % 2 == 0:
                        pe.wait_ge(w_slot_in[8 + d // 2], 16 * e + 16)
                    if d >= 4:
                        pe.wait_ge(yt_dve if d % 2 else yt_act, 4 * e + (d - 4) // 2 + 2)
                    for k in range(DK):
                        last = pe.matmul(ps[:, d % 4, 0:CAP], wslot[8 + d // 2][:, k, (d % 2) * P:(d % 2 + 1) * P],
                                         hid[:, k, :], start=(k == 0), stop=(k == DK - 1))
                    last.then_inc(dn_mm, 1)
                    if d == 1 and more:
                        pe.wait_ge(xe_ev, 3 * e + 6)
                    if d >= 1:
                        back(d - 1)
                back(DK - 1)

            pe.wait_ge(top_ev, 2)
            tokens_transposed(0)
            with pe.Fori(0, EXPERTS - 1) as e:
                expert(e, True)
            expert(EXPERTS - 1, False)

        @block.vector
        def _(dve):
            ch = Chain(dve, dve_chain)
            dve.wait_ge(vrow_t, 1)
            dve.tensor_copy(vcol[:, 0:VROWS], ps[:, 0, 0:VROWS]).then_inc(vcol_rd, 1)
            dve.wait_ge(vcol_rd, 1)
            g = vcol[:, R_GAM:R_GAM + 16].rearrange("p (a d h) -> p a d h", a=2, d=2)
            t = small.rearrange("p (n a h) -> p n a h", a=2, h=HG)
            ch.link(dve.tensor_tensor(t[:, 0], g[:, :, 1], g[:, :, 0], ALU.subtract))
            dve.tensor_copy(t[:, 1], t[:, 0]).then_inc(vcol_rd, 1)
            dve.wait_ge(scond_rd, 2)
            ch.link(dve.tensor_scalar_add(t[:, 3], t[:, 2], 1.0))
            ch.link(dve.reciprocal(lb, t[:, 3]))
            ch.link(dve.tensor_scalar(oml, lb, -1.0, 1.0, ALU.mult, ALU.add))
            ch.link(dve.tensor_scalar_mul(noml, oml, -1.0))

            def ada_add(lo, hi, bank, off):
                src = ps[:, bank, 0:2 * (hi - lo)].rearrange("p (j g) -> p j g", g=2)
                for gr in range(2):
                    ins = dve.tensor_tensor(modv[:, gr, lo:hi], src[:, :, gr],
                                            vcol[:, R_BADA + lo:R_BADA + hi], ALU.add)
                    ch.link(ins)

            dve.wait_ge(unit_used, 8)
            ada_add(0, 16, 0, 0)
            dve.tensor_scalar_add(modv[:, :, 8:16], modv[:, :, 8:16], 1.0).then_inc(mod_rd, 1)
            dve.wait_ge(mod_rd, 1)
            for b in range(BLK):
                gr = 0 if b < LBLK else 1
                dve.wait_ge(xt_done, 2 * b + 1)
                for q in range(4):
                    last = dve.tensor_scalar(hT[:, q, b * P:(b + 1) * P],
                                             ps[:, 1 + 2 * (b % 2), q * P:(q + 1) * P],
                                             modv[:, gr, 8 + q:9 + q], modv[:, gr, q:q + 1],
                                             ALU.mult, ALU.add)
                last.then_inc(h_dve, 1)
            for o in range(QT_ + KT_):
                for n in range(3):
                    i = o * 3 + n
                    dve.wait_ge(pr_mm, i + 1)
                    if o < QT_:
                        dst = chunk(cq[:, o], n)
                    else:
                        lo = TCH[n][0] if n < 2 else LAT + PAST
                        dst = ckn[:, o - QT_, lo:lo + TCH[n][1]]
                    dve.tensor_scalar(dst, ps[:, i % 5, 0:TCH[n][1]], vcol[:, R_QN + o:R_QN + o + 1],
                                      None, ALU.mult).then_inc(pr_dve, 1)
            for n in range(3):
                i = 24 + n
                dve.wait_ge(pr_mm, i + 1)
                lo = TCH[n][0] if n < 2 else LAT + PAST
                if n == 2:
                    dve.tensor_copy(kpc[0:QKD, :], ps[0:QKD, i % 5, 0:CTX]).then_inc(rs_rd, 1)
                dve.tensor_copy(kT[NOPE:QKD, lo:lo + TCH[n][1]],
                                ps[NOPE:QKD, i % 5, 0:TCH[n][1]]).then_inc(pr_dve, 1)
            dve.wait_ge(pr_dve, NPR)
            rt = rtmp[NOPE:QKD, :]
            kr = kT[NOPE:QKD, 0:LAT]
            dve.wait_ge(ssq_mm, 24)
            swap = [n ^ 1 for n in range(32)]
            ch.link(dve.stream_shuffle(rt, kr, swap))
            ch.link(dve.tensor_tensor(rt, rt, rope_t[NOPE:QKD, 1, :], ALU.mult))
            ch.link(dve.tensor_tensor(kr, kr, rope_t[NOPE:QKD, 0, :], ALU.mult))
            dve.tensor_tensor(kr, kr, rt, ALU.add).then_inc(rs_rd, 1)
            dve.wait_ge(rs_read, 3)
            dve.reciprocal(rsq, rsq).then_inc(rs_rd, 1)
            dve.wait_ge(rs_read, 6)
            dve.reciprocal(rsk, rsk).then_inc(rs_rd, 1)
            dve.wait_ge(rs_rd, 4)
            for k in range(KT_):
                dve.tensor_tensor(ckn[:, k, 0:LAT], ckn[:, k, 0:LAT], rsk[:, 0:LAT], ALU.mult).then_inc(rs_rd, 1)
                dve.tensor_tensor(ckn[:, k, LAT + PAST:], ckn[:, k, LAT + PAST:], rsk[:, LAT:TOK],
                                  ALU.mult).then_inc(rs_rd, 1)
            dve.wait_ge(ex_mm, 1)
            dve.tensor_copy(ckn[:, 0, LAT:LAT + PAST], ps[:, NPR % 5, :]).then_inc(ex_dve, 1)
            dve.wait_ge(ex_mm, 2)
            dve.tensor_copy(ckn[:, 1, LAT:LAT + PAST], ps[:, (NPR + 1) % 5, :]).then_inc(ex_dve, 1)
            dve.wait_ge(ex_mm, 3)
            dve.tensor_copy(kT[NOPE:QKD, LAT:LAT + PAST], ps[NOPE:QKD, (NPR + 2) % 5, :]).then_inc(ex_dve, 1)
            dve.wait_ge(rs_rd, 8)
            dve.sem_inc(rs_rd, 1)
            dve.wait_ge(unit_used, 28)
            ada_add(16, 48, 7, 0)
            dve.tensor_scalar_add(modv[:, :, 32:40], modv[:, :, 32:40], 1.0).then_inc(mod_rd, 1)
            dve.wait_ge(mod_rd, 2)
            dve.sem_inc(mod_rd, 1)
            dve.wait_ge(ex_mm, 4)
            dve.tensor_copy(nck.rearrange("p a b -> p (a b)"), ps[:, (NPR + 3) % 5, :]).then_inc(ex_dve, 1)
            dve.wait_ge(ex_mm, 5)
            dve.tensor_copy(nkp.rearrange("p a b -> p (a b)"), ps[:, (NPR + 4) % 5, 0:2 * QKD]).then_inc(ex_dve, 1)
            dve.wait_ge(mr_mm, 1)
            dve.tensor_copy(mrow[0:96, :], ps[0:96, 6, 0:P]).then_inc(mr_rd, 1)


            dve.wait_ge(outs, 32)
            dve.wait_ge(mr_out, 16)
            dve.sem_inc(o_ev, 2)
            dve.sem_inc(pt_dve, 1)
            with dve.Fori(0, HEADS) as h:
                ch.enter(h, 24)
                dve.wait_ge(qkv_mm, 2 * h + 1)
                for n in range(3):
                    last = dve.tensor_tensor(chunk(qT[0:QKD], n), ps[0:QKD, n, 0:TCH[n][1]],
                                             chunk(rsq[0:QKD], n), ALU.mult)
                dve.tensor_copy(kT[0:NOPE, LAT + PAST:KEYS], ps[0:NOPE, 2, 256:512])
                ch.link(last)
                after_loop_wait(dve)
                qr = qT[NOPE:QKD, 0:LAT]
                ch.link(dve.stream_shuffle(rt, qr, swap))
                ch.link(dve.tensor_tensor(rt, rt, rope_t[NOPE:QKD, 1, :], ALU.mult))
                ch.link(dve.tensor_tensor(qr, qr, rope_t[NOPE:QKD, 0, :], ALU.mult))
                dve.tensor_tensor(qr, qr, rt, ALU.add).then_inc(q_rd, 1)

                def neg_max(j):
                    dve.wait_ge(s_mm, QB * h + j + 1)
                    s = 3 * (j % 2)
                    src = ps[:, s:s + 3, :].rearrange("p a b -> p (a b)") if j < LBLK else ps[:, s, 0:CTX]
                    ch.link(dve.reduce_max(att[:, j % 2:j % 2 + 1], src, AX.X))
                    dve.tensor_scalar_mul(att[:, 2 + j % 2:3 + j % 2], att[:, j % 2:j % 2 + 1],
                                          -SCALE).then_inc(nb_rd, 1)

                neg_max(0)
                for j in range(QB):
                    if j + 1 < QB:
                        neg_max(j + 1)
                    for c in range(3 if j < LBLK else 1):
                        t = tiles_before(j) + c
                        if t % 2 == 0:
                            dve.wait_ge(t_mm, 2 * TPH * h + t + 1)
                            w = 4 if j < LBLK else 2
                            dve.tensor_copy(probT[j % 2][:, 4 * c:4 * c + w, :].rearrange("p a b -> p (a b)"),
                                            ps[:, 6, 0:w * P]).then_inc(pt_dve, 1)
                    dve.wait_ge(p_rd, QB * h + j + 1)
                    ch.link(dve.reciprocal(att[:, 6 + j % 2:7 + j % 2], att[:, 4 + j % 2:5 + j % 2]))
                    dve.wait_ge(pv_mm, QB * h + j + 1)
                    dve.tensor_scalar(o_tok[:, j, bass.ds(h * VD, VD)], ps[:, 3 * (j % 2), 0:VD],
                                      att[:, 6 + j % 2:7 + j % 2], None, ALU.mult).then_inc(o_ev, 1)
            ch.leave(HEADS)
            for b in range(0, BLK, 2):
                dve.wait_ge(om_mm, b + 1)
                dve.tensor_copy(om[:, :, b * P:(b + 1) * P],
                                ps[:, b % 6, :].rearrange("p (a b) -> p a b", b=P)).then_inc(om_dve, 1)

            dve.sem_inc(am_rd, 2)
            dve.sem_inc(u_free, 2)
            dve.sem_inc(tail_rd, 1)
            with dve.Fori(0, HG) as h:
                ch.enter(h, HLINKS)
                for d in range(2):
                    step = slice(None) if d == 0 else slice(None, None, -1)
                    dve.wait_ge(ln_rd, 2 * h + d + 1)
                    if d == 0:
                        dve.wait_ge(vx_rd, 4 * h + 4)
                    dve.tensor_tensor_scan(bd[d][:, step], reset, bd[d][:, step], 0.0,
                                           op0=ALU.mult, op1=ALU.add).then_inc(cs_rd, 1)
                    ch.link(dve.tensor_scalar(kd[d], kd[d], noml[:, d, bass.ds(h, 1)], oml[:, d, bass.ds(h, 1)],
                                              ALU.mult, ALU.add))
                    dve.wait_ge(e_rd, 4 * h + 2 * d + 2)
                    edge = CHUNK - 1 if d == 0 else 0
                    ch.link(dve.tensor_copy(dec[:, d, :], ed[d][:, edge:TOK:CHUNK]))
                    ch.link(dve.tensor_tensor(kd[d], kd[d], bd[d], ALU.mult))
                    ch.link(dve.tensor_tensor(
                        ke[d].rearrange("p (c t) -> p c t", t=CHUNK), kd[d].rearrange("p (c t) -> p c t", t=CHUNK),
                        dec[:, d, :].rearrange("p (c a) -> p c a", a=1).to_broadcast([P, TOK // CHUNK, CHUNK]),
                        ALU.mult))
                dve.wait_ge(hp_act, 15 * h + 15)
                for d in range(2):
                    dve.tensor_tensor(ed[d], ed[d], hq, ALU.mult).then_inc(hg_rd, 1)

                def scores_masked(s):
                    dve.wait_ge(a_mm, NS * h + s + 1)
                    dve.wait_ge(oo_mm, NS * h + s + 1)
                    dve.tensor_tensor(am[s % 2], ps[:, 1 + s % 2, 0:P], masks[:, SEQ[s][0], :],
                                      ALU.mult).then_inc(am_rd, 1)

                def add_backward(s):
                    b = SEQ[s][1]
                    dve.wait_ge(oo_mm, NS * h + s + 3)
                    dst = oh[:, bass.ds(h * TOK + b * P, P)]
                    dve.tensor_tensor(dst, ps[:, 0 if s % 2 else 5, 0:P], dst, ALU.add).then_inc(ob_ev, 1)

                scores_masked(0)
                dve.wait_ge(st_in, 16 * h + 16)
                for s in range(NS):
                    d, b = SEQ[s]
                    if s % BLK == 0:
                        dve.tensor_copy(sring[4 * s % 16], st0[:, d, :]).then_inc(s_init, 1)
                        dve.wait_ge(s_init, 2 * h + d + 1)
                    if s + 1 < NS:
                        scores_masked(s + 1)
                    dve.wait_ge(u_mm, NS * h + s + 1)
                    if s % BLK == BLK - 1:
                        dve.wait_ge(fin_out, 16 * h + 16)
                    for p in range(CPB):
                        cc = p if d == 0 else CPB - 1 - p
                        cur = sring[(4 * s + p) % 16]
                        nxt = sring[(4 * s + p + 1) % 16]
                        if p == CPB - 1 and s % BLK == LBLK - 1:
                            ins = dve.memset(nxt, 0.0)
                        else:
                            if p == CPB - 1 and s % BLK == BLK - 1:
                                nxt = fin[:, d, :]
                            ins = dve.scalar_tensor_tensor(
                                nxt, cur, dec[:, d, b * CPB + cc:b * CPB + cc + 1],
                                ps[:, 3 + s % 2, cc * P:(cc + 1) * P], op0=ALU.mult, op1=ALU.add)
                        if p == CPB - 2:
                            ins.then_inc(st_rd, 1)
                            dve.wait_ge(st_rd, NS * h + s + 1)
                        elif p == CPB - 1:
                            ins.then_inc(u_free, 1)
                            dve.wait_ge(u_free, NS * h + s + 3)
                        else:
                            ch.link(ins)
                    if s % BLK == BLK - 1:
                        dve.sem_inc(fin_rd, 1)
                    if s == BLK:
                        dve.wait_ge(of_ev, BLK * h + BLK)
                    if s > BLK:
                        add_backward(s - 1)
                add_backward(NS - 1)
                dve.wait_ge(hs_read, 3 * h + 6)
                dst = oh[:, bass.ds(h * TOK, TOK)]
                dve.wait_ge(ob_ev, BLK * h + BLK)
                ch.link(dve.reciprocal(bd[1], bd[1]))
                ch.link(dve.tensor_tensor(dst, dst, bd[1], ALU.mult))
                dve.scalar_tensor_tensor(dst, dst, vcol[:, R_HN:R_HN + 1], hgate, op0=ALU.mult,
                                         op1=ALU.mult).then_inc(tail_rd, 1)
            ch.leave(HG)


            dve.wait_ge(tail_rd, HG + 1)
            dve.sem_inc(mg_ev, 2)
            with dve.Fori(0, DK // 2) as i:
                ch.enter(i, 12)
                for s in range(2):
                    for n in range(3):
                        u = 3 * s + n
                        w, bank = TCH[n][1], 4 * (u % 2)
                        dve.wait_ge(mg_sig, 12 * i + 2 * u + 2)
                        ga, gb = gate_a[u % 2][:, 0:w], gate_b[u % 2][:, 0:w]
                        ch.link(dve.tensor_tensor(ga, ps[:, bank + 2, 0:w], ga, ALU.mult))
                        ch.link(dve.tensor_tensor(gb, ps[:, bank + 3, 0:w], gb, ALU.mult))
                        dve.tensor_tensor(mt[:, bass.ds((2 * i + s) * TOK + TCH[n][0], w)], ga, gb,
                                          ALU.add).then_inc(mg_ev, 1)
            ch.leave(DK // 2)

            dve.wait_ge(bc_in, 16 * 9)
            dve.wait_ge(pads, 3)

            def softmax(b):
                dve.wait_ge(lg_mm, b + 1)
                ch.link(dve.reduce_max(st5[:, 40:41], ps[:, 6, 0:EXPERTS], AX.X))
                dve.tensor_scalar_mul(st5[:, 41:42], st5[:, 40:41], -1.0).then_inc(lmax_rd, 1)
                dve.wait_ge(lexp_rd, b + 1)
                ch.link(dve.reciprocal(st5[:, 43:44], st5[:, 42:43]))
                c = 0 if b < LBLK else 32
                if b >= 2:
                    dve.wait_ge(af_mm, b - 1)
                dve.tensor_scalar(affp[b % 2][:, c:c + EXPERTS], ex5, st5[:, 43:44], None,
                                  ALU.mult).then_inc(af_rd, 1)

            def rows_out(b):
                dve.wait_ge(af_mm, b + 1)
                r, c = (0, b * P) if b < LBLK else (32, (b - LBLK) * P)
                dve.tensor_copy(aff[r:r + EXPERTS, c:c + P], ps[r:r + EXPERTS, 7, 0:P]).then_inc(af_ev, 1)

            for b in range(BLK + 3):
                if b < BLK:
                    g, q = (0 if b < LBLK else 1), b % 2
                    dve.wait_ge(wo_mm, b + 1)
                    z = zt[q]
                    dve.tensor_tensor(z, ps[:, 2 * q:2 * q + 2, :].rearrange("p a b -> p (a b)"), g1b[g],
                                      ALU.mult).then_inc(z_rd, 1)
                    dve.wait_ge(z_rd, b + 1)
                    dve.wait_ge(x_in[q], 16 * (b // 2 + 1))
                    dve.scalar_tensor_tensor(z, xt[q], ALPHA, z, op0=ALU.mult, op1=ALU.add).then_inc(z_sum, 1)
                    dve.wait_ge(z_sum, b + 1)
                    for n in range(2):
                        ch.link(dve.bn_stats(st5[:, 6 * n:6 * n + 6], z[:, n * 512:(n + 1) * 512]))
                    dve.bn_aggr(st5[:, 12:14], st5[:, 0:12]).then_inc(var_rd, 1)
                    dve.wait_ge(sd_rd, b + 1)
                    ch.link(dve.reciprocal(st5[:, 15:16], st5[:, 14:15]))
                    dve.scalar_tensor_tensor(st5[:, 16:17], st5[:, 12:13], -1.0, st5[:, 15:16],
                                             op0=ALU.mult, op1=ALU.mult).then_inc(nm_rd, 1)
                    dve.wait_ge(zn_rd, b + 1)
                    dve.tensor_tensor(zn[q], zn[q], ln1gb, ALU.mult).then_inc(zg_rd, 1)
                    dve.wait_ge(x1_rd, b + 1)
                    if b >= 2:
                        dve.wait_ge(h2_out[q], 16 * (b // 2))
                        dve.wait_ge(ht_mm, b - 1)
                    dve.tensor_tensor(h2[q], zn[q], scb[g], ALU.mult).then_inc(hs_rd, 1)
                if 2 <= b <= BLK + 1:
                    softmax(b - 2)
                if b >= 3:
                    rows_out(b - 3)

            dve.wait_ge(af_ev, BLK)
            for r in range(CAPL // 8):
                v8 = topv[0:48, 8 * r:8 * r + 8]
                ch.link(dve.max(v8, aff[0:48, :]))
                ch.link(dve.max_index(topi[0:48, 8 * r:8 * r + 8].bitcast(U32), v8, aff[0:48, :]))
                if r + 1 < CAPL // 8:
                    ch.link(dve.match_replace(aff[0:48, :], v8, aff[0:48, :], -2.0))
            ch.link(dve.tensor_copy(topf[0:48, :], topi[0:48, :].bitcast(U32)))
            dve.tensor_scalar_add(topf[32:48, :], topf[32:48, :], float(LAT)).then_inc(top_rd, 1)
            dve.wait_ge(top_mm, 2)
            dve.tensor_copy(gates, ps[:, 0, 0:48]).then_inc(top_ev, 1)
            dve.tensor_copy(rowi.bitcast(U32), ps[:, 1, 0:48]).then_inc(top_ev, 1)
            dve.wait_ge(top_ev, 2)

            def take_index(e):
                ch.link(dve.tensor_copy(idx_g[:, 0:1].bitcast(U32), rowi[:, bass.ds(e, 1)].bitcast(U32)))
                dve.tensor_copy(idx_g[0:CAPC, 1:2].bitcast(U32),
                                rowi[0:CAPC, bass.ds(e + 32, 1)].bitcast(U32)).then_inc(ix_rd, 1)

            def expert(e, more):
                if more:
                    dve.wait_ge(xg_in, 32 * e + 32)
                    take_index(e + 1)
                for f in range(DK):
                    dve.wait_ge(sl_rd, 8 * e + f + 1)
                    dve.tensor_tensor(hid[:, f, :], ps[:, 2 * (f % 2) + 1, 0:CAP], slu[f % 2],
                                      ALU.mult).then_inc(hid_ev, 1)
                if not isinstance(e, int) or e:
                    dve.wait_ge(sc_out, 32 * e)
                ch.link(dve.tensor_copy(idx_s[:, 0:1].bitcast(U32), rowi[:, bass.ds(e, 1)].bitcast(U32)))
                ch.link(dve.tensor_copy(idx_s[0:CAPC, 1:2].bitcast(U32),
                                        rowi[0:CAPC, bass.ds(e + 32, 1)].bitcast(U32)))
                ch.link(dve.tensor_copy(gate_s[:, 0:1], gates[:, bass.ds(e, 1)]))
                dve.tensor_copy(gate_s[0:CAPC, 1:2], gates[0:CAPC, bass.ds(e + 32, 1)]).then_inc(gs_rd, 1)
                dve.wait_ge(gs_rd, e + 1)
                for d in range(1, DK, 2):
                    dve.wait_ge(dn_mm, 8 * e + d + 1)
                    dve.tensor_scalar(yt[:, d, 0:CAPL], ps[:, d % 4, 0:CAPL], modv[:, 0, 40 + d:41 + d], None,
                                      ALU.mult)
                    dve.tensor_scalar(yt[:, d, CAPL:CAP], ps[:, d % 4, CAPL:CAP], modv[:, 1, 40 + d:41 + d],
                                      None, ALU.mult).then_inc(yt_dve, 1)
                    if d % 4 == 1 and d > 1 or d == DK - 1:
                        half = 0 if d < DK - 1 else 1
                        dve.wait_ge(yb_mm, 2 * e + half + 1)
                        dve.tensor_scalar(yl[:, half * 512:(half + 1) * 512], ps[:, 4 + half, :],
                                          gate_s[:, 0:1], None, ALU.mult).then_inc(yl_rd, 1)

            dve.sem_inc(hid_ev, 2)
            dve.sem_inc(yt_dve, 1)
            dve.sem_inc(yl_rd, 1)
            take_index(0)
            expert(0, True)
            with dve.Fori(1, EXPERTS - 1) as e:
                ch.enter(e, 4, 1)
                expert(e, True)
            ch.leave(EXPERTS - 1)
            expert(EXPERTS - 1, False)

            def stats(b):
                o = 18 * (b % 3)
                dve.wait_ge(a_in[b % 3], 16 * (b // 3 + 1))
                if b >= 3:
                    dve.wait_ge(zn_rd, BLK + b - 2)
                for n in range(2):
                    ch.link(dve.bn_stats(st8[:, o + 6 * n:o + 6 * n + 6], at_[b % 3][:, n * 512:(n + 1) * 512]))
                dve.bn_aggr(st8[:, o + 12:o + 14], st8[:, o:o + 12]).then_inc(var_rd, 1)

            def scales(b):
                o = 18 * (b % 3)
                dve.wait_ge(sd_rd, BLK + b + 1)
                ch.link(dve.reciprocal(st8[:, o + 15:o + 16], st8[:, o + 14:o + 15]))
                dve.scalar_tensor_tensor(st8[:, o + 16:o + 17], st8[:, o + 12:o + 13], -1.0,
                                         st8[:, o + 15:o + 16], op0=ALU.mult, op1=ALU.mult).then_inc(nm_rd, 1)

            dve.wait_ge(ln2_in, 32)
            stats(0)
            for b in range(BLK):
                scales(b)
                if b + 1 < BLK:
                    stats(b + 1)
                dve.wait_ge(zn_rd, BLK + b + 1)
                dve.tensor_tensor(zt8[b % 3], zt8[b % 3], ln2gb, ALU.mult).then_inc(zg_rd, 1)

        @block.scalar
        def _(act):
            ch = Chain(act, act_chain)
            act.wait_ge(vcol_rd, 1)
            ch.link(act.activation(scond[:, :, 0], vcol[:, R_C:R_C + 8], ACT.Silu))
            act.activation(scond[:, :, 1], vcol[:, R_C + 8:R_C + 16], ACT.Silu).then_inc(scond_rd, 1)
            act.wait_ge(vcol_rd, 2)
            act.activation(small[:, 16:24], small[:, 8:16], ACT.Exp).then_inc(scond_rd, 1)
            act.wait_ge(mod_rd, 1)
            for b in range(BLK):
                gr = 0 if b < LBLK else 1
                act.wait_ge(xt_done, 2 * b + 2)
                for q in range(4):
                    k = 4 + q
                    last = act.activation(hT[:, k, b * P:(b + 1) * P],
                                          ps[:, 2 + 2 * (b % 2), q * P:(q + 1) * P], ACT.Identity,
                                          bias=modv[:, gr, k:k + 1], scale=modv[:, gr, 8 + k:9 + k])
                last.then_inc(h_act, 1)

            act.wait_ge(memsets, 2)
            for o in range(QT_ + KT_):
                for n in range(3):
                    i = o * 3 + n
                    act.wait_ge(pr_dve, i + 1)
                    if i >= 3:
                        act.wait_ge(ssq_mm, i - 2)
                    act.activation(sqr[i % 3][:, 0:TCH[n][1]], ps[:, i % 5, 0:TCH[n][1]],
                                   ACT.Square).then_inc(pr_act, 1)
                if o == QT_:
                    for n in range(3):
                        act.wait_ge(ssq_mm, 16 + n)
                        act.activation(chunk(rsq, n), ps[:, 5 + n, 0:TCH[n][1]], ACT.Sqrt, bias=eps,
                                       scale=1.0 / QL).then_inc(rs_read, 1)
            for n in range(3):
                act.wait_ge(ssq_mm, 22 + n)
                act.activation(chunk(rsk, n), ps[:, 5 + n, 0:TCH[n][1]], ACT.Sqrt, bias=eps,
                               scale=1.0 / KVL).then_inc(rs_read, 1)
            for b in range(KEYS // P):
                act.wait_ge(ex_mm, 6 + b)
                act.activation(val[:, b, :], ps[:, (NPR + 5 + b) % 5, :], ACT.Copy).then_inc(v_act, 1)


            act.sem_inc(pt_act, 1)
            with act.Fori(0, HEADS) as h:
                act.wait_ge(qkv_mm, 2 * h + 2)
                act.activation(kT[0:NOPE, 0:1536], ps[0:NOPE, 3:6, :].rearrange("p a b -> p (a b)"),
                               ACT.Copy).then_inc(k_rd, 1)

                def probs(j):
                    act.wait_ge(nb_rd, QB * h + j + 1)
                    s = 3 * (j % 2)
                    w = 1536 if j < LBLK else CTX
                    src = ps[:, s:s + 3, :].rearrange("p a b -> p (a b)") if j < LBLK else ps[:, s, 0:CTX]
                    act.activation(prob[j % 2][:, 0:w], src, ACT.Exp, bias=att[:, 2 + j % 2:3 + j % 2],
                                   scale=SCALE, accum_out=att[:, 4 + j % 2:5 + j % 2]).then_inc(p_rd, 1)

                probs(0)
                for j in range(QB):
                    if j + 1 < QB:
                        probs(j + 1)
                    for c in range(3 if j < LBLK else 1):
                        t = tiles_before(j) + c
                        if t % 2 == 1:
                            act.wait_ge(t_mm, 2 * TPH * h + t + 1)
                            w = 4 if j < LBLK else 2
                            act.activation(probT[j % 2][:, 4 * c:4 * c + w, :].rearrange("p a b -> p (a b)"),
                                           ps[:, 7, 0:w * P], ACT.Copy).then_inc(pt_act, 1)
            for b in range(1, BLK, 2):
                act.wait_ge(om_mm, b + 1)
                act.activation(om[:, :, b * P:(b + 1) * P],
                               ps[:, b % 6, :].rearrange("p (a b) -> p a b", b=P), ACT.Copy).then_inc(om_act, 1)

            act.sem_inc(ket_rd, 2)
            act.sem_inc(hs_read, 3)
            with act.Fori(0, HG) as h:
                def proj(m, dst, func):
                    for n in range(3):
                        act.wait_ge(hp_mm, 15 * h + 3 * m + n + 1)
                        act.activation(chunk(dst, n), ps[:, 3 * (m % 2) + n, 0:TCH[n][1]], func).then_inc(hp_act, 1)

                def decays(d):
                    act.wait_ge(cs_rd, 2 * h + d + 1)
                    act.activation(ed[d], bd[d], ACT.Exp).then_inc(e_rd, 1)
                    act.activation(bd[d], bd[d], ACT.Exp, scale=-1.0).then_inc(e_rd, 1)

                def log_f(d):
                    act.wait_ge(hp_act, 15 * h + 6 + 3 * d)
                    act.activation(bd[d], kd[d], ACT.Ln, bias=lb[:, d, bass.ds(h, 1)],
                                   scale=oml[:, d, bass.ds(h, 1)]).then_inc(ln_rd, 1)

                proj(0, vh.rearrange("p b v -> p (b v)"), ACT.Copy)
                act.wait_ge(tail_rd, h + 1)
                proj(1, kd[0], ACT.Sigmoid)
                log_f(0)
                decays(0)
                proj(2, kd[1], ACT.Sigmoid)
                log_f(1)
                decays(1)
                proj(3, hgate, ACT.Silu)
                proj(4, hq, ACT.Silu)

                def keys_out(s):
                    act.wait_ge(kt_mm, NS * h + s + 1)
                    if s >= 2:
                        act.wait_ge(u_mm, NS * h + s - 1)
                    act.activation(ket[s % 2], ps[:, 6 + s % 2, 0:P], ACT.Copy).then_inc(ket_rd, 1)

                def out_forward(s):
                    act.wait_ge(oo_mm, NS * h + s + 3)
                    act.activation(oh[:, bass.ds(h * TOK + SEQ[s][1] * P, P)], ps[:, 0 if s % 2 else 5, 0:P],
                                   ACT.Copy).then_inc(of_ev, 1)

                keys_out(0)
                for s in range(NS):
                    if s + 1 < NS:
                        keys_out(s + 1)
                    if 1 <= s <= BLK:
                        out_forward(s - 1)
                act.wait_ge(ob_ev, BLK * h + BLK)
                after_loop_wait(act)
                act.activation(bd[0], oh[:, bass.ds(h * TOK, TOK)], ACT.Square).then_inc(sq_rd, 1)
                for n in range(3):
                    act.wait_ge(hss_mm, 3 * h + n + 1)
                    act.activation(chunk(bd[1], n), ps[:, (6, 7, 5)[n], 0:TCH[n][1]], ACT.Sqrt, bias=eps,
                                   scale=1.0 / P).then_inc(hs_read, 1)


            with act.Fori(0, DK // 2) as i:
                for u in range(6):
                    w, bank = TCH[u % 3][1], 4 * (u % 2)
                    act.wait_ge(mg_mm, 6 * i + u + 1)
                    act.activation(gate_a[u % 2][:, 0:w], ps[:, bank, 0:w], ACT.Sigmoid).then_inc(mg_sig, 1)
                    act.activation(gate_b[u % 2][:, 0:w], ps[:, bank + 1, 0:w], ACT.Sigmoid).then_inc(mg_sig, 1)

            for b in range(BLK + 3):
                if b < BLK:
                    q = b % 2
                    act.wait_ge(var_rd, b + 1)
                    act.activation(st5[:, 14:15], st5[:, 13:14], ACT.Sqrt, bias=eps).then_inc(sd_rd, 1)
                    act.wait_ge(nm_rd, b + 1)
                    if b >= 2:
                        act.wait_ge(hs_rd, b - 1)
                        act.wait_ge(xa_rd, b - 1)
                    act.activation(zn[q], zt[q], ACT.Identity, bias=st5[:, 16:17],
                                   scale=st5[:, 15:16]).then_inc(zn_rd, 1)
                if 1 <= b <= BLK:
                    act.wait_ge(ht_mm, b)
                    act.activation(h2T[(b - 1) % 2].rearrange("p a b -> p (a b)"),
                                   ps[:, 4:6, :].rearrange("p a b -> p (a b)"), ACT.Copy).then_inc(ht_ev, 1)
                if 2 <= b <= BLK + 1:
                    act.wait_ge(lmax_rd, b - 1)
                    if b >= 3:
                        act.wait_ge(af_rd, b - 2)
                    act.activation(ex5, ps[:, 6, 0:EXPERTS], ACT.Exp, bias=st5[:, 41:42],
                                   accum_out=st5[:, 42:43]).then_inc(lexp_rd, 1)

            def tokens_in(e):
                for n in range(3):
                    act.wait_ge(xe_mm, 3 * e + n + 1)
                    w = 3 if n < 2 else 2
                    act.activation(xeT[:, 3 * n:3 * n + w, :].rearrange("p a b -> p (a b)"),
                                   ps[:, 4 + n, 0:w * CAP], ACT.Copy).then_inc(xe_ev, 1)

            def expert(e, more):
                for f in range(DK):
                    act.wait_ge(up_mm, 8 * e + f + 1)
                    act.activation(slu[f % 2], ps[:, 2 * (f % 2), 0:CAP], ACT.Silu).then_inc(sl_rd, 1)
                if more:
                    tokens_in(e + 1)
                act.wait_ge(gs_rd, e + 1)
                for d in range(0, DK, 2):
                    act.wait_ge(dn_mm, 8 * e + d + 1)
                    act.activation(yt[:, d, 0:CAPL], ps[:, d % 4, 0:CAPL], ACT.Copy,
                                   scale=modv[:, 0, 40 + d:41 + d])
                    act.activation(yt[:, d, CAPL:CAP], ps[:, d % 4, CAPL:CAP], ACT.Copy,
                                   scale=modv[:, 1, 40 + d:41 + d]).then_inc(yt_act, 1)
                for half in range(2):
                    act.wait_ge(yb_mm, 2 * e + half + 1)
                    act.activation(yc[0:CAPC, half * 512:(half + 1) * 512], ps[0:CAPC, 6 + half, :], ACT.Copy,
                                   scale=gate_s[0:CAPC, 1:2]).then_inc(yc_rd, 1)

            act.sem_inc(yt_act, 1)
            act.sem_inc(yc_rd, 1)
            tokens_in(0)
            with act.Fori(0, EXPERTS - 1) as e:
                expert(e, True)
            expert(EXPERTS - 1, False)

            for b in range(BLK):
                o = 18 * (b % 3)
                act.wait_ge(var_rd, BLK + b + 1)
                act.activation(st8[:, o + 14:o + 15], st8[:, o + 13:o + 14], ACT.Sqrt, bias=eps).then_inc(sd_rd, 1)
                act.wait_ge(nm_rd, BLK + b + 1)
                if b >= 3:
                    act.wait_ge(y_out[b % 3], 16 * (b // 3))
                act.activation(zt8[b % 3], at_[b % 3], ACT.Identity, bias=st8[:, o + 16:o + 17],
                               scale=st8[:, o + 15:o + 16]).then_inc(zn_rd, 1)

        @block.gpsimd
        def _(pool):
            pool.memset(ones, 1.0).then_inc(memsets, 1)
            pool.memset(eps, EPS).then_inc(memsets, 1)
            pool.memset(ckpe_t, 0.0).then_inc(memsets, 1)
            pool.wait_ge(memsets, 3)
            pool.sem_inc(memsets, 1)

            pool.wait_ge(om_mm, 1)
            pool.memset(vx, 0.0).then_inc(pool_chain, 1)
            pool.memset(reset, 1.0).then_inc(pool_chain, 1)
            pool.wait_ge(pool_chain, 2)
            pool.memset(reset[:, 0:TOK:CHUNK], 0.0).then_inc(pool_chain, 1)
            pool.wait_ge(pool_chain, 3)
            with pool.Fori(0, HG) as h:
                pool.wait_ge(hp_act, 15 * h + 3)
                after_loop_wait(pool)
                for cc in range(CPB):
                    rows = slice(cc * CHUNK, (cc + 1) * CHUNK)
                    pool.tensor_copy(vx[rows, :, cc, :], vh[rows]).then_inc(vx_rd, 1)

            pool.wait_ge(mg_ev, 26)
            pool.memset(aff, -1.0).then_inc(pads, 1)
            for q in range(2):
                pool.memset(affp[q], 0.0).then_inc(pads, 1)
            pool.wait_ge(bc_in, 16 * 9)
            for b in range(BLK):
                g, q = (0 if b < LBLK else 1), b % 2
                pool.wait_ge(zg_rd, b + 1)
                pool.tensor_tensor(zn[q], zn[q], ln1bb, ALU.add).then_inc(x1_rd, 1)
                pool.wait_ge(x1_rd, b + 1)
                if b >= 2:
                    pool.wait_ge(acc_out[q], 16 * (b // 2))
                pool.tensor_scalar_mul(xa[q], zn[q], ALPHA).then_inc(xa_rd, 1)
                pool.wait_ge(hs_rd, b + 1)
                pool.tensor_tensor(h2[q], h2[q], shb[g], ALU.add).then_inc(h2_rd, 1)

            for n in range(2):
                pool.wait_ge(h2_out[n], 16 * (BLK // 2))
                pool.wait_ge(acc_out[n], 16 * (BLK // 2))

            def gather(e):
                pool.wait_ge(ix_rd, e + 1)
                after_loop_wait(pool)
                pool.indirect_dma_start(xl, None, h2_rows, bass.IndirectOffsetOnAxis(
                    ap=idx_g[:, 0:1].bitcast(U32), axis=0)).then_inc(xg_in, 16)
                pool.indirect_dma_start(xc[0:CAPC, :], None, h2_rows, bass.IndirectOffsetOnAxis(
                    ap=idx_g[0:CAPC, 1:2].bitcast(U32), axis=0)).then_inc(xg_in, 16)

            def scatter(e):
                pool.wait_ge(gs_rd, e + 1)
                pool.wait_ge(yl_rd, 2 * e + 3)
                after_loop_wait(pool)
                pool.indirect_dma_start(acc_rows, bass.IndirectOffsetOnAxis(
                    ap=idx_s[:, 0:1].bitcast(U32), axis=0), yl, None, compute_op=ALU.add).then_inc(sc_out, 16)
                pool.wait_ge(yc_rd, 2 * e + 3)
                after_loop_wait(pool)
                pool.indirect_dma_start(acc_rows, bass.IndirectOffsetOnAxis(
                    ap=idx_s[0:CAPC, 1:2].bitcast(U32), axis=0), yc[0:CAPC, :], None,
                    compute_op=ALU.add).then_inc(sc_out, 16)

            gather(0)
            with pool.Fori(0, EXPERTS - 1) as e:
                pool.wait_ge(xe_mm, 3 * e + 3)
                gather(e + 1)
                scatter(e)
            scatter(EXPERTS - 1)

            for b in range(BLK):
                pool.wait_ge(zg_rd, BLK + b + 1)
                pool.tensor_tensor(zt8[b % 3], zt8[b % 3], ln2bb, ALU.add).then_inc(x1_rd, 1)


def shape_tables():
    import numpy as np
    p = np.arange(P)
    same = p[:, None] // CHUNK == p[None] // CHUNK
    masks = [(same & (p[:, None] <= p[None])), (same & (p[:, None] >= p[None]))]
    tables = np.concatenate([np.eye(P)] + masks, axis=1).astype(np.float32)
    nf = ROPE // 4
    inv = (np.float32(10000.0) ** (-np.arange(nf, dtype=np.float32) / np.float32(nf))).astype(np.float32)
    t = np.arange(LAT)
    ang = np.concatenate([(t // GRID_W).astype(np.float32)[:, None] * inv,
                          (t % GRID_W).astype(np.float32)[:, None] * inv], axis=-1)
    cos, sin = np.repeat(np.cos(ang), 2, axis=1), np.repeat(np.sin(ang), 2, axis=1)
    sin[:, 0::2] *= -1
    return tables, np.ascontiguousarray(np.stack([cos.T, sin.T], axis=1), dtype=np.float32)


_INS = ['x_prompt', 'x_sample', 'c', 'cache_ckv', 'cache_kpe', 'state_hgrn', 'c_ctx', 'w_ada', 'b_ada', 'w_in',
        'mla_q_norm', 'mla_w_uq', 'mla_kv_norm', 'mla_w_ukv', 'mla_w_o', 'hgrn_gamma', 'hgrn_norm', 'hgrn_w_o',
        'w_out', 'ln1_g', 'ln1_b', 'moe_w_router', 'moe_w1', 'moe_w3', 'moe_w2', 'ln2_g', 'ln2_b']
_OUTS = [(1, CTX, D), (1, LAT, D), (1, 1, CTX, KVL), (1, 1, CTX, ROPE), (1, 1, 2, HG, P, P)]


def kernel(**inputs):
    import numpy as _np
    import concourse.bacc as _bacc
    from concourse import mybir as _mybir
    from concourse.bass_utils import run_bass_kernel_spmd as _run

    nc = _bacc.Bacc("TRN2", target_bir_lowering=False, num_devices=1)
    arrays, args = {}, []
    tables, rope = shape_tables()
    for name, a in [(n, inputs[n]) for n in _INS] + [("tables", tables), ("rope", rope)]:
        a = _np.ascontiguousarray(a)
        arrays[f"in_{name}_dram"] = a
        args.append(nc.dram_tensor(f"in_{name}_dram", a.shape, _mybir.dt.from_np(a.dtype), kind="ExternalInput").ap())
    for i, shape in enumerate(_OUTS):
        args.append(nc.dram_tensor(f"out_{i}_dram", shape, _mybir.dt.float32, kind="ExternalOutput").ap())
    flow_step(nc, *args)
    r = _run(nc, [arrays], core_ids=[0])
    return tuple(r.results[0][f"out_{i}_dram"] for i in range(len(_OUTS)))
```

```python
import concourse.bass as bass
from concourse import mybir
from contextlib import ExitStack

P = 128
D = 1024
DK = D // P
LAT, CTX, PAST = 1024, 256, 512
TOK = LAT + CTX
KEYS = LAT + PAST + CTX
BLK = TOK // P
LBLK, PBLK = LAT // P, PAST // P
HEADS, NOPE, ROPE, VD = 8, 64, 32, 64
QKD = NOPE + ROPE
QL, KVL = 768, 256
QT_, KT_ = QL // P, KVL // P
HG, CHUNK = 4, 32
HLINKS = 2 * 4 + 2 * 20 + 2
CPB = P // CHUNK
EXPERTS = 16
CAPL, CAPC = 2 * LAT // EXPERTS, 2 * CTX // EXPERTS
CAP = CAPL + CAPC
ALPHA = 2.0 ** 0.25
EPS = 1e-6
SCALE = float(QKD) ** -0.5
GRID_W = 64
UNIT = 256
O_CQ, O_CKV, O_KPE = 0, QL, QL + KVL
O_HQ = O_KPE + ROPE
O_HF, O_HB, O_HI, O_HG = (O_HQ + n * HG * P for n in range(1, 5))
O_GA = O_HG + HG * P
O_GB = O_GA + D
TCH = [(0, 512), (512, 512), (1024, 256)]
VROWS = 89
R_BADA, R_C, R_QN, R_KVN, R_HN, R_GAM = 0, 48, 64, 70, 72, 73


class Chain:

    def __init__(self, eng, sem):
        self.eng, self.sem, self.n, self.reg, self.per = eng, sem, 0, None, 0

    def link(self, ins):
        ins.then_inc(self.sem, 1)
        self.n += 1
        self.eng.wait_ge(self.sem, self.n if self.reg is None else self.reg * self.per + self.n)

    def enter(self, reg, per, first=0):
        self.n -= first * per
        self.reg, self.per, self.at = reg, per, self.n

    def leave(self, times):
        assert self.n - self.at == self.per, (self.n - self.at, self.per)
        self.n, self.reg = self.at + times * self.per, None


def flow_step(nc, x_prompt, x_sample, c, cache_ckv, cache_kpe, state_hgrn, c_ctx, w_ada, b_ada, w_in,
              q_norm, w_uq, kv_norm, w_ukv, w_o_mla, gamma, hg_norm, w_o_hg, w_out, ln1_g, ln1_b,
              w_router, w1, w3, w2, ln2_g, ln2_b, tables, rope, y_prompt, y_sample, new_ckv, new_kpe,
              new_state):
    F32, U32 = mybir.dt.float32, mybir.dt.uint32
    ALU, ACT, AX = mybir.AluOpType, mybir.ActivationFunctionType, mybir.AxisListType

    ctx = ExitStack()
    with ctx:
        def sem(name):
            return ctx.enter_context(nc.semaphore(name))

        WORDS = 53184
        arena = ctx.enter_context(nc.sbuf_tensor("arena", [P, WORDS], F32))
        ps = ctx.enter_context(nc.psum_tensor("ps", [P, 8, 512], F32))
        mod_rows = nc.dram_tensor("mod_rows", [96, P], F32, kind="Internal").ap()
        h2_rows = nc.dram_tensor("h2_rows", [TOK, D], F32, kind="Internal").ap()
        acc_rows = nc.dram_tensor("acc_rows", [TOK, D], F32, kind="Internal").ap()

        def at(off, *dims):
            size = 1
            for d in dims:
                size *= d
            assert off + size <= WORDS, (off, dims)
            v = arena[:, off:off + size]
            if len(dims) == 2:
                v = v.rearrange("p (a b) -> p a b", b=dims[1])
            if len(dims) == 3:
                v = v.rearrange("p (a b c) -> p a b c", b=dims[1], c=dims[2])
            return v

        K0 = 50000
        ident, ones = at(K0, P), at(K0 + 128, P)
        masks = at(K0 + 256, 2, P)
        modv = at(K0 + 512, 2, 48)
        vcol = at(K0 + 608, VROWS + 7)
        scond = at(K0 + 704, DK, 2)
        lb, oml, noml = at(K0 + 720, 2, HG), at(K0 + 728, 2, HG), at(K0 + 736, 2, HG)
        eps = at(K0 + 744, 1)
        small = at(K0 + 752, 48)
        rope_t = at(K0 + 816, 2, LAT)
        assert K0 + 816 + 2 * LAT <= WORDS
        hT = at(0, DK, TOK)
        xin = [at((10240 if b < 5 else 30464) + 1024 * b, D) for b in range(BLK)]
        cache_t, ckpe_t = at(15360, PBLK, KVL), at(16384, PBLK, QKD)
        kpc, nck, nkp = at(16768, CTX), at(17024, 2, KVL), at(17536, 2, QKD)
        vrow = at(17728, P)
        arow1 = at(17856, 512)
        cq = [at(10240 + TOK * n if n < 4 else 20480 + TOK * (n - 4), TOK) for n in range(QT_)]
        ring = [at(23040 + 2048 * s, DK, UNIT) for s in range(4)]
        prob = [at(23040 + 1536 * s, 1536) for s in range(2)]
        probT = [at(26112 + 1536 * s, 12, P) for s in range(2)]
        ckn = at(31232, KT_, KEYS)
        wkpe = at(34816, DK, QKD)
        vhead = [at(34816 + 1792 * s, KEYS // P, P) for s in range(2)]
        aslot = [at(o, DK, P) for o in (29184, 30208, 38400, 39424)]
        brow, arow, rin = at(47488, 512), at(40448, P), at(40576, P)
        kT, qT = at(41984, KEYS), at(43776, TOK)
        rsk, qm = at(43776, TOK), at(45056, TOK)
        wuq, wukk = at(46336, QT_, P), at(47104, KT_, NOPE)
        wukv = at(47232, KT_, 2 * VD)
        sqr = [at(48064 + 512 * s, 512) for s in range(3)]
        rtmp = at(48064, LAT)
        om = at(15360, HG * TOK)

        att = at(K0 + 800, 16)
        hw = [at(20480 + 1024 * s, DK, P) for s in range(5)]
        hq, hgate = at(25600, TOK), at(26880, TOK)
        kd, bd, ed, ke = ([at(28160 + 5120 * d + 1280 * n, TOK) for d in range(2)] for n in range(4))
        vh, vx = at(38400, BLK, P), at(39680, BLK, CPB, P)
        sring = [at(44800 + P * n, P) for n in range(16)]
        am = [at(o, P) for o in (46848, 46976, 49280, 49408)]
        ket = [at(47104 + P * n, P) for n in range(2)]
        st0, fin = at(47360, 2, P), at(47616, 2, P)
        reset = at(47872, TOK)
        dec = at(49152, 2, TOK // CHUNK)
        oh = at(10240, HG * TOK)

        gw = [at(20480 + 3072 * s, 24, P) for s in range(2)]
        mt = at(26624, DK * TOK)
        wout = at(36864, DK, D)
        gate_a = [at(45056 + 1024 * s, 512) for s in range(2)]
        gate_b = [at(45568 + 1024 * s, 512) for s in range(2)]
        g1b, scb, shb = ([at(2048 * n + 1024 * g, D) for g in range(2)] for n in range(3))
        ln1gb, ln1bb = at(6144, D), at(7168, D)
        xt, zt, zn, xa, h2 = ([at(8192 + 2048 * n + 1024 * s, D) for s in range(2)] for n in range(5))
        h2T = [at(18432 + 1024 * s, DK, P) for s in range(2)]
        wrt = at(49280, DK, EXPERTS)
        RQ = 80
        affp = [at(49408 + RQ * s, RQ) for s in range(2)]
        st5 = at(49568, 64)
        ex5 = at(49632, EXPERTS)
        HALFL = LAT // 2
        aff = at(45056, HALFL)
        topv, topi, topf = at(46080, P), at(46208, P), at(46336, P)
        topr = at(46464, 2, P)
        tsel = at(46720, 6, EXPERTS)
        gates, rowi = at(46816, 48), at(46864, 48)
        slots = [20480, 22528, 24576, 47104] + [26624 + 2048 * n for n in range(8)]
        wslot = [at(o, DK, UNIT) for o in slots]
        xl, xc, xeT = at(0, D), at(1024, D), at(2048, DK, CAP)
        hid, yt = at(3328, DK, CAP), at(4608, DK, CAP)
        slu = [at(5888 + CAP * s, CAP) for s in range(2)]
        yl, yc = at(6400, D), at(7424, D)
        idx_g, idx_s, gate_s = at(49696, 2), at(49700, 2), at(49704, 2)
        ln2gb, ln2bb = at(10240, D), at(11264, D)
        rows8, zt8 = ([at(20480 + 10240 * n + 1024 * b, D) for b in range(BLK)] for n in range(2))
        st8 = at(49712, BLK * 18)
        g2row = at(49800, P)

        vec_in, tab_in = sem("vec_in"), sem("tab_in")
        memsets = sem("memsets")
        vrow_t, vcol_rd, scond_rd = sem("vrow_transposed"), sem("vcol_ready"), sem("scond_ready")
        ring_in = [sem(f"ring_in{s}") for s in range(4)]
        unit_used = sem("unit_used")
        mod_rd = sem("mod_ready")
        xin_in = [sem(f"xin_in{s}") for s in range(5)]
        ar_mm, ar_rd, ar_t = sem("ada_rows_matmuls"), sem("ada_rows_ready"), sem("ada_rows_transposed")
        xt_done, h_dve, h_act = sem("x_transposed"), sem("h_by_dve"), sem("h_by_act")
        dve_chain, act_chain, pool_chain = sem("dve_chain"), sem("act_chain"), sem("pool_chain")
        pr_mm, pr_dve, pr_act, ssq_mm, rs_read = (sem(n) for n in (
            "proj_matmuls", "proj_by_dve", "proj_squared", "ssq_matmuls", "ssq_read"))
        rs_rd = sem("rstd_ready")
        wkpe_in, cache_in, wukv_in = sem("wkpe_in"), sem("cache_in"), sem("wukv_in")
        ex_mm, ex_dve = sem("extra_matmuls"), sem("extra_by_dve")
        outs = sem("stores_done")
        qm_rd = sem("query_factors_ready")

        wq_in, qkv_mm, q_rd, k_rd = sem("wq_in"), sem("qk_proj_matmuls"), sem("q_ready"), sem("k_ready")
        s_mm, nb_rd, p_rd, t_mm = sem("score_matmuls"), sem("neg_max_ready"), sem("probs_ready"), sem("probs_transposed")
        pt_dve, pt_act, pv_mm, o_ev = sem("probsT_by_dve"), sem("probsT_by_act"), sem("pv_matmuls"), sem("o_evacuated")
        wv_in, v_mm, v_ev, wsw_rd = sem("value_weights_in"), sem("value_matmuls"), sem("values_ready"), sem("swapped_ready")
        au_in, au_mm, au_ev, ar_out = [sem(f"ada_in{n}") for n in range(4)], sem("ada_matmuls"), sem("ada_copied"), sem("ada_rows_stored")
        vo_rd = sem("values_ones")
        br_in, g2_in = sem("ada_bias_in"), sem("g2_rows_in")
        hw_in = [sem(f"head_weights_in{n}") for n in range(5)]
        st_in, s_init, fin_rd, fin_out = sem("state_in"), sem("state_taken"), sem("final_ready"), sem("final_stored")
        hp_mm, hp_act, ln_rd, cs_rd, e_rd, hg_rd, vx_rd = (sem(n) for n in (
            "head_proj_matmuls", "head_proj_by_act", "logf_ready", "cumsum_ready", "exp_ready",
            "decayed_ready", "vx_ready"))
        kt_mm, a_mm, u_mm, oo_mm = sem("kend_transposed"), sem("a_matmuls"), sem("u_matmuls"), sem("o_matmuls")
        ket_rd, am_rd, st_rd, u_free, of_ev, ob_ev = (sem(n) for n in (
            "ket_ready", "am_ready", "states_ready", "u_read", "o_fwd_evacuated", "o_bwd_added"))
        sq_rd, hss_mm, hs_read, tail_rd = sem("head_squares"), sem("head_ssq"), sem("head_ssq_read"), sem("head_done")

        gw_in, GW0 = au_in[0:2], 16 * HEADS
        x_in, XIN0, HW0 = xin_in[0:2], 16, 16

        def tokens_in_sem(b):
            return xin_in[b] if b < 5 else hw_in[b - 5]

        def rows_in(b):
            if b < 5:
                return xin_in[b], XIN0 + (16 * (BLK // 2) if b < 2 else 0)
            return hw_in[b - 5], HW0 + 16 * HG

        mg_mm, mg_sig, mg_ev = sem("merge_matmuls"), sem("merge_gates"), sem("merged")
        wout_in, bc_in = sem("wout_in"), sem("broadcasts_in")
        wo_mm, z_rd, z_sum, var_rd, sd_rd, nm_rd, zn_rd, zg_rd, x1_rd = (sem(n) for n in (
            "out_proj_matmuls", "mix_read", "z_summed", "variance_ready", "deviation_ready", "norm_scale_ready",
            "normed", "norm_gained", "x1_ready"))
        hs_rd, h2_rd, xa_rd, pads = sem("h2_scaled"), sem("h2_ready"), sem("xa_ready"), sem("paddings")
        h2_out, acc_out = [sem(f"h2_stored{n}") for n in range(2)], [sem(f"acc_stored{n}") for n in range(2)]
        ht_mm, ht_ev, lg_mm, lmax_rd, lexp_rd, af_rd, af_mm, af_ev = (sem(n) for n in (
            "h2_transposed", "h2T_ready", "logits_matmuls", "logits_max", "logits_exp", "affinity_ready",
            "affinity_transposed", "affinity_in_rows"))
        top_rd, top_mm, top_ev = sem("top_ready"), sem("top_transposed"), sem("top_columns")
        w_in_sem = [sem(f"expert_weights_in{n}") for n in range(8)]
        ix_rd, xg_in, xe_mm, xe_ev = sem("index_ready"), sem("tokens_gathered"), sem("tokens_transposed"), sem("xeT_ready")
        up_mm, sl_rd, hid_ev, dn_mm = sem("up_matmuls"), sem("silu_ready"), sem("hidden_ready"), sem("down_matmuls")
        yt_act, yt_dve, yb_mm, gs_rd = sem("yt_by_act"), sem("yt_by_dve"), sem("y_transposed"), sem("gates_taken")
        yl_rd, yc_rd, sc_out = sem("latents_y_ready"), sem("context_y_ready"), sem("scattered")
        ln2_in, y_out = sem("ln2_in"), sem("y_stored")

        passed = sem("loop_waits_passed")

        block = ctx.enter_context(nc.Block())

        def chunk(t, n):
            return t[:, TCH[n][0]:TCH[n][0] + TCH[n][1]]

        W_IN = w_in[0].rearrange("(k p) n -> p k n", p=P)
        W_ADA = w_ada[0].rearrange("(k p) n -> p k n", p=P)
        W_UQ = w_uq[0].rearrange("(k p) n -> p k n", p=P)
        W_UKV = w_ukv[0].rearrange("(k p) n -> p k n", p=P)
        HCOLS = (O_HI, O_HF, O_HB, O_HG, O_HQ)
        W_OM = w_o_mla[0].rearrange("(k p) n -> p k n", p=P)
        W_OH = w_o_hg[0].rearrange("(k p) n -> p k n", p=P)
        NPR = 27

        def pr_free(eng, i):
            j = i - 5
            if j < 0:
                return
            if j < 24:
                eng.wait_ge(pr_act, j + 1)
            elif j < NPR:
                eng.wait_ge(pr_dve, j + 1)
            else:
                eng.wait_ge(ex_dve, j - NPR + 1)

        QB = BLK

        ORDER = [*range(LBLK, BLK), *range(LBLK)]
        NCH = [1 if j >= LBLK else 3 for j in ORDER]
        M0 = [sum(NCH[:r]) for r in range(QB + 1)]
        CPH = M0[QB]
        HALF = CPH // 2

        def steps(d):
            return list(range(BLK)) if d == 0 else [*range(LBLK - 1, -1, -1), *range(BLK - 1, LBLK - 1, -1)]

        SEQ = [(d, b) for d in range(2) for b in steps(d)]
        NS = len(SEQ)

        def after_loop_wait(eng):
            eng.sem_inc(passed, 1)

        @block.sync
        def _(sp):
            for r, n, src in ((R_BADA, 48, b_ada.rearrange("a (r p) -> (a r) p", p=P)),
                              (R_C, 8, c.rearrange("a (r p) -> (a r) p", p=P)),
                              (R_C + 8, 8, c_ctx.rearrange("(r p) -> r p", p=P)),
                              (R_QN, 6, q_norm.rearrange("a (r p) -> (a r) p", p=P)),
                              (R_KVN, 2, kv_norm.rearrange("a (r p) -> (a r) p", p=P)),
                              (R_HN, 1, hg_norm),
                              (R_GAM, 16, gamma.rearrange("a b (r p) -> (a b r) p", p=P))):
                sp.dma_start(vrow[r:r + n, :], src).then_inc(vec_in, 16)
            sp.dma_start(ident, tables[:, 0:P]).then_inc(tab_in, 16)
            sp.dma_start(masks, tables[:, P:3 * P].rearrange("p (a b) -> p a b", b=P)).then_inc(tab_in, 16)
            sp.dma_start(rope_t[NOPE:QKD, :, :], rope).then_inc(tab_in, 16)
            sp.dma_start(rope_t[QKD:P, 0, :], rope[:, 1, :]).then_inc(tab_in, 16)

            def token_rows(b, lat, con):
                return lat[0, b * P:(b + 1) * P, :] if b < LBLK else con[0, (b - LBLK) * P:(b - LBLK + 1) * P, :]

            for s in range(4):
                sp.dma_start(ring[s], W_ADA[:, :, s * UNIT:(s + 1) * UNIT]).then_inc(ring_in[s], 16)
            for s in range(4):
                sp.wait_ge(unit_used, s + 1)
                sp.dma_start(ring[s], W_ADA[:, :, (s + 4) * UNIT:(s + 5) * UNIT]).then_inc(ring_in[s], 16)
            for b in range(BLK):
                sp.dma_start(xin[b], token_rows(b, x_sample, x_prompt)).then_inc(tokens_in_sem(b), 16)
            sp.dma_start(wkpe, W_IN[:, :, O_KPE - NOPE:O_KPE + ROPE]).then_inc(wkpe_in, 16)
            for s in (3, 0, 1, 2):
                sp.wait_ge(unit_used, s + 5)
                sp.dma_start(ring[s], W_IN[:, :, s * UNIT:(s + 1) * UNIT]).then_inc(ring_in[s], 16)
            sp.dma_start(cache_t, cache_ckv[0, 0].rearrange("(b p) f -> p b f", p=P)).then_inc(cache_in, 16)
            sp.wait_ge(memsets, 4)
            sp.dma_start(ckpe_t[:, :, NOPE:QKD],
                         cache_kpe[0, 0].rearrange("(b p) f -> p b f", p=P)).then_inc(cache_in, 16)
            def head_weights(h):
                sp.dma_start(wuq[:, :, 0:QKD], W_UQ[:, :, bass.ds(h * QKD, QKD)]).then_inc(wq_in, 16)
                sp.dma_start(wukk, W_UKV[:, :, bass.ds(h * (NOPE + VD), NOPE)]).then_inc(wq_in, 16)

            def pair_weights(i):
                for s in range(2):
                    sp.dma_start(wukv[:, :, s * VD:(s + 1) * VD],
                                 W_UKV[:, :, bass.ds((2 * i + s) * (NOPE + VD) + NOPE, VD)]).then_inc(wv_in, 16)

            def ada_weights(h):
                for a in range(4):
                    sp.dma_start(aslot[a], W_ADA[:, :, bass.ds((16 + 4 * h + a) * P, P)]).then_inc(au_in[a], 16)
                sp.dma_start(brow[0:1, :], b_ada[:, bass.ds((16 + 4 * h) * P, 512)]).then_inc(br_in, 16)

            head_weights(0)
            pair_weights(0)
            sp.wait_ge(unit_used, 12)
            ada_weights(0)
            sp.wait_ge(ex_dve, 4)
            sp.dma_start(new_ckv[0, 0].rearrange("(b p) f -> p b f", p=P), nck).then_inc(outs, 16)
            sp.wait_ge(ex_dve, 5)
            sp.dma_start(new_kpe[0, 0].rearrange("(b p) f -> p b f", p=P),
                         nkp[:, :, NOPE:QKD]).then_inc(outs, 16)
            sp.sem_inc(ar_out, 16)

            def ada_rows_out(h):
                sp.wait_ge(au_ev, h + 1)
                for g in range(2):
                    sp.dma_start(mod_rows[bass.ds(g * 48 + 16 + 4 * h, 4), :], arow[g:g + 97:32, :]).then_inc(ar_out, 16)

            def next_head(h):
                ada_rows_out(h)
                sp.wait_ge(au_mm, h + 1)
                ada_weights(h + 1)
                sp.wait_ge(qkv_mm, 2 * h + 2)
                head_weights(h + 1)

            with sp.Fori(0, HEADS // 2 - 1) as i:
                next_head(2 * i)
                next_head(2 * i + 1)
                pair_weights(i + 1)
            next_head(HEADS - 2)
            ada_rows_out(HEADS - 1)
            sp.sem_inc(fin_out, 16)
            sp.wait_ge(o_ev, QB * HEADS + 1)
            for n, col in enumerate(HCOLS):
                sp.dma_start(hw[n], W_IN[:, :, col:col + P]).then_inc(hw_in[n], 16)
            sp.dma_start(st0, state_hgrn[0, 0, :, 0].rearrange("d k v -> k d v")).then_inc(st_in, 16)
            with sp.Fori(1, HG) as h:
                for n, col in enumerate(HCOLS):
                    sp.wait_ge(hp_mm, 15 * h - 12 + 3 * n)
                    sp.dma_start(hw[n], W_IN[:, :, bass.ds(col + h * P, P)]).then_inc(hw_in[n], 16)
                sp.wait_ge(s_init, 2 * h)
                sp.dma_start(st0, state_hgrn[0, 0, :, bass.ds(h, 1)].rearrange("d a k v -> k d (a v)"))\
                    .then_inc(st_in, 16)
                sp.wait_ge(fin_rd, 2 * h)
                sp.dma_start(new_state[0, 0, :, bass.ds(h - 1, 1)].rearrange("d a k v -> k d (a v)"), fin)\
                    .then_inc(fin_out, 16)
            sp.wait_ge(fin_rd, 2 * HG)
            sp.dma_start(new_state[0, 0, :, HG - 1].rearrange("d k v -> k d v"), fin).then_inc(fin_out, 16)

            def merge_weights(s, col):
                sp.dma_start(gw[s][:, 0:8, :], W_IN[:, :, bass.ds(O_GA + col, P)]).then_inc(gw_in[s], 16)
                sp.dma_start(gw[s][:, 8:16, :], W_IN[:, :, bass.ds(O_GB + col, P)]).then_inc(gw_in[s], 16)
                sp.dma_start(gw[s][:, 16:20, :], W_OM[:, :, bass.ds(col, P)]).then_inc(gw_in[s], 16)
                sp.dma_start(gw[s][:, 20:24, :], W_OH[:, :, bass.ds(col, P)]).then_inc(gw_in[s], 16)

            sp.wait_ge(hg_rd, 2 * HG)
            for s in range(2):
                merge_weights(s, s * P)
            sp.wait_ge(sq_rd, HG)
            sp.dma_start(wout, w_out[0].rearrange("(k p) n -> p k n", p=P)).then_inc(wout_in, 16)
            with sp.Fori(1, DK // 2) as i:
                for s in range(2):
                    sp.wait_ge(mg_mm, 6 * i + 3 * s - 3)
                    merge_weights(s, (2 * i + s) * P)

            def mod_row(g, j):
                return mod_rows[g * 48 + j * 8:g * 48 + j * 8 + 8, :].rearrange("(o a) p -> o (a p)", o=1)\
                    .to_broadcast([P, D])

            sp.wait_ge(mg_mm, 24)
            sp.wait_ge(ar_out, 32 * HEADS + 16)
            for g in range(2):
                sp.dma_start(g1b[g], mod_row(g, 2)).then_inc(bc_in, 16)
                sp.dma_start(shb[g], mod_row(g, 3)).then_inc(bc_in, 16)
                sp.dma_start(scb[g], mod_row(g, 4)).then_inc(bc_in, 16)
            for g in range(2):
                sp.dma_start(g2row[8 * g:8 * g + 8, :], mod_rows[g * 48 + 40:g * 48 + 48, :]).then_inc(g2_in, 16)
            sp.dma_start(ln1gb, ln1_g.to_broadcast([P, D])).then_inc(bc_in, 16)
            sp.dma_start(ln1bb, ln1_b.to_broadcast([P, D])).then_inc(bc_in, 16)
            sp.dma_start(wrt, w_router[0].rearrange("(k p) e -> p k e", p=P)).then_inc(bc_in, 16)

            for b in range(2):
                sp.dma_start(xt[b], token_rows(b, x_sample, x_prompt)).then_inc(x_in[b], 16)
            W = [w1, w3]
            def up_src(e, u, which):
                return W[which][0, e].rearrange("(k p) n -> p k n", p=P)[:, :, u * UNIT:(u + 1) * UNIT]

            for n in range(4):
                sp.dma_start(wslot[n], up_src(0, n // 2, n % 2)).then_inc(w_in_sem[n // 2], 16)
            for b in range(BLK):
                sp.wait_ge(x1_rd, b + 1)
                sp.wait_ge(xa_rd, b + 1)
                sp.dma_start(acc_rows[b * P:(b + 1) * P, :], xa[b % 2]).then_inc(acc_out[b % 2], 16)
                sp.wait_ge(h2_rd, b + 1)
                sp.dma_start(h2_rows[b * P:(b + 1) * P, :], h2[b % 2]).then_inc(h2_out[b % 2], 16)
                if b + 2 < BLK:
                    sp.wait_ge(z_sum, b + 1)
                    sp.dma_start(xt[b % 2], token_rows(b + 2, x_sample, x_prompt)).then_inc(x_in[b % 2], 16)
            for n in range(4, 8):
                sp.dma_start(wslot[n], up_src(0, n // 2, n % 2)).then_inc(w_in_sem[n // 2], 16)
            for n in range(4):
                sp.dma_start(wslot[8 + n], w2[0, 0].rearrange("(k p) n -> p k n", p=P)
                             [:, :, n * UNIT:(n + 1) * UNIT]).then_inc(w_in_sem[4 + n], 16)
            sp.wait_ge(top_ev, 2)
            sp.dma_start(ln2gb, ln2_g.to_broadcast([P, D])).then_inc(ln2_in, 16)
            sp.dma_start(ln2bb, ln2_b.to_broadcast([P, D])).then_inc(ln2_in, 16)
            with sp.Fori(1, EXPERTS) as e:
                for n in range(8):
                    if n % 2 == 0:
                        sp.wait_ge(up_mm, 8 * e + n - 6)
                    src = W[n % 2][0, bass.ds(e, 1)].rearrange("a (k p) n -> p (a k) n", p=P)
                    sp.dma_start(wslot[n], src[:, :, (n // 2) * UNIT:(n // 2 + 1) * UNIT]).then_inc(w_in_sem[n // 2], 16)
                for n in range(4):
                    sp.wait_ge(dn_mm, 8 * e + 2 * n - 6)
                    src = w2[0, bass.ds(e, 1)].rearrange("a (k p) n -> p (a k) n", p=P)
                    sp.dma_start(wslot[8 + n], src[:, :, n * UNIT:(n + 1) * UNIT]).then_inc(w_in_sem[4 + n], 16)

            sp.wait_ge(sc_out, 32 * EXPERTS)
            for b in range(BLK):
                sp.dma_start(rows8[b], acc_rows[b * P:(b + 1) * P, :]).then_inc(rows_in(b)[0], 16)
            for b in range(BLK):
                sp.wait_ge(x1_rd, BLK + b + 1)
                sp.dma_start(token_rows(b, y_sample, y_prompt), zt8[b]).then_inc(y_out, 16)
            sp.wait_ge(y_out, 16 * BLK)
            sp.wait_ge(outs, 32)
            sp.wait_ge(fin_out, 16 * (HG + 1))

        @block.tensor
        def _(pe):
            pe.wait_ge(vec_in, 16 * 7)
            pe.wait_ge(tab_in, 16 * 4)
            pe.transpose(ps[:, 0, 0:VROWS], vrow[0:VROWS, :], ident[0:VROWS, 0:VROWS]).then_inc(vrow_t, 1)

            pe.wait_ge(scond_rd, 1)
            for half in range(2):
                for a in range(4):
                    pe.wait_ge(ring_in[a], 16 * half + 16)
                    for k in range(DK):
                        last = pe.matmul(ps[32 * a:32 * a + 2, 1, half * UNIT:(half + 1) * UNIT], scond[:, k, :],
                                         ring[a][:, k, :], start=(k == 0), stop=(k == DK - 1))
                    last.then_inc(unit_used, 1)
            pe.wait_ge(ar_rd, 1)
            for q in range(4):
                last = pe.transpose(ps[:, 0, q * P:q * P + 98], arow1[0:98, q * P:(q + 1) * P], ident[0:98, 0:98])
            last.then_inc(ar_t, 1)

            for b in range(BLK):
                pe.wait_ge(tokens_in_sem(b), 16)
                for half in range(2):
                    bank = 1 + 2 * (b % 2) + half
                    if b >= 2:
                        pe.wait_ge(h_act if half else h_dve, b - 1)
                    for q in range(4):
                        k = half * 4 + q
                        last = pe.transpose(ps[:, bank, q * P:(q + 1) * P], xin[b][:, k * P:(k + 1) * P],
                                            ident)
                    last.then_inc(xt_done, 1)

            pe.wait_ge(h_act, BLK)
            pe.wait_ge(h_dve, BLK)
            pe.wait_ge(memsets, 1)

            def sums(o):
                for n in range(3):
                    i = o * 3 + n
                    pe.wait_ge(pr_act, i + 1)
                    if o >= QT_:
                        pe.wait_ge(rs_read, 3)
                    pe.matmul(ps[:, 5 + n, 0:TCH[n][1]], ones, sqr[i % 3][:, 0:TCH[n][1]],
                              start=(o in (0, QT_)), stop=(o in (QT_ - 1, QT_ + KT_ - 1))).then_inc(ssq_mm, 1)

            for o in range(QT_ + KT_):
                s = o // 2
                if o % 2 == 0:
                    pe.wait_ge(ring_in[s], 48)
                for n in range(3):
                    pr_free(pe, o * 3 + n)
                    for k in range(DK):
                        last = pe.matmul(ps[:, (o * 3 + n) % 5, 0:TCH[n][1]],
                                         ring[s][:, k, (o % 2) * P:(o % 2 + 1) * P], chunk(hT[:, k], n),
                                         start=(k == 0), stop=(k == DK - 1))
                    last.then_inc(pr_mm, 1)
                if o % 2 == 1:
                    pe.wait_ge(pr_mm, o * 3 + 3)
                    pe.sem_inc(unit_used, 1)
                if o >= 1:
                    sums(o - 1)
            pe.wait_ge(wkpe_in, 16)
            for n in range(3):
                pr_free(pe, 24 + n)
                for k in range(DK):
                    last = pe.matmul(ps[0:QKD, (24 + n) % 5, 0:TCH[n][1]], wkpe[:, k, :], chunk(hT[:, k], n),
                                     start=(k == 0), stop=(k == DK - 1))
                last.then_inc(pr_mm, 1)
            sums(QT_ + KT_ - 1)

            pe.wait_ge(cache_in, 32)
            for j in range(2):
                pr_free(pe, NPR + j)
                for b in range(PBLK):
                    last = pe.transpose(ps[:, (NPR + j) % 5, b * P:(b + 1) * P],
                                        cache_t[:, b, j * P:(j + 1) * P], ident)
                last.then_inc(ex_mm, 1)
            pr_free(pe, NPR + 2)
            for b in range(PBLK):
                last = pe.transpose(ps[0:QKD, (NPR + 2) % 5, b * P:(b + 1) * P], ckpe_t[:, b, :], ident)
            last.then_inc(ex_mm, 1)

            pe.wait_ge(rs_rd, 9)
            pr_free(pe, NPR + 3)
            for b in range(2):
                for k in range(KT_):
                    last = pe.transpose(ps[:, (NPR + 3) % 5, b * KVL + k * P:b * KVL + (k + 1) * P],
                                        ckn[:, k, LAT + PAST + b * P:LAT + PAST + (b + 1) * P], ident)
            last.then_inc(ex_mm, 1)
            pr_free(pe, NPR + 4)
            for b in range(2):
                last = pe.transpose(ps[:, (NPR + 4) % 5, b * QKD:(b + 1) * QKD],
                                    kpc[0:QKD, b * P:(b + 1) * P], ident[0:QKD, 0:QKD])
            last.then_inc(ex_mm, 1)

            pe.wait_ge(ex_dve, 5)
            pe.wait_ge(qm_rd, 4)
            with pe.Fori(0, HEADS // 2) as i:
                pe.wait_ge(wv_in, 32 * i + 32)
                for kb in range(KEYS // P):
                    for k in range(KT_):
                        last = pe.matmul(ps[:, kb // 4, (kb % 4) * P:(kb % 4 + 1) * P],
                                         ckn[:, k, kb * P:(kb + 1) * P], wukv[:, k, :],
                                         start=(k == 0), stop=(k == KT_ - 1))
                    if kb % 4 == 3 or kb == KEYS // P - 1:
                        last.then_inc(v_mm, 1)
                for s in range(2):
                    h = 2 * i + s
                    pe.wait_ge(o_ev, QB * h + 1)
                    for a in range(4):
                        pe.wait_ge(au_in[a], 16 * h + 16)
                    pe.wait_ge(br_in, 16 * h + 16)
                    for k in range(DK):
                        for a in range(4):
                            pe.matmul(ps[32 * a:32 * a + 2, 5, 0:P], scond[:, k, :], aslot[a][:, k, :],
                                      start=(k == 0), stop=False)
                    for a in range(4):
                        last = pe.matmul(ps[32 * a:32 * a + 2, 5, 0:P], ones[0:1, 0:2],
                                         brow[0:1, a * P:(a + 1) * P], start=False, stop=True)
                    last.then_inc(au_mm, 1)
                    pe.wait_ge(wsw_rd, h + 1)
                    for n in range(3):
                        if s == 0:
                            pe.wait_ge(v_ev, 4 * i + n + 1)
                        for k in range(QT_):
                            pe.matmul(ps[:, n, 0:TCH[n][1]], wuq[:, k, :], chunk(cq[k], n),
                                      start=(k == 0), stop=(k == QT_ - 1))
                    for k in range(KT_):
                        last = pe.matmul(ps[0:NOPE, 2, 256:512], wukk[:, k, :], ckn[:, k, LAT + PAST:KEYS],
                                         start=(k == 0), stop=(k == KT_ - 1))
                    last.then_inc(qkv_mm, 1)
                    if s == 0:
                        pe.wait_ge(v_ev, 4 * i + 4)
                    pe.wait_ge(au_ev, h + 1)
                    for n in range(3):
                        for k in range(KT_):
                            last = pe.matmul(ps[0:NOPE, 3 + n, :], wukk[:, k, :], ckn[:, k, n * 512:(n + 1) * 512],
                                             start=(k == 0), stop=(k == KT_ - 1))
                    last.then_inc(qkv_mm, 1)

                    def scores(r, c):
                        m, j = M0[r] + c, ORDER[r]
                        if m == 0:
                            pe.wait_ge(q_rd, 4 * h + 4)
                        if m == 2:
                            pe.wait_ge(k_rd, h + 1)
                        if m >= 5:
                            pe.wait_ge(p_rd, CPH * h + m - 4)
                        w, lo = (512, c * 512) if j < LBLK else (CTX, LAT + PAST)
                        pe.matmul(ps[:, m % 5, 0:w], qT[:, j * P:(j + 1) * P], kT[:, lo:lo + w],
                                  start=True, stop=True).then_inc(s_mm, 1)

                    def turned(r, c):
                        m = M0[r] + c
                        pe.wait_ge(p_rd, CPH * h + m + 1)
                        pe.wait_ge(pt_act if m % 2 else pt_dve, HALF * h + m // 2 + 1)
                        for q in range(4 if NCH[r] == 3 else 2):
                            last = pe.transpose(ps[:, 6 + m % 2, q * P:(q + 1) * P],
                                                prob[r % 2][:, (c * 4 + q) * P:(c * 4 + q + 1) * P], ident)
                        last.then_inc(t_mm, 1)

                    def weighted(r, c):
                        m = M0[r] + c
                        if c == 0:
                            if r == 0:
                                pe.wait_ge(k_rd, h + 1)
                            pe.wait_ge(o_ev, QB * h + r + 1)
                        pe.wait_ge(pt_act if m % 2 else pt_dve, HALF * h + m // 2 + 2)
                        n = 4 if NCH[r] == 3 else 2
                        for q in range(n):
                            vb = 4 * c + q if n == 4 else LBLK + PBLK + q
                            end = c == NCH[r] - 1 and q == n - 1
                            last = pe.matmul(ps[:, 5, 0:P], vhead[s][:, vb, :], probT[r % 2][:, 4 * c + q, :],
                                             start=(c == 0 and q == 0), stop=end)
                        if end:
                            last.then_inc(pv_mm, 1)

                    scores(0, 0)
                    for r in range(QB):
                        ahead = NCH[r + 1] if r + 1 < QB else 0
                        for c in range(min(ahead, 2)):
                            scores(r + 1, c)
                        turned(r, 0)
                        if ahead == 3:
                            scores(r + 1, 2)
                        if NCH[r] == 3:
                            turned(r, 1)
                            weighted(r, 0)
                            turned(r, 2)
                            weighted(r, 1)
                            weighted(r, 2)
                        else:
                            weighted(r, 0)

            pe.wait_ge(o_ev, QB * HEADS + 1)
            pe.sem_inc(oo_mm, 2)
            with pe.Fori(0, HG) as h:
                pe.wait_ge(hw_in[0], HW0 + 16 * h + 16)
                for n in range(3):
                    for b in range(4 * n, min(4 * n + 4, BLK)):
                        for k in range(DK):
                            last = pe.matmul(ps[:, n, (b % 4) * P:(b % 4 + 1) * P], hT[:, k, b * P:(b + 1) * P],
                                             hw[0][:, k, :], start=(k == 0), stop=(k == DK - 1))
                    last.then_inc(hp_mm, 1)
                for m in range(1, 5):
                    pe.wait_ge(hw_in[m], HW0 + 16 * h + 16)
                    for n in range(3):
                        if m == 1:
                            pe.wait_ge(hs_read, 3 * h + 1 + n)
                        else:
                            pe.wait_ge(hp_act, 15 * h + 3 * (m - 2) + n + 1)
                        for k in range(DK):
                            last = pe.matmul(ps[:, 3 * (m % 2) + n, 0:TCH[n][1]], hw[m][:, k, :],
                                             chunk(hT[:, k], n), start=(k == 0), stop=(k == DK - 1))
                        last.then_inc(hp_mm, 1)

                def products(s):
                    d, b = SEQ[s]
                    blk = slice(b * P, (b + 1) * P)
                    pe.wait_ge(ket_rd, NS * h + s + 1)
                    pe.transpose(ps[:, 6 + s % 2, 0:P], ke[d][:, blk], ident).then_inc(kt_mm, 1)
                    pe.wait_ge(am_rd, NS * h + s + 1)
                    pe.matmul(ps[:, 1 + s % 2, 0:P], kd[d][:, blk], ed[d][:, blk],
                              start=True, stop=True).then_inc(a_mm, 1)

                def update(s):
                    b = SEQ[s][1]
                    pe.wait_ge(ket_rd, NS * h + s + 3)
                    pe.wait_ge(u_free, NS * h + s + 1)
                    pe.matmul(ps[:, 3 + s % 2, :], ket[s % 2], vx[:, b].rearrange("p c v -> p (c v)"),
                              start=True, stop=True).then_inc(u_mm, 1)

                pe.wait_ge(hp_act, 15 * h + 15)
                pe.wait_ge(hg_rd, 2 * h + 1)
                pe.wait_ge(vx_rd, 4 * h + 4)
                products(0)
                products(1)
                update(0)
                for s in range(NS):
                    d, b = SEQ[s]
                    if s + 2 == BLK:
                        pe.wait_ge(hg_rd, 2 * h + 2)
                    if s + 2 < NS:
                        products(s + 2)
                    if s + 1 < NS:
                        update(s + 1)
                    pe.wait_ge(am_rd, NS * h + s + 3)
                    pe.wait_ge(st_rd, NS * h + s + 1)
                    if 2 <= s < BLK + 2:
                        pe.wait_ge(of_ev, BLK * h + s - 1)
                    elif s >= BLK + 2:
                        pe.wait_ge(ob_ev, BLK * h + s - BLK - 1)
                    ob = 0 if s % 2 else 5
                    pe.matmul(ps[:, ob, 0:P], vh[:, b, :], am[s % 4], start=True, stop=False)
                    for p in range(CPB):
                        cc = p if d == 0 else CPB - 1 - p
                        last = pe.matmul(ps[:, ob, cc * CHUNK:(cc + 1) * CHUNK], sring[(4 * s + p) % 16],
                                         ed[d][:, b * P + cc * CHUNK:b * P + (cc + 1) * CHUNK],
                                         start=False, stop=(p == CPB - 1))
                    last.then_inc(oo_mm, 1)
                pe.wait_ge(sq_rd, h + 1)
                for n in range(3):
                    pe.matmul(ps[:, (6, 7, 5)[n], 0:TCH[n][1]], ones, chunk(bd[0], n),
                              start=True, stop=True).then_inc(hss_mm, 1)


            pe.wait_ge(hs_read, 3 * HG + 3)
            with pe.Fori(0, DK // 2) as i:
                for s in range(2):
                    pe.wait_ge(gw_in[s], GW0 + 64 * i + 64)
                    for n in range(3):
                        u = 3 * s + n
                        bank = 4 * (u % 2)
                        w = TCH[n][1]
                        pe.wait_ge(mg_ev, 6 * i + u + 1)
                        for q in range(2):
                            for k in range(DK):
                                pe.matmul(ps[:, bank + q, 0:w], gw[s][:, 8 * q + k, :], chunk(hT[:, k], n),
                                          start=(k == 0), stop=(k == DK - 1))
                        for k in range(HG):
                            pe.matmul(ps[:, bank + 2, 0:w], gw[s][:, 16 + k, :], om[:, k * TOK + TCH[n][0]:k * TOK + TCH[n][0] + w],
                                      start=(k == 0), stop=(k == HG - 1))
                        pe.wait_ge(tail_rd, HG + 1)
                        for k in range(HG):
                            last = pe.matmul(ps[:, bank + 3, 0:w], gw[s][:, 20 + k, :],
                                             oh[:, k * TOK + TCH[n][0]:k * TOK + TCH[n][0] + w],
                                             start=(k == 0), stop=(k == HG - 1))
                        last.then_inc(mg_mm, 1)

            mtk = mt.rearrange("p (k t) -> p k t", t=TOK)
            pe.wait_ge(mg_ev, 26)
            pe.wait_ge(wout_in, 16)

            def h2_transposed(b):
                pe.wait_ge(h2_rd, b + 1)
                if b >= 1:
                    pe.wait_ge(ht_ev, b)
                for k in range(DK):
                    last = pe.transpose(ps[:, 4 + k // 4, (k % 4) * P:(k % 4 + 1) * P],
                                        h2[b % 2][:, k * P:(k + 1) * P], ident)
                last.then_inc(ht_mm, 1)

            def logits(b):
                pe.wait_ge(ht_ev, b + 1)
                if b >= 1:
                    pe.wait_ge(lexp_rd, b)
                else:
                    pe.wait_ge(bc_in, 16 * 9)
                for k in range(DK):
                    last = pe.matmul(ps[:, 6, 0:EXPERTS], h2T[b % 2][:, k, :], wrt[:, k, :],
                                     start=(k == 0), stop=(k == DK - 1))
                last.then_inc(lg_mm, 1)

            def affinities(b):
                pe.wait_ge(af_rd, b + 1)
                if b >= 1:
                    pe.wait_ge(af_ev, b)
                pe.transpose(ps[0:RQ, 7, 0:P], affp[b % 2], ident).then_inc(af_mm, 1)

            for b in range(BLK + 3):
                if b < BLK:
                    if b >= 2:
                        pe.wait_ge(z_rd, b - 1)
                    for half in range(2):
                        for k in range(DK):
                            last = pe.matmul(ps[:, 2 * (b % 2) + half, :], mtk[:, k, b * P:(b + 1) * P],
                                             wout[:, k, half * 512:(half + 1) * 512],
                                             start=(k == 0), stop=(k == DK - 1))
                    last.then_inc(wo_mm, 1)
                if 1 <= b <= BLK:
                    h2_transposed(b - 1)
                if 2 <= b <= BLK + 1:
                    logits(b - 2)
                if b >= 3:
                    affinities(b - 3)

            pe.wait_ge(top_rd, 1)
            pe.wait_ge(af_ev, BLK)
            pe.transpose(ps[:, 0, 0:RQ], topv[0:RQ, :], ident[0:RQ, 0:RQ]).then_inc(top_mm, 1)
            pe.transpose(ps[:, 1, 0:RQ], topf[0:RQ, :], ident[0:RQ, 0:RQ]).then_inc(top_mm, 1)
            pe.wait_ge(g2_in, 32)
            pe.transpose(ps[:, 2, 0:16], g2row[0:16, :], ident[0:16, 0:16]).then_inc(top_mm, 1)

            def tokens_transposed(e):
                pe.wait_ge(xg_in, 32 * e + 32)
                for k in range(DK):
                    bank, c = 4 + k // 3, (k % 3) * CAP
                    pe.transpose(ps[:, bank, c:c + CAPL], xl[:, k * P:(k + 1) * P], ident)
                    last = pe.transpose(ps[:, bank, c + CAPL:c + CAP], xc[0:CAPC, k * P:(k + 1) * P],
                                        ident[0:CAPC, 0:CAPC])
                    if k % 3 == 2 or k == DK - 1:
                        last.then_inc(xe_mm, 1)

            def expert(e, more):
                pe.wait_ge(xe_ev, 3 * e + 3)
                pe.wait_ge(yt_act, 4 * e + 1)
                pe.wait_ge(yt_dve, 4 * e + 1)
                for f in range(DK):
                    bank, c = 2 * (f % 2), (f % 2) * P
                    if f % 2 == 0:
                        pe.wait_ge(w_in_sem[f // 2], 32 * e + 32)
                    pe.wait_ge(hid_ev, 8 * e + f + 1)
                    for q in range(2):
                        for k in range(DK):
                            last = pe.matmul(ps[:, bank + q, 0:CAP], wslot[f // 2 * 2 + q][:, k, c:c + P],
                                             xeT[:, k, :], start=(k == 0), stop=(k == DK - 1))
                    last.then_inc(up_mm, 1)
                pe.wait_ge(yl_rd, 2 * e + 1)
                pe.wait_ge(yc_rd, 2 * e + 1)
                if more:
                    tokens_transposed(e + 1)
                pe.wait_ge(hid_ev, 8 * e + 10)

                def back(d):
                    if d % 2:
                        pe.wait_ge(yt_dve, 4 * e + d // 2 + 2)
                    else:
                        pe.wait_ge(yt_act, 4 * e + d // 2 + 2)
                    c = (d % 4) * P
                    pe.transpose(ps[:, 4 + d // 4, c:c + P], yt[:, d, 0:CAPL], ident)
                    last = pe.transpose(ps[0:CAPC, 6 + d // 4, c:c + P], yt[:, d, CAPL:CAP], ident)
                    if d % 4 == 3:
                        last.then_inc(yb_mm, 1)

                for d in range(DK):
                    if d % 2 == 0:
                        pe.wait_ge(w_in_sem[4 + d // 2], 16 * e + 16)
                    if d >= 4:
                        pe.wait_ge(yt_dve if d % 2 else yt_act, 4 * e + (d - 4) // 2 + 2)
                    for k in range(DK):
                        last = pe.matmul(ps[:, d % 4, 0:CAP], wslot[8 + d // 2][:, k, (d % 2) * P:(d % 2 + 1) * P],
                                         hid[:, k, :], start=(k == 0), stop=(k == DK - 1))
                    last.then_inc(dn_mm, 1)
                    if d == 1 and more:
                        pe.wait_ge(xe_ev, 3 * e + 6)
                    if d >= 1:
                        back(d - 1)
                back(DK - 1)

            pe.wait_ge(top_ev, 2)
            tokens_transposed(0)
            with pe.Fori(0, EXPERTS - 1) as e:
                expert(e, True)
            expert(EXPERTS - 1, False)

        @block.vector
        def _(dve):
            ch = Chain(dve, dve_chain)
            dve.wait_ge(vrow_t, 1)
            dve.tensor_copy(vcol[:, 0:VROWS], ps[:, 0, 0:VROWS]).then_inc(vcol_rd, 1)
            dve.wait_ge(vcol_rd, 1)
            g = vcol[:, R_GAM:R_GAM + 16].rearrange("p (a d h) -> p a d h", a=2, d=2)
            t = small.rearrange("p (n a h) -> p n a h", a=2, h=HG)
            ch.link(dve.tensor_tensor(t[:, 0], g[:, :, 1], g[:, :, 0], ALU.subtract))
            dve.tensor_copy(t[:, 1], t[:, 0]).then_inc(vcol_rd, 1)
            dve.wait_ge(scond_rd, 2)
            ch.link(dve.tensor_scalar_add(t[:, 3], t[:, 2], 1.0))
            ch.link(dve.reciprocal(lb, t[:, 3]))
            ch.link(dve.tensor_scalar(oml, lb, -1.0, 1.0, ALU.mult, ALU.add))
            ch.link(dve.tensor_scalar_mul(noml, oml, -1.0))

            dve.wait_ge(unit_used, 8)
            dve.wait_ge(pads, 1)
            for a in range(4):
                last = dve.tensor_copy(arow1[32 * a:32 * a + 2, :], ps[32 * a:32 * a + 2, 1, :])
            last.then_inc(ar_rd, 1)
            dve.wait_ge(ar_t, 1)
            for q in range(4):
                lo = 8 * (q // 2) + q % 2
                src = ps[:, 0, q * P:(q + 1) * P].rearrange("p (a r) -> p a r", r=32)
                for g in range(2):
                    ch.link(dve.tensor_tensor(modv[:, g, lo:lo + 7:2], src[:, :, g],
                                              vcol[:, R_BADA + lo:R_BADA + lo + 7:2], ALU.add))
            dve.tensor_scalar_add(modv[:, :, 8:16], modv[:, :, 8:16], 1.0).then_inc(mod_rd, 1)
            dve.wait_ge(mod_rd, 1)
            for b in range(BLK):
                gr = 0 if b < LBLK else 1
                dve.wait_ge(xt_done, 2 * b + 1)
                for q in range(4):
                    last = dve.tensor_scalar(hT[:, q, b * P:(b + 1) * P],
                                             ps[:, 1 + 2 * (b % 2), q * P:(q + 1) * P],
                                             modv[:, gr, 8 + q:9 + q], modv[:, gr, q:q + 1],
                                             ALU.mult, ALU.add)
                last.then_inc(h_dve, 1)
            for o in range(QT_ + KT_):
                for n in range(3):
                    i = o * 3 + n
                    dve.wait_ge(pr_mm, i + 1)
                    if o < QT_:
                        dst = chunk(cq[o], n)
                    else:
                        lo = TCH[n][0] if n < 2 else LAT + PAST
                        dst = ckn[:, o - QT_, lo:lo + TCH[n][1]]
                    dve.tensor_scalar(dst, ps[:, i % 5, 0:TCH[n][1]], vcol[:, R_QN + o:R_QN + o + 1],
                                      None, ALU.mult).then_inc(pr_dve, 1)
            for n in range(3):
                i = 24 + n
                dve.wait_ge(pr_mm, i + 1)
                lo = TCH[n][0] if n < 2 else LAT + PAST
                if n == 2:
                    dve.tensor_copy(kpc[0:QKD, :], ps[0:QKD, i % 5, 0:CTX]).then_inc(rs_rd, 1)
                dve.tensor_copy(kT[NOPE:QKD, lo:lo + TCH[n][1]],
                                ps[NOPE:QKD, i % 5, 0:TCH[n][1]]).then_inc(pr_dve, 1)
            dve.wait_ge(pr_dve, NPR)
            rt = rtmp[NOPE:QKD, :]
            kr = kT[NOPE:QKD, 0:LAT]
            dve.wait_ge(ssq_mm, 24)
            swap = [n ^ 1 for n in range(32)]
            ch.link(dve.stream_shuffle(rt, kr, swap))
            ch.link(dve.tensor_tensor(rt, rt, rope_t[NOPE:QKD, 1, :], ALU.mult))
            ch.link(dve.tensor_tensor(kr, kr, rope_t[NOPE:QKD, 0, :], ALU.mult))
            dve.tensor_tensor(kr, kr, rt, ALU.add).then_inc(rs_rd, 1)
            dve.wait_ge(rs_read, 3)
            dve.reciprocal(qm, qm).then_inc(rs_rd, 1)
            dve.wait_ge(rs_read, 6)
            dve.reciprocal(rsk, rsk).then_inc(rs_rd, 1)
            dve.wait_ge(rs_rd, 4)
            for k in range(KT_):
                dve.tensor_tensor(ckn[:, k, 0:LAT], ckn[:, k, 0:LAT], rsk[:, 0:LAT], ALU.mult).then_inc(rs_rd, 1)
                dve.tensor_tensor(ckn[:, k, LAT + PAST:], ckn[:, k, LAT + PAST:], rsk[:, LAT:TOK],
                                  ALU.mult).then_inc(rs_rd, 1)
            dve.wait_ge(ex_mm, 1)
            dve.tensor_copy(ckn[:, 0, LAT:LAT + PAST], ps[:, NPR % 5, :]).then_inc(ex_dve, 1)
            dve.wait_ge(ex_mm, 2)
            dve.tensor_copy(ckn[:, 1, LAT:LAT + PAST], ps[:, (NPR + 1) % 5, :]).then_inc(ex_dve, 1)
            dve.wait_ge(ex_mm, 3)
            dve.tensor_copy(kT[NOPE:QKD, LAT:LAT + PAST], ps[NOPE:QKD, (NPR + 2) % 5, :]).then_inc(ex_dve, 1)
            dve.wait_ge(rs_rd, 8)
            dve.sem_inc(rs_rd, 1)
            ch.link(dve.tensor_tensor(qm[NOPE:QKD, 0:LAT], qm[NOPE:QKD, 0:LAT], rope_t[NOPE:QKD, 0, :], ALU.mult))
            ch.link(dve.tensor_tensor(qm[QKD:P, 0:LAT], qm[QKD:P, 0:LAT], rope_t[QKD:P, 0, :], ALU.mult))
            dve.memset(qm[QKD:P, LAT:TOK], 0.0).then_inc(qm_rd, 1)
            dve.wait_ge(ex_dve, 3)
            dve.tensor_copy(kT[QKD:P, :], kT[NOPE:QKD, :]).then_inc(qm_rd, 1)
            dve.wait_ge(qm_rd, 2)
            dve.sem_inc(qm_rd, 2)
            dve.wait_ge(ex_mm, 4)
            dve.tensor_copy(nck.rearrange("p a b -> p (a b)"), ps[:, (NPR + 3) % 5, :]).then_inc(ex_dve, 1)
            dve.wait_ge(ex_mm, 5)
            dve.tensor_copy(nkp.rearrange("p a b -> p (a b)"), ps[:, (NPR + 4) % 5, 0:2 * QKD]).then_inc(ex_dve, 1)

            dve.sem_inc(o_ev, 1)
            dve.sem_inc(pt_dve, 1)
            dve.wait_ge(outs, 32)
            with dve.Fori(0, HEADS // 2) as i:
                ch.enter(i, 2 * (3 * (QB - 2) + 2 + QB - (QB - 2)))
                for s in range(2):
                    h = 2 * i + s
                    dve.wait_ge(qkv_mm, 2 * h + 1)
                    for n in range(3):
                        dve.tensor_tensor(chunk(qT, n), ps[:, n, 0:TCH[n][1]], chunk(qm, n),
                                          ALU.mult).then_inc(q_rd, 1)
                    dve.tensor_copy(kT[0:NOPE, LAT + PAST:KEYS], ps[0:NOPE, 2, 256:512]).then_inc(q_rd, 1)

                    def chunk_max(r, c):
                        m = M0[r] + c
                        dve.wait_ge(s_mm, CPH * h + m + 1)
                        w = 512 if NCH[r] == 3 else CTX
                        o = 8 * (r % 2) + (c if NCH[r] == 3 else 3)
                        ins = dve.reduce_max(att[:, o:o + 1], ps[:, m % 5, 0:w], AX.X)
                        if c == NCH[r] - 1:
                            ch.link(ins)

                    def neg_max(r):
                        o = 8 * (r % 2)
                        if NCH[r] == 3:
                            ch.link(dve.reduce_max(att[:, o + 3:o + 4], att[:, o:o + 3], AX.X))
                        dve.tensor_scalar_mul(att[:, o + 4:o + 5], att[:, o + 3:o + 4], -SCALE).then_inc(nb_rd, 1)

                    def turned_out(r, c):
                        m = M0[r] + c
                        if c < NCH[r] and m % 2 == 0:
                            dve.wait_ge(t_mm, CPH * h + m + 1)
                            w = 4 if NCH[r] == 3 else 2
                            dve.tensor_copy(probT[r % 2][:, 4 * c:4 * c + w, :].rearrange("p a b -> p (a b)"),
                                            ps[:, 6, 0:w * P]).then_inc(pt_dve, 1)

                    chunk_max(0, 0)
                    neg_max(0)
                    for r in range(QB):
                        ahead = NCH[r + 1] if r + 1 < QB else 0
                        for c in range(min(ahead, 2)):
                            chunk_max(r + 1, c)
                        if ahead == 1:
                            neg_max(r + 1)
                        turned_out(r, 0)
                        if ahead == 3:
                            chunk_max(r + 1, 2)
                            neg_max(r + 1)
                        turned_out(r, 1)
                        turned_out(r, 2)
                        dve.wait_ge(pv_mm, QB * h + r + 1)
                        vo, so = VD * s, VD * (1 - s)
                        ch.link(dve.reciprocal(rin[vo:vo + VD, :], ps[so:so + VD, 5, 0:P]))
                        dve.tensor_tensor(om[vo:vo + VD, bass.ds(i * TOK + ORDER[r] * P, P)],
                                          ps[vo:vo + VD, 5, 0:P], rin[vo:vo + VD, :], ALU.mult).then_inc(o_ev, 1)
            ch.leave(HEADS // 2)

            dve.sem_inc(am_rd, 2)
            dve.sem_inc(u_free, 2)
            dve.sem_inc(tail_rd, 1)
            with dve.Fori(0, HG) as h:
                ch.enter(h, HLINKS)
                for d in range(2):
                    step = slice(None) if d == 0 else slice(None, None, -1)
                    dve.wait_ge(ln_rd, 2 * h + d + 1)
                    if d == 0:
                        dve.wait_ge(vx_rd, 4 * h + 4)
                    dve.tensor_tensor_scan(bd[d][:, step], reset, bd[d][:, step], 0.0,
                                           op0=ALU.mult, op1=ALU.add).then_inc(cs_rd, 1)
                    ch.link(dve.tensor_scalar(kd[d], kd[d], noml[:, d, bass.ds(h, 1)], oml[:, d, bass.ds(h, 1)],
                                              ALU.mult, ALU.add))
                    dve.wait_ge(e_rd, 4 * h + 2 * d + 2)
                    edge = CHUNK - 1 if d == 0 else 0
                    ch.link(dve.tensor_copy(dec[:, d, :], ed[d][:, edge:TOK:CHUNK]))
                    ch.link(dve.tensor_tensor(kd[d], kd[d], bd[d], ALU.mult))
                    ch.link(dve.tensor_tensor(
                        ke[d].rearrange("p (c t) -> p c t", t=CHUNK), kd[d].rearrange("p (c t) -> p c t", t=CHUNK),
                        dec[:, d, :].rearrange("p (c a) -> p c a", a=1).to_broadcast([P, TOK // CHUNK, CHUNK]),
                        ALU.mult))
                dve.wait_ge(hp_act, 15 * h + 15)
                for d in range(2):
                    dve.tensor_tensor(ed[d], ed[d], hq, ALU.mult).then_inc(hg_rd, 1)

                def scores_masked(s):
                    dve.wait_ge(a_mm, NS * h + s + 1)
                    if s >= 2:
                        dve.wait_ge(oo_mm, NS * h + s - 1)
                    dve.tensor_tensor(am[s % 4], ps[:, 1 + s % 2, 0:P], masks[:, SEQ[s][0], :],
                                      ALU.mult).then_inc(am_rd, 1)

                def add_backward(s):
                    b = SEQ[s][1]
                    dve.wait_ge(oo_mm, NS * h + s + 3)
                    dst = oh[:, bass.ds(h * TOK + b * P, P)]
                    dve.tensor_tensor(dst, ps[:, 0 if s % 2 else 5, 0:P], dst, ALU.add).then_inc(ob_ev, 1)

                scores_masked(0)
                dve.wait_ge(st_in, 16 * h + 16)
                for s in range(NS):
                    d, b = SEQ[s]
                    if s % BLK == 0:
                        dve.tensor_copy(sring[4 * s % 16], st0[:, d, :]).then_inc(s_init, 1)
                        dve.wait_ge(s_init, 2 * h + d + 1)
                    if s + 1 < NS:
                        scores_masked(s + 1)
                    dve.wait_ge(u_mm, NS * h + s + 1)
                    if s % BLK == BLK - 1:
                        dve.wait_ge(fin_out, 16 * h + 16)
                    for p in range(CPB):
                        cc = p if d == 0 else CPB - 1 - p
                        cur = sring[(4 * s + p) % 16]
                        nxt = sring[(4 * s + p + 1) % 16]
                        if p == CPB - 1 and s % BLK == LBLK - 1:
                            ins = dve.memset(nxt, 0.0)
                        else:
                            if p == CPB - 1 and s % BLK == BLK - 1:
                                nxt = fin[:, d, :]
                            ins = dve.scalar_tensor_tensor(
                                nxt, cur, dec[:, d, b * CPB + cc:b * CPB + cc + 1],
                                ps[:, 3 + s % 2, cc * P:(cc + 1) * P], op0=ALU.mult, op1=ALU.add)
                        if p == CPB - 2:
                            ins.then_inc(st_rd, 1)
                            dve.wait_ge(st_rd, NS * h + s + 1)
                        elif p == CPB - 1:
                            ins.then_inc(u_free, 1)
                            dve.wait_ge(u_free, NS * h + s + 3)
                        else:
                            ch.link(ins)
                    if s % BLK == BLK - 1:
                        dve.sem_inc(fin_rd, 1)
                    if s == BLK:
                        dve.wait_ge(of_ev, BLK * h + BLK)
                    if s > BLK:
                        add_backward(s - 1)
                add_backward(NS - 1)
                dve.wait_ge(hs_read, 3 * h + 6)
                dst = oh[:, bass.ds(h * TOK, TOK)]
                dve.wait_ge(ob_ev, BLK * h + BLK)
                ch.link(dve.reciprocal(bd[1], bd[1]))
                ch.link(dve.tensor_tensor(dst, dst, bd[1], ALU.mult))
                dve.scalar_tensor_tensor(dst, dst, vcol[:, R_HN:R_HN + 1], hgate, op0=ALU.mult,
                                         op1=ALU.mult).then_inc(tail_rd, 1)
            ch.leave(HG)


            dve.wait_ge(tail_rd, HG + 1)
            dve.sem_inc(mg_ev, 2)
            with dve.Fori(0, DK // 2) as i:
                ch.enter(i, 12)
                for s in range(2):
                    for n in range(3):
                        u = 3 * s + n
                        w, bank = TCH[n][1], 4 * (u % 2)
                        dve.wait_ge(mg_sig, 12 * i + 2 * u + 2)
                        ga, gb = gate_a[u % 2][:, 0:w], gate_b[u % 2][:, 0:w]
                        ch.link(dve.tensor_tensor(ga, ps[:, bank + 2, 0:w], ga, ALU.mult))
                        ch.link(dve.tensor_tensor(gb, ps[:, bank + 3, 0:w], gb, ALU.mult))
                        dve.tensor_tensor(mt[:, bass.ds((2 * i + s) * TOK + TCH[n][0], w)], ga, gb,
                                          ALU.add).then_inc(mg_ev, 1)
            ch.leave(DK // 2)

            dve.wait_ge(bc_in, 16 * 9)
            dve.wait_ge(pads, 4)

            def aff_row(b):
                return 32 * (b // (LBLK // 2))

            def softmax(b):
                dve.wait_ge(lg_mm, b + 1)
                ch.link(dve.reduce_max(st5[:, 40:41], ps[:, 6, 0:EXPERTS], AX.X))
                dve.tensor_scalar_mul(st5[:, 41:42], st5[:, 40:41], -1.0).then_inc(lmax_rd, 1)
                dve.wait_ge(lexp_rd, b + 1)
                ch.link(dve.reciprocal(st5[:, 43:44], st5[:, 42:43]))
                c = aff_row(b)
                if b >= 2:
                    dve.wait_ge(af_mm, b - 1)
                dve.tensor_scalar(affp[b % 2][:, c:c + EXPERTS], ex5, st5[:, 43:44], None,
                                  ALU.mult).then_inc(af_rd, 1)

            def rows_out(b):
                dve.wait_ge(af_mm, b + 1)
                r, c = aff_row(b), b % (LBLK // 2) * P
                dve.tensor_copy(aff[r:r + EXPERTS, c:c + P], ps[r:r + EXPERTS, 7, 0:P]).then_inc(af_ev, 1)

            for b in range(BLK + 3):
                if b < BLK:
                    g, q = (0 if b < LBLK else 1), b % 2
                    dve.wait_ge(wo_mm, b + 1)
                    z = zt[q]
                    dve.tensor_tensor(z, ps[:, 2 * q:2 * q + 2, :].rearrange("p a b -> p (a b)"), g1b[g],
                                      ALU.mult).then_inc(z_rd, 1)
                    dve.wait_ge(z_rd, b + 1)
                    dve.wait_ge(x_in[q], XIN0 + 16 * (b // 2 + 1))
                    dve.scalar_tensor_tensor(z, xt[q], ALPHA, z, op0=ALU.mult, op1=ALU.add).then_inc(z_sum, 1)
                    dve.wait_ge(z_sum, b + 1)
                    for n in range(2):
                        ch.link(dve.bn_stats(st5[:, 6 * n:6 * n + 6], z[:, n * 512:(n + 1) * 512]))
                    dve.bn_aggr(st5[:, 12:14], st5[:, 0:12]).then_inc(var_rd, 1)
                    dve.wait_ge(sd_rd, b + 1)
                    ch.link(dve.reciprocal(st5[:, 15:16], st5[:, 14:15]))
                    dve.scalar_tensor_tensor(st5[:, 16:17], st5[:, 12:13], -1.0, st5[:, 15:16],
                                             op0=ALU.mult, op1=ALU.mult).then_inc(nm_rd, 1)
                    dve.wait_ge(zn_rd, b + 1)
                    dve.tensor_tensor(zn[q], zn[q], ln1gb, ALU.mult).then_inc(zg_rd, 1)
                    dve.wait_ge(x1_rd, b + 1)
                    if b >= 2:
                        dve.wait_ge(h2_out[q], 16 * (b // 2))
                        dve.wait_ge(ht_mm, b - 1)
                    dve.scalar_tensor_tensor(h2[q], scb[g], 1.0, zn[q], op0=ALU.add, op1=ALU.mult)\
                        .then_inc(hs_rd, 1)
                if 2 <= b <= BLK + 1:
                    softmax(b - 2)
                if b >= 3:
                    rows_out(b - 3)

            dve.wait_ge(af_ev, BLK)
            for r in range(CAPL // 8):
                v8 = topv[0:RQ, 8 * r:8 * r + 8]
                ch.link(dve.max(v8, aff[0:RQ, :]))
                ch.link(dve.max_index(topi[0:RQ, 8 * r:8 * r + 8].bitcast(U32), v8, aff[0:RQ, :]))
                if r + 1 < CAPL // 8:
                    ch.link(dve.match_replace(aff[0:RQ, :], v8, aff[0:RQ, :], -2.0))
            ch.link(dve.tensor_copy(topf[0:RQ, :], topi[0:RQ, :].bitcast(U32)))
            dve.tensor_scalar_add(topf[64:80, :], topf[64:80, :], float(LAT))
            dve.tensor_copy(topr[32:48, 0, :], topv[32:48, ::-1])
            ch.link(dve.tensor_scalar_add(topr[32:48, 1, :], topf[32:48, ::-1], float(HALFL)))
            dve.tensor_copy(topv[32:48, :], topr[32:48, 0, :])
            dve.tensor_copy(topf[32:48, :], topr[32:48, 1, :]).then_inc(top_rd, 1)
            dve.wait_ge(top_mm, 3)
            dve.tensor_copy(modv[:, :, 40:48], ps[:, 2, 0:16].rearrange("p (g k) -> p g k", k=DK))
            dve.tensor_copy(gates[:, 32:48], ps[:, 0, 64:80])
            dve.tensor_copy(rowi[:, 32:48].bitcast(U32), ps[:, 1, 64:80])
            for n, (bank, c) in enumerate(((0, 0), (0, 32), (1, 0), (1, 32))):
                last = dve.tensor_copy(tsel[:, n, :], ps[:, bank, c:c + EXPERTS])
            ch.link(last)
            dve.tensor_tensor(gates[:, 0:16], tsel[:, 0, :], tsel[:, 1, :], ALU.max).then_inc(top_ev, 1)
            dve.tensor_tensor(tsel[:, 4, :], tsel[:, 0, :], tsel[:, 1, :], ALU.is_ge)
            ch.link(dve.tensor_tensor(tsel[:, 5, :], tsel[:, 2, :], tsel[:, 3, :], ALU.subtract))
            ch.link(dve.tensor_tensor(tsel[:, 5, :], tsel[:, 5, :], tsel[:, 4, :], ALU.mult))
            dve.tensor_tensor(rowi[:, 0:16].bitcast(U32), tsel[:, 5, :], tsel[:, 3, :], ALU.add).then_inc(top_ev, 1)
            dve.wait_ge(top_ev, 2)

            def take_index(e):
                ch.link(dve.tensor_copy(idx_g[:, 0:1].bitcast(U32), rowi[:, bass.ds(e, 1)].bitcast(U32)))
                dve.tensor_copy(idx_g[0:CAPC, 1:2].bitcast(U32),
                                rowi[0:CAPC, bass.ds(e + 32, 1)].bitcast(U32)).then_inc(ix_rd, 1)

            def expert(e, more):
                if more:
                    dve.wait_ge(xg_in, 32 * e + 32)
                    take_index(e + 1)
                for f in range(DK):
                    dve.wait_ge(sl_rd, 8 * e + f + 1)
                    dve.tensor_tensor(hid[:, f, :], ps[:, 2 * (f % 2) + 1, 0:CAP], slu[f % 2],
                                      ALU.mult).then_inc(hid_ev, 1)
                if not isinstance(e, int) or e:
                    dve.wait_ge(sc_out, 32 * e)
                ch.link(dve.tensor_copy(idx_s[:, 0:1].bitcast(U32), rowi[:, bass.ds(e, 1)].bitcast(U32)))
                ch.link(dve.tensor_copy(idx_s[0:CAPC, 1:2].bitcast(U32),
                                        rowi[0:CAPC, bass.ds(e + 32, 1)].bitcast(U32)))
                ch.link(dve.tensor_copy(gate_s[:, 0:1], gates[:, bass.ds(e, 1)]))
                dve.tensor_copy(gate_s[0:CAPC, 1:2], gates[0:CAPC, bass.ds(e + 32, 1)]).then_inc(gs_rd, 1)
                dve.wait_ge(gs_rd, e + 1)
                for d in range(1, DK, 2):
                    dve.wait_ge(dn_mm, 8 * e + d + 1)
                    dve.tensor_scalar(yt[:, d, 0:CAPL], ps[:, d % 4, 0:CAPL], modv[:, 0, 40 + d:41 + d], None,
                                      ALU.mult)
                    dve.tensor_scalar(yt[:, d, CAPL:CAP], ps[:, d % 4, CAPL:CAP], modv[:, 1, 40 + d:41 + d],
                                      None, ALU.mult).then_inc(yt_dve, 1)
                    if d % 4 == 1 and d > 1 or d == DK - 1:
                        half = 0 if d < DK - 1 else 1
                        dve.wait_ge(yb_mm, 2 * e + half + 1)
                        dve.tensor_scalar(yl[:, half * 512:(half + 1) * 512], ps[:, 4 + half, :],
                                          gate_s[:, 0:1], None, ALU.mult).then_inc(yl_rd, 1)

            dve.sem_inc(hid_ev, 2)
            dve.sem_inc(yt_dve, 1)
            dve.sem_inc(yl_rd, 1)
            take_index(0)
            expert(0, True)
            with dve.Fori(1, EXPERTS - 1) as e:
                ch.enter(e, 4, 1)
                expert(e, True)
            ch.leave(EXPERTS - 1)
            expert(EXPERTS - 1, False)

            def stats(b):
                o = 18 * b
                dve.wait_ge(rows_in(b)[0], rows_in(b)[1] + 16)
                for n in range(2):
                    ch.link(dve.bn_stats(st8[:, o + 6 * n:o + 6 * n + 6], rows8[b][:, n * 512:(n + 1) * 512]))
                dve.bn_aggr(st8[:, o + 12:o + 14], st8[:, o:o + 12]).then_inc(var_rd, 1)

            def scales(b):
                o = 18 * b
                dve.wait_ge(sd_rd, BLK + b + 1)
                ch.link(dve.reciprocal(st8[:, o + 15:o + 16], st8[:, o + 14:o + 15]))
                dve.scalar_tensor_tensor(st8[:, o + 16:o + 17], st8[:, o + 12:o + 13], -1.0,
                                         st8[:, o + 15:o + 16], op0=ALU.mult, op1=ALU.mult).then_inc(nm_rd, 1)

            dve.wait_ge(ln2_in, 32)
            stats(0)
            for b in range(BLK):
                scales(b)
                if b + 1 < BLK:
                    stats(b + 1)
                dve.wait_ge(zn_rd, BLK + b + 1)
                dve.tensor_tensor(zt8[b], zt8[b], ln2gb, ALU.mult).then_inc(zg_rd, 1)

        @block.scalar
        def _(act):
            ch = Chain(act, act_chain)
            act.wait_ge(vcol_rd, 1)
            ch.link(act.activation(scond[:, :, 0], vcol[:, R_C:R_C + 8], ACT.Silu))
            act.activation(scond[:, :, 1], vcol[:, R_C + 8:R_C + 16], ACT.Silu).then_inc(scond_rd, 1)
            act.wait_ge(vcol_rd, 2)
            act.activation(small[:, 16:24], small[:, 8:16], ACT.Exp).then_inc(scond_rd, 1)
            act.wait_ge(mod_rd, 1)
            for b in range(BLK):
                gr = 0 if b < LBLK else 1
                act.wait_ge(xt_done, 2 * b + 2)
                for q in range(4):
                    k = 4 + q
                    last = act.activation(hT[:, k, b * P:(b + 1) * P],
                                          ps[:, 2 + 2 * (b % 2), q * P:(q + 1) * P], ACT.Identity,
                                          bias=modv[:, gr, k:k + 1], scale=modv[:, gr, 8 + k:9 + k])
                last.then_inc(h_act, 1)

            act.wait_ge(memsets, 2)
            for o in range(QT_ + KT_):
                for n in range(3):
                    i = o * 3 + n
                    act.wait_ge(pr_dve, i + 1)
                    if i >= 3:
                        act.wait_ge(ssq_mm, i - 2)
                    act.activation(sqr[i % 3][:, 0:TCH[n][1]], ps[:, i % 5, 0:TCH[n][1]],
                                   ACT.Square).then_inc(pr_act, 1)
                if o == QT_:
                    for n in range(3):
                        act.wait_ge(ssq_mm, 16 + n)
                        act.activation(chunk(qm, n), ps[:, 5 + n, 0:TCH[n][1]], ACT.Sqrt, bias=eps,
                                       scale=1.0 / QL).then_inc(rs_read, 1)
            for n in range(3):
                act.wait_ge(ssq_mm, 22 + n)
                act.activation(chunk(rsk, n), ps[:, 5 + n, 0:TCH[n][1]], ACT.Sqrt, bias=eps,
                               scale=1.0 / KVL).then_inc(rs_read, 1)

            act.sem_inc(pt_act, 1)
            act.wait_ge(vo_rd, 2)
            with act.Fori(0, HEADS // 2) as i:
                for n in range(4):
                    act.wait_ge(v_mm, 4 * i + n + 1)
                    w = 4 if n < 3 else 2
                    for s in range(2):
                        src = ps[:, n, 0:w * P].rearrange("p (a b) -> p a b", b=P)[:, :, s * VD:(s + 1) * VD]
                        last = act.activation(vhead[s][:, 4 * n:4 * n + w, s * VD:(s + 1) * VD], src, ACT.Copy)
                    last.then_inc(v_ev, 1)
                for s in range(2):
                    h = 2 * i + s
                    act.wait_ge(au_mm, h + 1)
                    act.wait_ge(ar_out, 32 * h + 16)
                    for a in range(4):
                        last = act.activation(arow[32 * a:32 * a + 2, :], ps[32 * a:32 * a + 2, 5, 0:P], ACT.Copy)
                    last.then_inc(au_ev, 1)
                    act.wait_ge(qkv_mm, 2 * h + 2)
                    act.activation(kT[0:NOPE, 0:1536], ps[0:NOPE, 3:6, :].rearrange("p a b -> p (a b)"),
                                   ACT.Copy).then_inc(k_rd, 1)

                    def probs(r):
                        o = 8 * (r % 2)
                        act.wait_ge(nb_rd, QB * h + r + 1)
                        for c in range(NCH[r]):
                            w = 512 if NCH[r] == 3 else CTX
                            act.activation(prob[r % 2][:, c * 512:c * 512 + w], ps[:, (M0[r] + c) % 5, 0:w],
                                           ACT.Exp, bias=att[:, o + 4:o + 5], scale=SCALE).then_inc(p_rd, 1)

                    probs(0)
                    for r in range(QB):
                        for c in range(NCH[r]):
                            m = M0[r] + c
                            if m % 2:
                                act.wait_ge(t_mm, CPH * h + m + 1)
                                w = 4 if NCH[r] == 3 else 2
                                act.activation(probT[r % 2][:, 4 * c:4 * c + w, :].rearrange("p a b -> p (a b)"),
                                               ps[:, 7, 0:w * P], ACT.Copy).then_inc(pt_act, 1)
                        if r + 1 < QB:
                            probs(r + 1)

            act.sem_inc(ket_rd, 2)
            act.sem_inc(hs_read, 3)
            with act.Fori(0, HG) as h:
                def proj(m, dst, func):
                    for n in range(3):
                        act.wait_ge(hp_mm, 15 * h + 3 * m + n + 1)
                        act.activation(chunk(dst, n), ps[:, 3 * (m % 2) + n, 0:TCH[n][1]], func).then_inc(hp_act, 1)

                def decays(d):
                    act.wait_ge(cs_rd, 2 * h + d + 1)
                    act.activation(ed[d], bd[d], ACT.Exp).then_inc(e_rd, 1)
                    act.activation(bd[d], bd[d], ACT.Exp, scale=-1.0).then_inc(e_rd, 1)

                def log_f(d):
                    act.wait_ge(hp_act, 15 * h + 6 + 3 * d)
                    act.activation(bd[d], kd[d], ACT.Ln, bias=lb[:, d, bass.ds(h, 1)],
                                   scale=oml[:, d, bass.ds(h, 1)]).then_inc(ln_rd, 1)

                proj(0, vh.rearrange("p b v -> p (b v)"), ACT.Copy)
                act.wait_ge(tail_rd, h + 1)
                proj(1, kd[0], ACT.Sigmoid)
                log_f(0)
                decays(0)
                proj(2, kd[1], ACT.Sigmoid)
                log_f(1)
                decays(1)
                proj(3, hgate, ACT.Silu)
                proj(4, hq, ACT.Silu)

                def keys_out(s):
                    act.wait_ge(kt_mm, NS * h + s + 1)
                    if s >= 2:
                        act.wait_ge(u_mm, NS * h + s - 1)
                    act.activation(ket[s % 2], ps[:, 6 + s % 2, 0:P], ACT.Copy).then_inc(ket_rd, 1)

                def out_forward(s):
                    act.wait_ge(oo_mm, NS * h + s + 3)
                    act.activation(oh[:, bass.ds(h * TOK + SEQ[s][1] * P, P)], ps[:, 0 if s % 2 else 5, 0:P],
                                   ACT.Copy).then_inc(of_ev, 1)

                keys_out(0)
                for s in range(NS):
                    if s + 1 < NS:
                        keys_out(s + 1)
                    if 1 <= s <= BLK:
                        out_forward(s - 1)
                act.wait_ge(ob_ev, BLK * h + BLK)
                after_loop_wait(act)
                act.activation(bd[0], oh[:, bass.ds(h * TOK, TOK)], ACT.Square).then_inc(sq_rd, 1)
                for n in range(3):
                    act.wait_ge(hss_mm, 3 * h + n + 1)
                    act.activation(chunk(bd[1], n), ps[:, (6, 7, 5)[n], 0:TCH[n][1]], ACT.Sqrt, bias=eps,
                                   scale=1.0 / P).then_inc(hs_read, 1)


            with act.Fori(0, DK // 2) as i:
                for u in range(6):
                    w, bank = TCH[u % 3][1], 4 * (u % 2)
                    act.wait_ge(mg_mm, 6 * i + u + 1)
                    act.activation(gate_a[u % 2][:, 0:w], ps[:, bank, 0:w], ACT.Sigmoid).then_inc(mg_sig, 1)
                    act.activation(gate_b[u % 2][:, 0:w], ps[:, bank + 1, 0:w], ACT.Sigmoid).then_inc(mg_sig, 1)

            for b in range(BLK + 3):
                if b < BLK:
                    q = b % 2
                    act.wait_ge(var_rd, b + 1)
                    act.activation(st5[:, 14:15], st5[:, 13:14], ACT.Sqrt, bias=eps).then_inc(sd_rd, 1)
                    act.wait_ge(nm_rd, b + 1)
                    if b >= 2:
                        act.wait_ge(hs_rd, b - 1)
                        act.wait_ge(xa_rd, b - 1)
                    act.activation(zn[q], zt[q], ACT.Identity, bias=st5[:, 16:17],
                                   scale=st5[:, 15:16]).then_inc(zn_rd, 1)
                if 1 <= b <= BLK:
                    act.wait_ge(ht_mm, b)
                    act.activation(h2T[(b - 1) % 2].rearrange("p a b -> p (a b)"),
                                   ps[:, 4:6, :].rearrange("p a b -> p (a b)"), ACT.Copy).then_inc(ht_ev, 1)
                if 2 <= b <= BLK + 1:
                    act.wait_ge(lmax_rd, b - 1)
                    if b >= 3:
                        act.wait_ge(af_rd, b - 2)
                    act.activation(ex5, ps[:, 6, 0:EXPERTS], ACT.Exp, bias=st5[:, 41:42],
                                   accum_out=st5[:, 42:43]).then_inc(lexp_rd, 1)

            def tokens_in(e):
                for n in range(3):
                    act.wait_ge(xe_mm, 3 * e + n + 1)
                    w = 3 if n < 2 else 2
                    act.activation(xeT[:, 3 * n:3 * n + w, :].rearrange("p a b -> p (a b)"),
                                   ps[:, 4 + n, 0:w * CAP], ACT.Copy).then_inc(xe_ev, 1)

            def expert(e, more):
                for f in range(DK):
                    act.wait_ge(up_mm, 8 * e + f + 1)
                    act.activation(slu[f % 2], ps[:, 2 * (f % 2), 0:CAP], ACT.Silu).then_inc(sl_rd, 1)
                if more:
                    tokens_in(e + 1)
                act.wait_ge(gs_rd, e + 1)
                for d in range(0, DK, 2):
                    act.wait_ge(dn_mm, 8 * e + d + 1)
                    act.activation(yt[:, d, 0:CAPL], ps[:, d % 4, 0:CAPL], ACT.Copy,
                                   scale=modv[:, 0, 40 + d:41 + d])
                    act.activation(yt[:, d, CAPL:CAP], ps[:, d % 4, CAPL:CAP], ACT.Copy,
                                   scale=modv[:, 1, 40 + d:41 + d]).then_inc(yt_act, 1)
                for half in range(2):
                    act.wait_ge(yb_mm, 2 * e + half + 1)
                    act.activation(yc[0:CAPC, half * 512:(half + 1) * 512], ps[0:CAPC, 6 + half, :], ACT.Copy,
                                   scale=gate_s[0:CAPC, 1:2]).then_inc(yc_rd, 1)

            act.sem_inc(yt_act, 1)
            act.sem_inc(yc_rd, 1)
            tokens_in(0)
            with act.Fori(0, EXPERTS - 1) as e:
                expert(e, True)
            expert(EXPERTS - 1, False)

            for b in range(BLK):
                o = 18 * b
                act.wait_ge(var_rd, BLK + b + 1)
                act.activation(st8[:, o + 14:o + 15], st8[:, o + 13:o + 14], ACT.Sqrt, bias=eps).then_inc(sd_rd, 1)
                act.wait_ge(nm_rd, BLK + b + 1)
                act.activation(zt8[b], rows8[b], ACT.Identity, bias=st8[:, o + 16:o + 17],
                               scale=st8[:, o + 15:o + 16]).then_inc(zn_rd, 1)

        @block.gpsimd
        def _(pool):
            pool.memset(arow1, 0.0).then_inc(pads, 1)
            pool.memset(ones, 1.0).then_inc(memsets, 1)
            pool.memset(eps, EPS).then_inc(memsets, 1)
            pool.memset(ckpe_t, 0.0).then_inc(memsets, 1)
            pool.wait_ge(memsets, 3)
            pool.sem_inc(memsets, 1)


            pool.wait_ge(ex_mm, 3)
            pool.memset(vhead[0][:, :, VD:P], 1.0).then_inc(vo_rd, 1)
            pool.memset(vhead[1][:, :, 0:VD], 1.0).then_inc(vo_rd, 1)
            with pool.Fori(0, HEADS) as h:
                pool.wait_ge(wq_in, 32 * h + 32)
                after_loop_wait(pool)
                for n in range(2):
                    last = pool.tensor_copy(wuq[:, :, QKD + n:P:2], wuq[:, :, NOPE + 1 - n:QKD:2])
                last.then_inc(wsw_rd, 1)

            pool.wait_ge(o_ev, QB * HEADS + 1)
            pool.wait_ge(ar_out, 32 * HEADS + 16)
            pool.memset(vx, 0.0).then_inc(pool_chain, 1)
            pool.memset(reset, 1.0).then_inc(pool_chain, 1)
            pool.wait_ge(pool_chain, 2)
            pool.memset(reset[:, 0:TOK:CHUNK], 0.0).then_inc(pool_chain, 1)
            pool.wait_ge(pool_chain, 3)
            with pool.Fori(0, HG) as h:
                pool.wait_ge(hp_act, 15 * h + 3)
                after_loop_wait(pool)
                for cc in range(CPB):
                    rows = slice(cc * CHUNK, (cc + 1) * CHUNK)
                    pool.tensor_copy(vx[rows, :, cc, :], vh[rows]).then_inc(vx_rd, 1)

            pool.wait_ge(mg_ev, 26)
            pool.memset(aff, -1.0).then_inc(pads, 1)
            for q in range(2):
                pool.memset(affp[q], 0.0).then_inc(pads, 1)
            pool.wait_ge(bc_in, 16 * 9)
            for b in range(BLK):
                g, q = (0 if b < LBLK else 1), b % 2
                pool.wait_ge(zg_rd, b + 1)
                pool.tensor_tensor(zn[q], zn[q], ln1bb, ALU.add).then_inc(x1_rd, 1)
                pool.wait_ge(x1_rd, b + 1)
                if b >= 2:
                    pool.wait_ge(acc_out[q], 16 * (b // 2))
                pool.tensor_scalar_mul(xa[q], zn[q], ALPHA).then_inc(xa_rd, 1)
                pool.wait_ge(hs_rd, b + 1)
                pool.tensor_tensor(h2[q], h2[q], shb[g], ALU.add).then_inc(h2_rd, 1)

            for n in range(2):
                pool.wait_ge(h2_out[n], 16 * (BLK // 2))
                pool.wait_ge(acc_out[n], 16 * (BLK // 2))

            def gather(e):
                pool.wait_ge(ix_rd, e + 1)
                after_loop_wait(pool)
                pool.indirect_dma_start(xl, None, h2_rows, bass.IndirectOffsetOnAxis(
                    ap=idx_g[:, 0:1].bitcast(U32), axis=0)).then_inc(xg_in, 16)
                pool.indirect_dma_start(xc[0:CAPC, :], None, h2_rows, bass.IndirectOffsetOnAxis(
                    ap=idx_g[0:CAPC, 1:2].bitcast(U32), axis=0)).then_inc(xg_in, 16)

            def scatter(e):
                pool.wait_ge(gs_rd, e + 1)
                pool.wait_ge(yl_rd, 2 * e + 3)
                after_loop_wait(pool)
                pool.indirect_dma_start(acc_rows, bass.IndirectOffsetOnAxis(
                    ap=idx_s[:, 0:1].bitcast(U32), axis=0), yl, None, compute_op=ALU.add).then_inc(sc_out, 16)
                pool.wait_ge(yc_rd, 2 * e + 3)
                after_loop_wait(pool)
                pool.indirect_dma_start(acc_rows, bass.IndirectOffsetOnAxis(
                    ap=idx_s[0:CAPC, 1:2].bitcast(U32), axis=0), yc[0:CAPC, :], None,
                    compute_op=ALU.add).then_inc(sc_out, 16)

            gather(0)
            with pool.Fori(0, EXPERTS - 1) as e:
                pool.wait_ge(xe_mm, 3 * e + 3)
                gather(e + 1)
                scatter(e)
            scatter(EXPERTS - 1)

            for b in range(BLK):
                pool.wait_ge(zg_rd, BLK + b + 1)
                pool.tensor_tensor(zt8[b], zt8[b], ln2bb, ALU.add).then_inc(x1_rd, 1)


def shape_tables():
    import numpy as np
    p = np.arange(P)
    same = p[:, None] // CHUNK == p[None] // CHUNK
    masks = [(same & (p[:, None] <= p[None])), (same & (p[:, None] >= p[None]))]
    tables = np.concatenate([np.eye(P)] + masks, axis=1).astype(np.float32)
    nf = ROPE // 4
    inv = (np.float32(10000.0) ** (-np.arange(nf, dtype=np.float32) / np.float32(nf))).astype(np.float32)
    t = np.arange(LAT)
    ang = np.concatenate([(t // GRID_W).astype(np.float32)[:, None] * inv,
                          (t % GRID_W).astype(np.float32)[:, None] * inv], axis=-1)
    cos, sin = np.repeat(np.cos(ang), 2, axis=1), np.repeat(np.sin(ang), 2, axis=1)
    sin[:, 0::2] *= -1
    return tables, np.ascontiguousarray(np.stack([cos.T, sin.T], axis=1), dtype=np.float32)


_INS = ['x_prompt', 'x_sample', 'c', 'cache_ckv', 'cache_kpe', 'state_hgrn', 'c_ctx', 'w_ada', 'b_ada', 'w_in',
        'mla_q_norm', 'mla_w_uq', 'mla_kv_norm', 'mla_w_ukv', 'mla_w_o', 'hgrn_gamma', 'hgrn_norm', 'hgrn_w_o',
        'w_out', 'ln1_g', 'ln1_b', 'moe_w_router', 'moe_w1', 'moe_w3', 'moe_w2', 'ln2_g', 'ln2_b']
_OUTS = [(1, CTX, D), (1, LAT, D), (1, 1, CTX, KVL), (1, 1, CTX, ROPE), (1, 1, 2, HG, P, P)]


def kernel(**inputs):
    import numpy as _np
    import concourse.bacc as _bacc
    from concourse import mybir as _mybir
    from concourse.bass_utils import run_bass_kernel_spmd as _run

    nc = _bacc.Bacc("TRN2", target_bir_lowering=False, num_devices=1)
    arrays, args = {}, []
    tables, rope = shape_tables()
    for name, a in [(n, inputs[n]) for n in _INS] + [("tables", tables), ("rope", rope)]:
        a = _np.ascontiguousarray(a)
        arrays[f"in_{name}_dram"] = a
        args.append(nc.dram_tensor(f"in_{name}_dram", a.shape, _mybir.dt.from_np(a.dtype), kind="ExternalInput").ap())
    for i, shape in enumerate(_OUTS):
        args.append(nc.dram_tensor(f"out_{i}_dram", shape, _mybir.dt.float32, kind="ExternalOutput").ap())
    flow_step(nc, *args)
    r = _run(nc, [arrays], core_ids=[0])
    return tuple(r.results[0][f"out_{i}_dram"] for i in range(len(_OUTS)))
```

```python
import concourse.bass as bass
from concourse import mybir
from contextlib import ExitStack

P = 128
D = 1024
DK = D // P
LAT, CTX, PAST = 1024, 256, 512
TOK = LAT + CTX
KEYS = LAT + PAST + CTX
BLK = TOK // P
LBLK, PBLK = LAT // P, PAST // P
HEADS, NOPE, ROPE, VD = 8, 64, 32, 64
QKD = NOPE + ROPE
QL, KVL = 768, 256
QT_, KT_ = QL // P, KVL // P
HG, CHUNK = 4, 32
HLINKS = 2 * 4 + 2 * 20 + 1
CPB = P // CHUNK
EXPERTS = 16
CAPL, CAPC = 2 * LAT // EXPERTS, 2 * CTX // EXPERTS
CAP = CAPL + CAPC
ALPHA = 2.0 ** 0.25
EPS = 1e-6
SCALE = float(QKD) ** -0.5
GRID_W = 64
UNIT = 256
O_CQ, O_CKV, O_KPE = 0, QL, QL + KVL
O_HQ = O_KPE + ROPE
O_HF, O_HB, O_HI, O_HG = (O_HQ + n * HG * P for n in range(1, 5))
O_GA = O_HG + HG * P
O_GB = O_GA + D
TCH = [(0, 512), (512, 512), (1024, 256)]
VROWS = 89
R_BADA, R_C, R_QN, R_KVN, R_HN, R_GAM = 0, 48, 64, 70, 72, 73


class Chain:

    def __init__(self, eng, sem):
        self.eng, self.sem, self.n, self.reg, self.per = eng, sem, 0, None, 0

    def link(self, ins):
        ins.then_inc(self.sem, 1)
        self.n += 1
        self.eng.wait_ge(self.sem, self.n if self.reg is None else self.reg * self.per + self.n)

    def mark(self, ins):
        ins.then_inc(self.sem, 1)
        self.n += 1

    def meet(self, but=0):
        self.eng.wait_ge(self.sem, self.n - but)

    def enter(self, reg, per, first=0):
        self.n -= first * per
        self.reg, self.per, self.at = reg, per, self.n

    def leave(self, times):
        assert self.n - self.at == self.per, (self.n - self.at, self.per)
        self.n, self.reg = self.at + times * self.per, None


def flow_step(nc, x_prompt, x_sample, c, cache_ckv, cache_kpe, state_hgrn, c_ctx, w_ada, b_ada, w_in,
              q_norm, w_uq, kv_norm, w_ukv, w_o_mla, gamma, hg_norm, w_o_hg, w_out, ln1_g, ln1_b,
              w_router, w1, w3, w2, ln2_g, ln2_b, tables, rope, y_prompt, y_sample, new_ckv, new_kpe,
              new_state):
    F32, U32 = mybir.dt.float32, mybir.dt.uint32
    ALU, ACT, AX = mybir.AluOpType, mybir.ActivationFunctionType, mybir.AxisListType

    ctx = ExitStack()
    with ctx:
        def sem(name):
            return ctx.enter_context(nc.semaphore(name))

        WORDS = 53184
        arena = ctx.enter_context(nc.sbuf_tensor("arena", [P, WORDS], F32))
        ps = ctx.enter_context(nc.psum_tensor("ps", [P, 8, 512], F32))
        mod_rows = nc.dram_tensor("mod_rows", [96, P], F32, kind="Internal").ap()
        h2_rows = nc.dram_tensor("h2_rows", [TOK, D], F32, kind="Internal").ap()
        acc_rows = nc.dram_tensor("acc_rows", [TOK, D], F32, kind="Internal").ap()

        def at(off, *dims):
            size = 1
            for d in dims:
                size *= d
            assert off + size <= WORDS, (off, dims)
            v = arena[:, off:off + size]
            if len(dims) == 2:
                v = v.rearrange("p (a b) -> p a b", b=dims[1])
            if len(dims) == 3:
                v = v.rearrange("p (a b c) -> p a b c", b=dims[1], c=dims[2])
            return v

        K0 = 50000
        ident, ones = at(K0, P), at(K0 + 128, P)
        masks = at(K0 + 256, 2, P)
        modv = at(K0 + 512, 2, 48)
        vcol = at(K0 + 608, VROWS + 7)
        scond = at(K0 + 704, DK, 2)
        lb, oml, noml = at(K0 + 720, 2, HG), at(K0 + 728, 2, HG), at(K0 + 736, 2, HG)
        eps = at(K0 + 744, 1)
        small = at(K0 + 752, 48)
        rope_t = at(K0 + 816, 2, LAT)
        assert K0 + 816 + 2 * LAT <= WORDS
        hT = at(0, DK, TOK)
        xin = [at((10240 if b < 5 else 30464) + 1024 * b, D) for b in range(BLK)]
        cache_t, ckpe_t = at(15360, PBLK, KVL), at(16384, PBLK, QKD)
        kpc, nck, nkp = at(16768, CTX), at(17024, 2, KVL), at(17536, 2, QKD)
        vrow = at(17728, P)
        arow1 = at(17856, 512)
        cq = [at(10240 + TOK * n if n < 4 else 20480 + TOK * (n - 4), TOK) for n in range(QT_)]
        ring = [at(23040 + 2048 * s, DK, UNIT) for s in range(4)]
        prob = [at(23040 + 1536 * s, 1536) for s in range(2)]
        probT = [at(26112 + 1536 * s, 12, P) for s in range(2)]
        ckn = at(31232, KT_, KEYS)
        wkpe = at(34816, DK, QKD)
        vhead = [at(34816 + 1792 * s, KEYS // P, P) for s in range(2)]
        aslot = [at(o, DK, P) for o in (29184, 30208, 38400, 39424)]
        brow, arow, rin = at(47488, 512), at(40448, P), at(40576, P)
        kT, qT = [at(o, KEYS) for o in (41984, 48064)], at(43776, TOK)
        rsk, qm = at(43776, TOK), at(45056, TOK)
        wuq, wukk = at(46336, QT_, P), at(40704, KT_, 2 * NOPE)
        wukv = at(47232, KT_, 2 * VD)
        sqr = [at(48064 + 512 * s, 512) for s in range(3)]
        rtmp = at(18368, LAT)
        om = at(15360, HG * TOK)

        att = at(K0 + 800, 16)
        hw = [at(20480 + 1024 * s, DK, P) for s in range(5)]
        hq, hgate = at(25600, TOK), at(26880, TOK)
        kd, bd, ed, ke = ([at(28160 + 5120 * d + 1280 * n, TOK) for d in range(2)] for n in range(4))
        vh, vx = at(38400, BLK, P), at(39680, BLK, CPB, P)
        sring = [at(44800 + P * n, P) for n in range(16)]
        am = [at(o, P) for o in (46848, 46976, 49280, 49408)]
        ket = [at(47104 + P * n, P) for n in range(2)]
        st0, fin = at(47360, 2, P), at(47616, 2, P)
        reset = at(47872, TOK)
        dec = at(49152, 2, TOK // CHUNK)
        ot, osq = at(29440, BLK, P), at(34560, BLK, P)
        oss, orm, orr = (at(49232 + 12 * n, BLK) for n in range(3))
        oh = at(10240, HG * TOK)

        gw = [at(20480 + 3072 * s, 24, P) for s in range(2)]
        mt = at(26624, DK * TOK)
        wout = at(36864, DK, D)
        gate_a = [at(45056 + 1024 * s, 512) for s in range(2)]
        gate_b = [at(45568 + 1024 * s, 512) for s in range(2)]
        g1b, scb, shb = ([at(2048 * n + 1024 * g, D) for g in range(2)] for n in range(3))
        ln1gb, ln1bb = at(6144, D), at(7168, D)
        xt, zt, zn, xa, h2 = ([at(8192 + 2048 * n + 1024 * s, D) for s in range(2)] for n in range(5))
        h2T = [at(18432 + 1024 * s, DK, P) for s in range(2)]
        wrt = at(K0 + 816, DK, 32)
        stack = at(K0 + 1072, EXPERTS)
        lgt = [at(K0 + 1088 + P * s, P) for s in range(2)]
        RQ, SPLIT = 80, 4
        affp = [at(49408 + RQ * s, RQ) for s in range(2)]
        st5 = at(49568, 64)
        ex5 = at(49632, EXPERTS)
        aff = [at(45056 + 512 * s, SPLIT * P) for s in range(2)]
        topv, topi, topf = at(46080, P), at(46208, P), at(46336, P)
        topr = at(46464, 2, P)
        tsel = at(46720, 6, EXPERTS)
        gates, rowi = at(46816, 48), at(46864, 48)
        slots = [20480, 22528, 24576, 47104] + [26624 + 2048 * n for n in range(8)]
        wslot = [at(o, DK, UNIT) for o in slots]
        xl, xc, xeT = at(0, D), at(1024, D), at(2048, DK, CAP)
        hid, yt = at(3328, DK, CAP), at(4608, DK, CAP)
        slu = [at(5888 + CAP * s, CAP) for s in range(2)]
        yl, yc = at(6400, D), at(7424, D)
        idx_g, idx_s, gate_s = at(49696, 2), at(49700, 2), at(49704, 2)
        ln2gb, ln2bb = at(10240, D), at(11264, D)
        rows8, zt8 = ([at(20480 + 10240 * n + 1024 * b, D) for b in range(BLK)] for n in range(2))
        st8 = at(49712, BLK * 18)
        g2row = at(49800, P)

        vec_in, tab_in = sem("vec_in"), sem("tab_in")
        memsets = sem("memsets")
        vrow_t, vcol_rd, scond_rd = sem("vrow_transposed"), sem("vcol_ready"), sem("scond_ready")
        ring_in = [sem(f"ring_in{s}") for s in range(4)]
        unit_used = sem("unit_used")
        mod_rd = sem("mod_ready")
        xin_in = [sem(f"xin_in{s}") for s in range(5)]
        ar_mm, ar_rd, ar_t = sem("ada_rows_matmuls"), sem("ada_rows_ready"), sem("ada_rows_transposed")
        xt_done, h_dve, h_act = sem("x_transposed"), sem("h_by_dve"), sem("h_by_act")
        dve_chain, act_chain, pool_chain = sem("dve_chain"), sem("act_chain"), sem("pool_chain")
        pr_mm, pr_dve, pr_act, ssq_mm, rs_read = (sem(n) for n in (
            "proj_matmuls", "proj_by_dve", "proj_squared", "ssq_matmuls", "ssq_read"))
        rs_rd = sem("rstd_ready")
        wkpe_in, cache_in, wukv_in = sem("wkpe_in"), sem("cache_in"), sem("wukv_in")
        ex_mm, ex_dve = sem("extra_matmuls"), sem("extra_by_dve")
        outs = sem("stores_done")
        qm_rd = sem("query_factors_ready")

        wq_in, q_mm, q_rd = sem("wq_in"), sem("q_proj_matmuls"), sem("q_ready")
        k_mm, k_act, k_dve = sem("k_proj_matmuls"), sem("k_by_act"), sem("k_by_dve")
        s_mm, nb_rd, p_rd, t_mm = sem("score_matmuls"), sem("neg_max_ready"), sem("probs_ready"), sem("probs_transposed")
        pt_dve, pt_act, pv_mm, o_ev = sem("probsT_by_dve"), sem("probsT_by_act"), sem("pv_matmuls"), sem("o_evacuated")
        wv_in, v_mm, v_ev, wsw_rd = sem("value_weights_in"), sem("value_matmuls"), sem("values_ready"), sem("swapped_ready")
        au_in, au_mm, au_ev, ar_out = [sem(f"ada_in{n}") for n in range(4)], sem("ada_matmuls"), sem("ada_copied"), sem("ada_rows_stored")
        vo_rd = sem("values_ones")
        br_in = sem("ada_bias_in")
        hw_in = [sem(f"head_weights_in{n}") for n in range(5)]
        st_in, s_init, fin_rd, fin_out = sem("state_in"), sem("state_taken"), sem("final_ready"), sem("final_stored")
        hp_mm, hp_act, ln_rd, cs_rd, e_rd, hg_rd, vx_rd = (sem(n) for n in (
            "head_proj_matmuls", "head_proj_by_act", "logf_ready", "cumsum_ready", "exp_ready",
            "decayed_ready", "vx_ready"))
        kt_mm, a_mm, u_mm, oo_mm = sem("kend_transposed"), sem("a_matmuls"), sem("u_matmuls"), sem("o_matmuls")
        ket_rd, am_rd, st_rd, u_free, of_ev, ob_ev = (sem(n) for n in (
            "ket_ready", "am_ready", "states_ready", "u_read", "o_fwd_evacuated", "o_bwd_added"))
        sq_rd, rms_rd, ot_mm, oh_rd = sem("head_normed"), sem("head_rms"), sem("head_transposed"), sem("head_out")

        gw_in, GW0 = au_in[0:2], 16 * HEADS
        x_in, XIN0, HW0 = xin_in[0:2], 16, 16

        def tokens_in_sem(b):
            return xin_in[b] if b < 5 else hw_in[b - 5]

        def rows_in(b):
            if b < 5:
                return xin_in[b], XIN0 + (16 * (BLK // 2) if b < 2 else 0)
            return hw_in[b - 5], HW0 + 16 * HG

        mg_mm, mg_sig, mg_ev = sem("merge_matmuls"), sem("merge_gates"), sem("merged")
        wout_in, bc_in = sem("wout_in"), sem("broadcasts_in")
        wo_mm, z_rd, z_sum, var_rd, sd_rd, nm_rd, zn_rd, zg_rd, x1_rd = (sem(n) for n in (
            "out_proj_matmuls", "mix_read", "z_summed", "variance_ready", "deviation_ready", "norm_scale_ready",
            "normed", "norm_gained", "x1_ready"))
        hs_rd, h2_rd, xa_rd, pads = sem("h2_scaled"), sem("h2_ready"), sem("xa_ready"), sem("paddings")
        h2_out, acc_out = [sem(f"h2_stored{n}") for n in range(2)], [sem(f"acc_stored{n}") for n in range(2)]
        ht_mm, ht_ev, lg_mm, lmax_rd, lexp_rd, af_rd, af_mm, af_ev = (sem(n) for n in (
            "h2_transposed", "h2T_ready", "logits_matmuls", "logits_max", "logits_exp", "affinity_ready",
            "affinity_transposed", "affinity_in_rows"))
        lt_mm, lt_rd = sem("logit_shares_matmuls"), sem("logit_shares_ready")
        top_rd, top_mm, top_ev = sem("top_ready"), sem("top_transposed"), sem("top_columns")
        w_in_sem = [sem(f"expert_weights_in{n}") for n in range(8)]
        ix_rd, xg_in, xe_mm, xe_ev = sem("index_ready"), sem("tokens_gathered"), sem("tokens_transposed"), sem("xeT_ready")
        up_mm, sl_rd, hid_ev, dn_mm = sem("up_matmuls"), sem("silu_ready"), sem("hidden_ready"), sem("down_matmuls")
        yt_act, yt_dve, yb_mm, gs_rd = sem("yt_by_act"), sem("yt_by_dve"), sem("y_transposed"), sem("gates_taken")
        yl_rd, yc_rd, sc_out = sem("latents_y_ready"), sem("context_y_ready"), sem("scattered")
        ln2_in, y_out = sem("ln2_in"), sem("y_stored")

        passed = sem("loop_waits_passed")

        block = ctx.enter_context(nc.Block())

        def chunk(t, n):
            return t[:, TCH[n][0]:TCH[n][0] + TCH[n][1]]

        W_IN = w_in[0].rearrange("(k p) n -> p k n", p=P)
        W_ADA = w_ada[0].rearrange("(k p) n -> p k n", p=P)
        W_UQ = w_uq[0].rearrange("(k p) n -> p k n", p=P)
        W_UKV = w_ukv[0].rearrange("(k p) n -> p k n", p=P)
        HCOLS = (O_HI, O_HF, O_HB, O_HQ, O_HG)
        W_OM = w_o_mla[0].rearrange("(k p) n -> p k n", p=P)
        W_OH = w_o_hg[0].rearrange("(k p) n -> p k n", p=P)
        NPR = 27

        FIRST = [*range(QT_, QT_ + KT_), None, *range(QT_)]

        def squares(pos):
            return 3 * sum(o is not None for o in FIRST[:pos])

        def pr_free(eng, i):
            j = i - 5
            if j < 0:
                return
            if j >= NPR:
                eng.wait_ge(ex_dve, j - NPR + 1)
            elif FIRST[j // 3] is None:
                eng.wait_ge(pr_dve, j + 1)
            else:
                eng.wait_ge(pr_act, squares(j // 3) + j % 3 + 1)

        QB = BLK

        ORDER = [*range(LBLK, BLK), *range(LBLK)]
        NCH = [1 if j >= LBLK else 3 for j in ORDER]
        M0 = [sum(NCH[:r]) for r in range(QB + 1)]
        CPH = M0[QB]
        HALF = CPH // 2

        def steps(d):
            return list(range(BLK)) if d == 0 else [*range(LBLK - 1, -1, -1), *range(BLK - 1, LBLK - 1, -1)]

        SEQ = [(d, b) for d in range(2) for b in steps(d)]
        NS = len(SEQ)

        def after_loop_wait(eng):
            eng.sem_inc(passed, 1)

        @block.sync
        def _(sp):
            for r, n, src in ((R_BADA, 48, b_ada.rearrange("a (r p) -> (a r) p", p=P)),
                              (R_C, 8, c.rearrange("a (r p) -> (a r) p", p=P)),
                              (R_C + 8, 8, c_ctx.rearrange("(r p) -> r p", p=P)),
                              (R_QN, 6, q_norm.rearrange("a (r p) -> (a r) p", p=P)),
                              (R_KVN, 2, kv_norm.rearrange("a (r p) -> (a r) p", p=P)),
                              (R_HN, 1, hg_norm),
                              (R_GAM, 16, gamma.rearrange("a b (r p) -> (a b r) p", p=P))):
                sp.dma_start(vrow[r:r + n, :], src).then_inc(vec_in, 16)
            sp.dma_start(ident, tables[:, 0:P]).then_inc(tab_in, 16)
            sp.dma_start(masks, tables[:, P:3 * P].rearrange("p (a b) -> p a b", b=P)).then_inc(tab_in, 16)
            sp.dma_start(rope_t[NOPE:QKD, :, :], rope).then_inc(tab_in, 16)
            sp.dma_start(rope_t[QKD:P, 0, :], rope[:, 1, :]).then_inc(tab_in, 16)

            def token_rows(b, lat, con):
                return lat[0, b * P:(b + 1) * P, :] if b < LBLK else con[0, (b - LBLK) * P:(b - LBLK + 1) * P, :]

            for s in range(4):
                sp.dma_start(ring[s], W_ADA[:, :, s * UNIT:(s + 1) * UNIT]).then_inc(ring_in[s], 16)
            for s in range(4):
                sp.wait_ge(unit_used, s + 1)
                sp.dma_start(ring[s], W_ADA[:, :, (s + 4) * UNIT:(s + 5) * UNIT]).then_inc(ring_in[s], 16)
            for b in range(BLK):
                sp.dma_start(xin[b], token_rows(b, x_sample, x_prompt)).then_inc(tokens_in_sem(b), 16)
            sp.dma_start(wkpe, W_IN[:, :, O_KPE - NOPE:O_KPE + ROPE]).then_inc(wkpe_in, 16)
            for s in (3, 0, 1, 2):
                sp.wait_ge(unit_used, s + 5)
                sp.dma_start(ring[s], W_IN[:, :, s * UNIT:(s + 1) * UNIT]).then_inc(ring_in[s], 16)
            sp.dma_start(cache_t, cache_ckv[0, 0].rearrange("(b p) f -> p b f", p=P)).then_inc(cache_in, 16)
            sp.wait_ge(memsets, 4)
            sp.dma_start(ckpe_t[:, :, NOPE:QKD],
                         cache_kpe[0, 0].rearrange("(b p) f -> p b f", p=P)).then_inc(cache_in, 16)
            def head_weights(h):
                sp.dma_start(wuq[:, :, 0:QKD], W_UQ[:, :, bass.ds(h * QKD, QKD)]).then_inc(wq_in, 16)

            def pair_weights(i):
                for s in range(2):
                    sp.dma_start(wukk[:, :, s * NOPE:(s + 1) * NOPE],
                                 W_UKV[:, :, bass.ds((2 * i + s) * (NOPE + VD), NOPE)]).then_inc(wv_in, 16)
                    sp.dma_start(wukv[:, :, s * VD:(s + 1) * VD],
                                 W_UKV[:, :, bass.ds((2 * i + s) * (NOPE + VD) + NOPE, VD)]).then_inc(wv_in, 16)

            def ada_weights(h):
                for a in range(4):
                    sp.dma_start(aslot[a], W_ADA[:, :, bass.ds((16 + 4 * h + a) * P, P)]).then_inc(au_in[a], 16)
                sp.dma_start(brow[0:1, :], b_ada[:, bass.ds((16 + 4 * h) * P, 512)]).then_inc(br_in, 16)

            head_weights(0)
            pair_weights(0)
            sp.wait_ge(unit_used, 12)
            ada_weights(0)
            sp.wait_ge(ex_dve, 4)
            sp.dma_start(new_ckv[0, 0].rearrange("(b p) f -> p b f", p=P), nck).then_inc(outs, 16)
            sp.wait_ge(ex_dve, 5)
            sp.dma_start(new_kpe[0, 0].rearrange("(b p) f -> p b f", p=P),
                         nkp[:, :, NOPE:QKD]).then_inc(outs, 16)
            sp.sem_inc(ar_out, 16)

            def ada_rows_out(h):
                sp.wait_ge(au_ev, h + 1)
                for g in range(2):
                    sp.dma_start(mod_rows[bass.ds(g * 48 + 16 + 4 * h, 4), :], arow[g:g + 97:32, :]).then_inc(ar_out, 16)

            def next_head(h):
                ada_rows_out(h)
                sp.wait_ge(au_mm, h + 1)
                ada_weights(h + 1)
                sp.wait_ge(q_mm, 3 * h + 3)
                head_weights(h + 1)

            with sp.Fori(0, HEADS // 2 - 1) as i:
                next_head(2 * i)
                next_head(2 * i + 1)
                pair_weights(i + 1)
            next_head(HEADS - 2)
            sp.sem_inc(fin_out, 16)
            sp.wait_ge(q_mm, 3 * HEADS)
            for n, col in enumerate(HCOLS[0:2]):
                sp.dma_start(hw[n], W_IN[:, :, col:col + P]).then_inc(hw_in[n], 16)
            ada_rows_out(HEADS - 1)
            sp.wait_ge(o_ev, QB * HEADS + 1)
            for n, col in list(enumerate(HCOLS))[2:]:
                sp.dma_start(hw[n], W_IN[:, :, col:col + P]).then_inc(hw_in[n], 16)
            sp.dma_start(st0, state_hgrn[0, 0, :, 0].rearrange("d k v -> k d v")).then_inc(st_in, 16)
            with sp.Fori(1, HG) as h:
                for n, col in enumerate(HCOLS):
                    sp.wait_ge(hp_mm, 15 * h - 12 + 3 * n)
                    sp.dma_start(hw[n], W_IN[:, :, bass.ds(col + h * P, P)]).then_inc(hw_in[n], 16)
                sp.wait_ge(s_init, 2 * h)
                sp.dma_start(st0, state_hgrn[0, 0, :, bass.ds(h, 1)].rearrange("d a k v -> k d (a v)"))\
                    .then_inc(st_in, 16)
                sp.wait_ge(fin_rd, 2 * h)
                sp.dma_start(new_state[0, 0, :, bass.ds(h - 1, 1)].rearrange("d a k v -> k d (a v)"), fin)\
                    .then_inc(fin_out, 16)

            def merge_weights(s, col):
                sp.dma_start(gw[s][:, 0:8, :], W_IN[:, :, bass.ds(O_GA + col, P)]).then_inc(gw_in[s], 16)
                sp.dma_start(gw[s][:, 8:16, :], W_IN[:, :, bass.ds(O_GB + col, P)]).then_inc(gw_in[s], 16)
                sp.dma_start(gw[s][:, 16:20, :], W_OM[:, :, bass.ds(col, P)]).then_inc(gw_in[s], 16)
                sp.dma_start(gw[s][:, 20:24, :], W_OH[:, :, bass.ds(col, P)]).then_inc(gw_in[s], 16)

            sp.wait_ge(hp_mm, 15 * HG)
            sp.wait_ge(hg_rd, 2 * HG)
            for s in range(2):
                merge_weights(s, s * P)
            sp.wait_ge(fin_rd, 2 * HG)
            sp.dma_start(new_state[0, 0, :, HG - 1].rearrange("d k v -> k d v"), fin).then_inc(fin_out, 16)
            sp.wait_ge(sq_rd, HG)
            sp.dma_start(wout, w_out[0].rearrange("(k p) n -> p k n", p=P)).then_inc(wout_in, 16)
            with sp.Fori(1, DK // 2) as i:
                for s in range(2):
                    sp.wait_ge(mg_mm, 6 * i + 3 * s - 3)
                    merge_weights(s, (2 * i + s) * P)

            def mod_row(g, j):
                return mod_rows[g * 48 + j * 8:g * 48 + j * 8 + 8, :].rearrange("(o a) p -> o (a p)", o=1)\
                    .to_broadcast([P, D])

            sp.wait_ge(mg_mm, 24)
            sp.wait_ge(ar_out, 32 * HEADS + 16)
            for g in range(2):
                sp.dma_start(g1b[g], mod_row(g, 2)).then_inc(bc_in, 16)
                sp.dma_start(shb[g], mod_row(g, 3)).then_inc(bc_in, 16)
                sp.dma_start(scb[g], mod_row(g, 4)).then_inc(bc_in, 16)
            for g in range(2):
                sp.dma_start(g2row[8 * g:8 * g + 8, :], mod_rows[g * 48 + 40:g * 48 + 48, :]).then_inc(bc_in, 16)
            sp.dma_start(ln1gb, ln1_g.to_broadcast([P, D])).then_inc(bc_in, 16)
            sp.dma_start(ln1bb, ln1_b.to_broadcast([P, D])).then_inc(bc_in, 16)
            sp.wait_ge(pads, 5)
            sp.dma_start(wrt[:, :, 0:EXPERTS], w_router[0].rearrange("(k p) e -> p k e", p=P)).then_inc(bc_in, 16)

            for b in range(2):
                sp.dma_start(xt[b], token_rows(b, x_sample, x_prompt)).then_inc(x_in[b], 16)
            W = [w1, w3]
            def up_src(e, u, which):
                return W[which][0, e].rearrange("(k p) n -> p k n", p=P)[:, :, u * UNIT:(u + 1) * UNIT]

            for n in range(4):
                sp.dma_start(wslot[n], up_src(0, n // 2, n % 2)).then_inc(w_in_sem[n // 2], 16)
            for b in range(BLK):
                sp.wait_ge(x1_rd, b + 1)
                sp.wait_ge(xa_rd, b + 1)
                sp.dma_start(acc_rows[b * P:(b + 1) * P, :], xa[b % 2]).then_inc(acc_out[b % 2], 16)
                sp.wait_ge(h2_rd, b + 1)
                sp.dma_start(h2_rows[b * P:(b + 1) * P, :], h2[b % 2]).then_inc(h2_out[b % 2], 16)
                if b + 2 < BLK:
                    sp.wait_ge(z_sum, b + 1)
                    sp.dma_start(xt[b % 2], token_rows(b + 2, x_sample, x_prompt)).then_inc(x_in[b % 2], 16)
            for n in range(4, 8):
                sp.dma_start(wslot[n], up_src(0, n // 2, n % 2)).then_inc(w_in_sem[n // 2], 16)
            for n in range(4):
                sp.dma_start(wslot[8 + n], w2[0, 0].rearrange("(k p) n -> p k n", p=P)
                             [:, :, n * UNIT:(n + 1) * UNIT]).then_inc(w_in_sem[4 + n], 16)
            sp.wait_ge(top_ev, 2)
            sp.dma_start(ln2gb, ln2_g.to_broadcast([P, D])).then_inc(ln2_in, 16)
            sp.dma_start(ln2bb, ln2_b.to_broadcast([P, D])).then_inc(ln2_in, 16)
            with sp.Fori(1, EXPERTS) as e:
                for n in range(8):
                    if n % 2 == 0:
                        sp.wait_ge(up_mm, 8 * e + n - 6)
                    src = W[n % 2][0, bass.ds(e, 1)].rearrange("a (k p) n -> p (a k) n", p=P)
                    sp.dma_start(wslot[n], src[:, :, (n // 2) * UNIT:(n // 2 + 1) * UNIT]).then_inc(w_in_sem[n // 2], 16)
                for n in range(4):
                    sp.wait_ge(dn_mm, 8 * e + 2 * n - 6)
                    src = w2[0, bass.ds(e, 1)].rearrange("a (k p) n -> p (a k) n", p=P)
                    sp.dma_start(wslot[8 + n], src[:, :, n * UNIT:(n + 1) * UNIT]).then_inc(w_in_sem[4 + n], 16)

            sp.wait_ge(sc_out, 32 * EXPERTS)
            for b in range(BLK):
                sp.dma_start(rows8[b], acc_rows[b * P:(b + 1) * P, :]).then_inc(rows_in(b)[0], 16)
            for b in range(BLK):
                sp.wait_ge(x1_rd, BLK + b + 1)
                sp.dma_start(token_rows(b, y_sample, y_prompt), zt8[b]).then_inc(y_out, 16)
            sp.wait_ge(y_out, 16 * BLK)
            sp.wait_ge(outs, 32)
            sp.wait_ge(fin_out, 16 * (HG + 1))

        @block.tensor
        def _(pe):
            pe.wait_ge(vec_in, 16 * 7)
            pe.wait_ge(tab_in, 16 * 4)
            pe.transpose(ps[:, 0, 0:VROWS], vrow[0:VROWS, :], ident[0:VROWS, 0:VROWS]).then_inc(vrow_t, 1)

            pe.wait_ge(scond_rd, 1)
            for half in range(2):
                for a in range(4):
                    pe.wait_ge(ring_in[a], 16 * half + 16)
                    for k in range(DK):
                        last = pe.matmul(ps[32 * a:32 * a + 2, 1, half * UNIT:(half + 1) * UNIT], scond[:, k, :],
                                         ring[a][:, k, :], start=(k == 0), stop=(k == DK - 1))
                    last.then_inc(unit_used, 1)
            pe.wait_ge(ar_rd, 1)
            for q in range(4):
                last = pe.transpose(ps[:, 0, q * P:q * P + 98], arow1[0:98, q * P:(q + 1) * P], ident[0:98, 0:98])
            last.then_inc(ar_t, 1)

            for b in range(BLK):
                pe.wait_ge(tokens_in_sem(b), 16)
                for half in range(2):
                    bank = 1 + 2 * (b % 2) + half
                    if b >= 2:
                        pe.wait_ge(h_act if half else h_dve, b - 1)
                    for q in range(4):
                        k = half * 4 + q
                        last = pe.transpose(ps[:, bank, q * P:(q + 1) * P], xin[b][:, k * P:(k + 1) * P],
                                            ident)
                    last.then_inc(xt_done, 1)

            pe.wait_ge(memsets, 1)

            def sums(pos):
                o = FIRST[pos]
                for n in range(3):
                    q = squares(pos) + n
                    pe.wait_ge(pr_act, q + 1)
                    if o < QT_:
                        pe.wait_ge(rs_read, 3)
                    pe.matmul(ps[:, 5 + n, 0:TCH[n][1]], ones, sqr[q % 3][:, 0:TCH[n][1]],
                              start=(o in (0, QT_)), stop=(o in (QT_ - 1, QT_ + KT_ - 1))).then_inc(ssq_mm, 1)

            for pos, o in enumerate(FIRST):
                if o is None:
                    pe.wait_ge(wkpe_in, 16)
                elif o % 2 == 0:
                    pe.wait_ge(ring_in[o // 2], 48)
                for n in range(3):
                    pr_free(pe, pos * 3 + n)
                    if pos == 0:
                        pe.wait_ge(h_act, min(5 * n + 4, BLK))
                        pe.wait_ge(h_dve, min(5 * n + 4, BLK))
                    out = ps[0:QKD if o is None else P, (pos * 3 + n) % 5, 0:TCH[n][1]]
                    for k in range(DK):
                        w = wkpe[:, k, :] if o is None else ring[o // 2][:, k, (o % 2) * P:(o % 2 + 1) * P]
                        last = pe.matmul(out, w, chunk(hT[:, k], n), start=(k == 0), stop=(k == DK - 1))
                    last.then_inc(pr_mm, 1)
                if o is not None and o % 2 == 1:
                    pe.wait_ge(pr_mm, pos * 3 + 3)
                    pe.sem_inc(unit_used, 1)
                if pos >= 1 and FIRST[pos - 1] is not None:
                    sums(pos - 1)

            pe.wait_ge(cache_in, 32)
            for j in range(2):
                pr_free(pe, NPR + j)
                for b in range(PBLK):
                    last = pe.transpose(ps[:, (NPR + j) % 5, b * P:(b + 1) * P],
                                        cache_t[:, b, j * P:(j + 1) * P], ident)
                last.then_inc(ex_mm, 1)
            pr_free(pe, NPR + 2)
            for b in range(PBLK):
                last = pe.transpose(ps[0:QKD, (NPR + 2) % 5, b * P:(b + 1) * P], ckpe_t[:, b, :], ident)
            last.then_inc(ex_mm, 1)
            sums(len(FIRST) - 1)

            pe.wait_ge(rs_rd, 7)
            pr_free(pe, NPR + 3)
            for b in range(2):
                for k in range(KT_):
                    last = pe.transpose(ps[:, (NPR + 3) % 5, b * KVL + k * P:b * KVL + (k + 1) * P],
                                        ckn[:, k, LAT + PAST + b * P:LAT + PAST + (b + 1) * P], ident)
            last.then_inc(ex_mm, 1)
            pr_free(pe, NPR + 4)
            for b in range(2):
                last = pe.transpose(ps[:, (NPR + 4) % 5, b * QKD:(b + 1) * QKD],
                                    kpc[0:QKD, b * P:(b + 1) * P], ident[0:QKD, 0:QKD])
            last.then_inc(ex_mm, 1)

            pe.wait_ge(ex_dve, 5)
            with pe.Fori(0, HEADS // 2) as i:
                pe.wait_ge(wv_in, 64 * i + 64)
                for kb in range(KEYS // P):
                    for k in range(KT_):
                        last = pe.matmul(ps[:, kb // 4, (kb % 4) * P:(kb % 4 + 1) * P],
                                         ckn[:, k, kb * P:(kb + 1) * P], wukv[:, k, :],
                                         start=(k == 0), stop=(k == KT_ - 1))
                    if kb % 4 == 3:
                        last.then_inc(v_mm, 1)
                for k in range(KT_):
                    last = pe.matmul(ps[:, 3, 256:512], wukk[:, k, :], ckn[:, k, LAT + PAST:KEYS],
                                     start=(k == 0), stop=(k == KT_ - 1))
                last.then_inc(v_mm, 1)
                pe.wait_ge(rs_read, 6)
                for n in range(3):
                    for k in range(KT_):
                        last = pe.matmul(ps[:, (4, 6, 7)[n], :], wukk[:, k, :], ckn[:, k, n * 512:(n + 1) * 512],
                                         start=(k == 0), stop=(k == KT_ - 1))
                    last.then_inc(k_mm, 1)
                for s in range(2):
                    h = 2 * i + s
                    def ada_rows():
                        pe.wait_ge(o_ev, QB * h + 1)
                        for a in range(4):
                            pe.wait_ge(au_in[a], 16 * h + 16)
                        pe.wait_ge(br_in, 16 * h + 16)
                        for k in range(DK):
                            for a in range(4):
                                pe.matmul(ps[32 * a:32 * a + 2, 5, 0:P], scond[:, k, :], aslot[a][:, k, :],
                                          start=(k == 0), stop=False)
                        for a in range(4):
                            last = pe.matmul(ps[32 * a:32 * a + 2, 5, 0:P], ones[0:1, 0:2],
                                             brow[0:1, a * P:(a + 1) * P], start=False, stop=True)
                        last.then_inc(au_mm, 1)

                    def queries(n):
                        bank = (3, 4, 2)[n]
                        if s == 0:
                            if n == 2:
                                pe.wait_ge(v_ev, 4 * i + 3)
                            else:
                                pe.wait_ge(v_ev, 4 * i + 4)
                                pe.wait_ge(k_act, 2 * i + n + 1)
                        for k in range(QT_):
                            last = pe.matmul(ps[:, bank, 0:TCH[n][1]], wuq[:, k, :], chunk(cq[k], n),
                                             start=(k == 0), stop=(k == QT_ - 1))
                        last.then_inc(q_mm, 1)

                    def scores(r, c):
                        m, j = M0[r] + c, ORDER[r]
                        if m == 0:
                            pe.wait_ge(q_rd, 3 * h + 1)
                            pe.wait_ge(qm_rd, 2)
                            pe.wait_ge(k_act, 2 * i + 2)
                            pe.wait_ge(k_dve, i + 1)
                        if m == 2:
                            pe.wait_ge(q_rd, 3 * h + 2)
                        if m == 4:
                            pe.wait_ge(q_rd, 3 * h + 3)
                        if m >= 5:
                            pe.wait_ge(p_rd, CPH * h + m - 4)
                        w, lo = (512, c * 512) if j < LBLK else (CTX, LAT + PAST)
                        pe.matmul(ps[:, m % 5, 0:w], qT[:, j * P:(j + 1) * P], kT[s][:, lo:lo + w],
                                  start=True, stop=True).then_inc(s_mm, 1)

                    def turned(r, c):
                        m = M0[r] + c
                        pe.wait_ge(p_rd, CPH * h + m + 1)
                        pe.wait_ge(pt_act if m % 2 else pt_dve, HALF * h + m // 2 + 1)
                        for q in range(4 if NCH[r] == 3 else 2):
                            last = pe.transpose(ps[:, 6 + m % 2, q * P:(q + 1) * P],
                                                prob[r % 2][:, (c * 4 + q) * P:(c * 4 + q + 1) * P], ident)
                        last.then_inc(t_mm, 1)

                    def weighted(r, c):
                        m = M0[r] + c
                        if c == 0:
                            if r == 0:
                                pe.wait_ge(au_ev, h + 1)
                            pe.wait_ge(o_ev, QB * h + r + 1)
                        pe.wait_ge(pt_act if m % 2 else pt_dve, HALF * h + m // 2 + 2)
                        n = 4 if NCH[r] == 3 else 2
                        for q in range(n):
                            vb = 4 * c + q if n == 4 else LBLK + PBLK + q
                            end = c == NCH[r] - 1 and q == n - 1
                            last = pe.matmul(ps[:, 5, 0:P], vhead[s][:, vb, :], probT[r % 2][:, 4 * c + q, :],
                                             start=(c == 0 and q == 0), stop=end)
                        if end:
                            last.then_inc(pv_mm, 1)

                    pe.wait_ge(wsw_rd, h + 1)
                    queries(2)
                    queries(0)
                    scores(0, 0)
                    ada_rows()
                    for r in range(QB):
                        ahead = NCH[r + 1] if r + 1 < QB else 0
                        for c in range(min(ahead, 2)):
                            scores(r + 1, c)
                        turned(r, 0)
                        if ahead == 3:
                            scores(r + 1, 2)
                        if NCH[r] == 3:
                            turned(r, 1)
                            weighted(r, 0)
                            turned(r, 2)
                            weighted(r, 1)
                            weighted(r, 2)
                        else:
                            if r == 0:
                                queries(1)
                            weighted(r, 0)

            pe.sem_inc(oo_mm, 2)

            def values(h):
                pe.wait_ge(hw_in[0], HW0 + 16 * h + 16)
                for n in range(3):
                    if n == 2 and not isinstance(h, int):
                        pe.wait_ge(ob_ev, BLK * h)
                    for b in range(4 * n, min(4 * n + 4, BLK)):
                        for k in range(DK):
                            last = pe.matmul(ps[:, (1, 2, 0)[n], (b % 4) * P:(b % 4 + 1) * P],
                                             hT[:, k, b * P:(b + 1) * P], hw[0][:, k, :],
                                             start=(k == 0), stop=(k == DK - 1))
                    last.then_inc(hp_mm, 1)

            def head(h, more):
                for m in range(1, 5):
                    pe.wait_ge(hw_in[m], HW0 + 16 * h + 16)
                    for n in range(3):
                        if m == 1:
                            if n == 2:
                                pe.wait_ge(oh_rd, 3 * h + 3)
                        else:
                            pe.wait_ge(hp_act, 15 * h + (3 if m == 2 else 3 * (m - 2) + n + 1))
                        for k in range(DK):
                            last = pe.matmul(ps[:, 3 * (m % 2) + n, 0:TCH[n][1]], hw[m][:, k, :],
                                             chunk(hT[:, k], n), start=(k == 0), stop=(k == DK - 1))
                        last.then_inc(hp_mm, 1)

                def products(s):
                    d, b = SEQ[s]
                    blk = slice(b * P, (b + 1) * P)
                    pe.wait_ge(ket_rd, NS * h + s + 1)
                    pe.transpose(ps[:, 6 + s % 2, 0:P], ke[d][:, blk], ident).then_inc(kt_mm, 1)
                    pe.wait_ge(am_rd, NS * h + s + 1)
                    pe.matmul(ps[:, 1 + s % 2, 0:P], kd[d][:, blk], ed[d][:, blk],
                              start=True, stop=True).then_inc(a_mm, 1)

                def update(s):
                    b = SEQ[s][1]
                    pe.wait_ge(ket_rd, NS * h + s + 3)
                    pe.wait_ge(u_free, NS * h + s + 1)
                    pe.matmul(ps[:, 3 + s % 2, :], ket[s % 2], vx[:, b].rearrange("p c v -> p (c v)"),
                              start=True, stop=True).then_inc(u_mm, 1)

                pe.wait_ge(hp_act, 15 * h + 15)
                pe.wait_ge(hg_rd, 2 * h + 1)
                pe.wait_ge(vx_rd, 4 * h + 4)
                products(0)
                products(1)
                update(0)
                for s in range(NS):
                    d, b = SEQ[s]
                    if s + 2 == BLK:
                        pe.wait_ge(hg_rd, 2 * h + 2)
                    if s + 2 < NS:
                        products(s + 2)
                    if s + 1 < NS:
                        update(s + 1)
                    pe.wait_ge(am_rd, NS * h + s + 3)
                    pe.wait_ge(st_rd, NS * h + s + 1)
                    if 2 <= s < BLK + 2:
                        pe.wait_ge(of_ev, BLK * h + s - 1)
                    elif s >= BLK + 2:
                        pe.wait_ge(ob_ev, BLK * h + s - BLK - 1)
                    ob = 0 if s % 2 else 5
                    pe.matmul(ps[:, ob, 0:P], am[s % 4], vh[:, b, :], start=True, stop=False)
                    for p in range(CPB):
                        cc = p if d == 0 else CPB - 1 - p
                        last = pe.matmul(ps[cc * CHUNK:(cc + 1) * CHUNK, ob, 0:P],
                                         ed[d][:, b * P + cc * CHUNK:b * P + (cc + 1) * CHUNK],
                                         sring[(4 * s + p) % 16], start=False, stop=True)
                    last.then_inc(oo_mm, 1)
                if more:
                    values(h + 1)
                    outputs(h)

            def outputs(h):
                pe.wait_ge(sq_rd, h + 1)
                for n in range(3):
                    for b in range(4 * n, min(4 * n + 4, BLK)):
                        last = pe.transpose(ps[:, (6, 7, 5)[n], (b % 4) * P:(b % 4 + 1) * P], ot[:, b, :], ident)
                    last.then_inc(ot_mm, 1)

            values(0)
            pe.wait_ge(o_ev, QB * HEADS + 1)
            with pe.Fori(0, HG - 1) as h:
                head(h, True)
            head(HG - 1, False)

            pe.wait_ge(ob_ev, BLK * HG)
            def merge(i, first):
                for s in range(2):
                    pe.wait_ge(gw_in[s], GW0 + 64 * i + 64)
                    for n in range(3):
                        u = 3 * s + n
                        bank = 4 * (u % 2)
                        w = TCH[n][1]
                        pe.wait_ge(mg_ev, 6 * i + u + 1)
                        for q in range(2):
                            for k in range(DK):
                                pe.matmul(ps[:, bank + q, 0:w], gw[s][:, 8 * q + k, :], chunk(hT[:, k], n),
                                          start=(k == 0), stop=(k == DK - 1))
                        if first and u == 0:
                            outputs(HG - 1)
                        for k in range(HG):
                            pe.matmul(ps[:, bank + 2, 0:w], gw[s][:, 16 + k, :], om[:, k * TOK + TCH[n][0]:k * TOK + TCH[n][0] + w],
                                      start=(k == 0), stop=(k == HG - 1))
                        pe.wait_ge(oh_rd, 3 * HG + 3)
                        for k in range(HG):
                            last = pe.matmul(ps[:, bank + 3, 0:w], gw[s][:, 20 + k, :],
                                             oh[:, k * TOK + TCH[n][0]:k * TOK + TCH[n][0] + w],
                                             start=(k == 0), stop=(k == HG - 1))
                        last.then_inc(mg_mm, 1)

            merge(0, True)
            with pe.Fori(1, DK // 2) as i:
                merge(i, False)

            mtk = mt.rearrange("p (k t) -> p k t", t=TOK)
            pe.wait_ge(mg_ev, 25)
            pe.wait_ge(wout_in, 16)

            def h2_transposed(b):
                if b == 0:
                    pe.wait_ge(mg_ev, 26)
                pe.wait_ge(h2_rd, b + 1)
                if b >= 1:
                    pe.wait_ge(ht_ev, b)
                for k in range(DK):
                    last = pe.transpose(ps[:, 4 + k // 4, (k % 4) * P:(k % 4 + 1) * P],
                                        h2[b % 2][:, k * P:(k + 1) * P], ident)
                last.then_inc(ht_mm, 1)

            def logit_shares(b):
                pe.wait_ge(ht_ev, b + 1)
                if b >= 1:
                    pe.wait_ge(lexp_rd, b)
                else:
                    pe.wait_ge(bc_in, 16 * 11)
                for k in range(DK):
                    j = 32 * (k % 4)
                    last = pe.matmul(ps[j:j + 32, 6, P:2 * P], wrt[:, k, :], h2T[b % 2][:, k, :],
                                     start=(k < 4), stop=(k >= 4))
                last.then_inc(lt_mm, 1)

            def logits(b):
                if b == 0:
                    pe.wait_ge(pads, 6)
                pe.wait_ge(lt_rd, b + 1)
                pe.matmul(ps[:, 6, 0:EXPERTS], lgt[b % 2], stack, start=True, stop=True).then_inc(lg_mm, 1)

            def affinities(b):
                pe.wait_ge(af_rd, b + 1)
                if b >= 1:
                    pe.wait_ge(af_ev, b)
                pe.transpose(ps[0:RQ, 7, 0:P], affp[b % 2], ident).then_inc(af_mm, 1)

            for b in range(BLK + 3):
                if b < BLK:
                    if b >= 2:
                        pe.wait_ge(z_rd, b - 1)
                    for half in range(2):
                        for k in range(DK):
                            last = pe.matmul(ps[:, 2 * (b % 2) + half, :], mtk[:, k, b * P:(b + 1) * P],
                                             wout[:, k, half * 512:(half + 1) * 512],
                                             start=(k == 0), stop=(k == DK - 1))
                    last.then_inc(wo_mm, 1)
                if 2 <= b <= BLK + 1:
                    logit_shares(b - 2)
                if 1 <= b < BLK:
                    h2_transposed(b - 1)
                if 2 <= b <= BLK + 1:
                    logits(b - 2)
                if b == BLK:
                    h2_transposed(b - 1)
                if b >= 3:
                    affinities(b - 3)

            pe.wait_ge(top_rd, 1)
            pe.wait_ge(af_ev, BLK)
            pe.transpose(ps[:, 0, 0:RQ], topv[0:RQ, :], ident[0:RQ, 0:RQ]).then_inc(top_mm, 1)
            pe.transpose(ps[:, 1, 0:RQ], topf[0:RQ, :], ident[0:RQ, 0:RQ]).then_inc(top_mm, 1)
            pe.transpose(ps[:, 2, 0:16], g2row[0:16, :], ident[0:16, 0:16]).then_inc(top_mm, 1)

            def tokens_transposed(e):
                pe.wait_ge(xg_in, 32 * e + 32)
                for k in range(DK):
                    bank, c = 4 + k // 3, (k % 3) * CAP
                    pe.transpose(ps[:, bank, c:c + CAPL], xl[:, k * P:(k + 1) * P], ident)
                    last = pe.transpose(ps[:, bank, c + CAPL:c + CAP], xc[0:CAPC, k * P:(k + 1) * P],
                                        ident[0:CAPC, 0:CAPC])
                    if k % 3 == 2 or k == DK - 1:
                        last.then_inc(xe_mm, 1)

            def expert(e, more):
                pe.wait_ge(xe_ev, 3 * e + 3)
                pe.wait_ge(yt_act, 4 * e + 1)
                pe.wait_ge(yt_dve, 4 * e + 1)
                for f in range(DK):
                    bank, c = 2 * (f % 2), (f % 2) * P
                    if f % 2 == 0:
                        pe.wait_ge(w_in_sem[f // 2], 32 * e + 32)
                    pe.wait_ge(hid_ev, 8 * e + f + 1)
                    for q in range(2):
                        for k in range(DK):
                            last = pe.matmul(ps[:, bank + q, 0:CAP], wslot[f // 2 * 2 + q][:, k, c:c + P],
                                             xeT[:, k, :], start=(k == 0), stop=(k == DK - 1))
                    last.then_inc(up_mm, 1)
                pe.wait_ge(yl_rd, 2 * e + 1)
                pe.wait_ge(yc_rd, 2 * e + 1)
                if more:
                    tokens_transposed(e + 1)
                pe.wait_ge(hid_ev, 8 * e + 10)

                def back(d):
                    if d % 2:
                        pe.wait_ge(yt_dve, 4 * e + d // 2 + 2)
                    else:
                        pe.wait_ge(yt_act, 4 * e + d // 2 + 2)
                    c = (d % 4) * P
                    pe.transpose(ps[:, 4 + d // 4, c:c + P], yt[:, d, 0:CAPL], ident)
                    last = pe.transpose(ps[0:CAPC, 6 + d // 4, c:c + P], yt[:, d, CAPL:CAP], ident)
                    if d % 4 == 3:
                        last.then_inc(yb_mm, 1)

                for d in range(DK):
                    if d % 2 == 0:
                        pe.wait_ge(w_in_sem[4 + d // 2], 16 * e + 16)
                    if d >= 4:
                        pe.wait_ge(yt_dve if d % 2 else yt_act, 4 * e + (d - 4) // 2 + 2)
                    for k in range(DK):
                        last = pe.matmul(ps[:, d % 4, 0:CAP], wslot[8 + d // 2][:, k, (d % 2) * P:(d % 2 + 1) * P],
                                         hid[:, k, :], start=(k == 0), stop=(k == DK - 1))
                    last.then_inc(dn_mm, 1)
                    if d == 1 and more:
                        pe.wait_ge(xe_ev, 3 * e + 6)
                    if 1 <= d < DK - 2:
                        back(d - 1)
                for d in range(DK - 3, DK):
                    back(d)

            pe.wait_ge(top_ev, 2)
            tokens_transposed(0)
            with pe.Fori(0, EXPERTS // 2 - 1) as i:
                expert(2 * i, True)
                expert(2 * i + 1, True)
            expert(EXPERTS - 2, True)
            expert(EXPERTS - 1, False)

        @block.vector
        def _(dve):
            ch = Chain(dve, dve_chain)
            dve.wait_ge(vrow_t, 1)
            dve.tensor_copy(vcol[:, 0:VROWS], ps[:, 0, 0:VROWS]).then_inc(vcol_rd, 1)
            dve.wait_ge(vcol_rd, 1)
            g = vcol[:, R_GAM:R_GAM + 16].rearrange("p (a d h) -> p a d h", a=2, d=2)
            t = small.rearrange("p (n a h) -> p n a h", a=2, h=HG)
            ch.link(dve.tensor_tensor(t[:, 0], g[:, :, 1], g[:, :, 0], ALU.subtract))
            dve.tensor_copy(t[:, 1], t[:, 0]).then_inc(vcol_rd, 1)
            dve.wait_ge(scond_rd, 2)
            ch.link(dve.tensor_scalar_add(t[:, 3], t[:, 2], 1.0))
            ch.link(dve.reciprocal(lb, t[:, 3]))
            ch.link(dve.tensor_scalar(oml, lb, -1.0, 1.0, ALU.mult, ALU.add))
            ch.link(dve.tensor_scalar_mul(noml, oml, -1.0))

            dve.wait_ge(unit_used, 8)
            dve.wait_ge(pads, 1)
            for a in range(4):
                last = dve.tensor_copy(arow1[32 * a:32 * a + 2, :], ps[32 * a:32 * a + 2, 1, :])
            last.then_inc(ar_rd, 1)
            dve.wait_ge(ar_t, 1)
            for q in range(4):
                lo = 8 * (q // 2) + q % 2
                src = ps[:, 0, q * P:(q + 1) * P].rearrange("p (a r) -> p a r", r=32)
                for g in range(2):
                    ch.link(dve.tensor_tensor(modv[:, g, lo:lo + 7:2], src[:, :, g],
                                              vcol[:, R_BADA + lo:R_BADA + lo + 7:2], ALU.add))
            dve.tensor_scalar_add(modv[:, :, 8:16], modv[:, :, 8:16], 1.0).then_inc(mod_rd, 1)
            dve.wait_ge(mod_rd, 1)
            for b in range(BLK):
                gr = 0 if b < LBLK else 1
                dve.wait_ge(xt_done, 2 * b + 1)
                for q in range(4):
                    last = dve.tensor_scalar(hT[:, q, b * P:(b + 1) * P],
                                             ps[:, 1 + 2 * (b % 2), q * P:(q + 1) * P],
                                             modv[:, gr, 8 + q:9 + q], modv[:, gr, q:q + 1],
                                             ALU.mult, ALU.add)
                last.then_inc(h_dve, 1)
            for pos, o in enumerate(FIRST):
                for n in range(3):
                    i = pos * 3 + n
                    dve.wait_ge(pr_mm, i + 1)
                    lo = TCH[n][0] if n < 2 else LAT + PAST
                    if o is None:
                        if n == 2:
                            dve.tensor_copy(kpc[0:QKD, :], ps[0:QKD, i % 5, 0:CTX]).then_inc(rs_rd, 1)
                        dve.tensor_copy(kT[0][NOPE:QKD, lo:lo + TCH[n][1]],
                                        ps[NOPE:QKD, i % 5, 0:TCH[n][1]]).then_inc(pr_dve, 1)
                        continue
                    dst = chunk(cq[o], n) if o < QT_ else ckn[:, o - QT_, lo:lo + TCH[n][1]]
                    dve.tensor_scalar(dst, ps[:, i % 5, 0:TCH[n][1]], vcol[:, R_QN + o:R_QN + o + 1],
                                      None, ALU.mult).then_inc(pr_dve, 1)
                if o is None:
                    dve.wait_ge(pr_dve, 3 * pos + 3)
                    rt, kr = rtmp[NOPE:QKD, :], kT[0][NOPE:QKD, 0:LAT]
                    swap = [n ^ 1 for n in range(32)]
                    ch.link(dve.stream_shuffle(rt, kr, swap))
                    ch.link(dve.tensor_tensor(rt, rt, rope_t[NOPE:QKD, 1, :], ALU.mult))
                    ch.link(dve.tensor_tensor(kr, kr, rope_t[NOPE:QKD, 0, :], ALU.mult))
                    dve.tensor_tensor(kr, kr, rt, ALU.add).then_inc(rs_rd, 1)
                    dve.wait_ge(rs_read, 3)
                    dve.reciprocal(rsk, rsk).then_inc(rs_rd, 1)
                    dve.wait_ge(rs_rd, 3)
                    for k in range(KT_):
                        dve.tensor_tensor(ckn[:, k, 0:LAT], ckn[:, k, 0:LAT], rsk[:, 0:LAT],
                                          ALU.mult).then_inc(rs_rd, 1)
                        dve.tensor_tensor(ckn[:, k, LAT + PAST:], ckn[:, k, LAT + PAST:], rsk[:, LAT:TOK],
                                          ALU.mult).then_inc(rs_rd, 1)
            for k in range(KT_):
                dve.wait_ge(ex_mm, k + 1)
                dve.tensor_copy(ckn[:, k, LAT:LAT + PAST], ps[:, (NPR + k) % 5, :]).then_inc(ex_dve, 1)
            dve.wait_ge(ex_mm, 3)
            dve.tensor_copy(kT[0][NOPE:QKD, LAT:LAT + PAST], ps[NOPE:QKD, (NPR + 2) % 5, :]).then_inc(ex_dve, 1)
            dve.wait_ge(ex_dve, 3)
            dve.tensor_copy(kT[0][QKD:P, :], kT[0][NOPE:QKD, :]).then_inc(qm_rd, 1)
            dve.wait_ge(ex_mm, 4)
            dve.tensor_copy(nck.rearrange("p a b -> p (a b)"), ps[:, (NPR + 3) % 5, :]).then_inc(ex_dve, 1)
            dve.wait_ge(ex_mm, 5)
            dve.tensor_copy(nkp.rearrange("p a b -> p (a b)"), ps[:, (NPR + 4) % 5, 0:2 * QKD]).then_inc(ex_dve, 1)
            dve.wait_ge(rs_read, 6)
            ch.link(dve.reciprocal(qm, qm))
            dve.tensor_tensor(qm[NOPE:QKD, 0:LAT], qm[NOPE:QKD, 0:LAT], rope_t[NOPE:QKD, 0, :], ALU.mult)
            dve.memset(qm[QKD:P, LAT:TOK], 0.0)
            ch.link(dve.tensor_tensor(qm[QKD:P, 0:LAT], qm[QKD:P, 0:LAT], rope_t[QKD:P, 0, :], ALU.mult))

            dve.sem_inc(o_ev, 1)
            dve.sem_inc(pt_dve, 1)
            dve.wait_ge(outs, 32)
            with dve.Fori(0, HEADS // 2) as i:
                ch.enter(i, 2 * (3 * (QB - 2) + 2 + QB - (QB - 2)))
                for n in range(1, 3):
                    dve.wait_ge(k_mm, 3 * i + n + 1)
                    for s in range(2):
                        last = dve.tensor_copy(kT[s][0:NOPE, n * 512:(n + 1) * 512],
                                               ps[s * NOPE:(s + 1) * NOPE, 5 + n, :])
                last.then_inc(k_dve, 1)
                for s in range(2):
                    h = 2 * i + s
                    def queries_out(n, place):
                        dve.wait_ge(q_mm, 3 * h + place + 1)
                        dve.tensor_tensor(chunk(qT, n), ps[:, (3, 4, 2)[n], 0:TCH[n][1]], chunk(qm, n),
                                          ALU.mult).then_inc(q_rd, 1)

                    def chunk_max(r, c):
                        m = M0[r] + c
                        dve.wait_ge(s_mm, CPH * h + m + 1)
                        w = 512 if NCH[r] == 3 else CTX
                        o = 8 * (r % 2) + (c if NCH[r] == 3 else 3)
                        ins = dve.reduce_max(att[:, o:o + 1], ps[:, m % 5, 0:w], AX.X)
                        if c == NCH[r] - 1:
                            ch.link(ins)

                    def neg_max(r):
                        o = 8 * (r % 2)
                        if NCH[r] == 3:
                            ch.link(dve.reduce_max(att[:, o + 3:o + 4], att[:, o:o + 3], AX.X))
                        dve.tensor_scalar_mul(att[:, o + 4:o + 5], att[:, o + 3:o + 4], -SCALE).then_inc(nb_rd, 1)

                    def turned_out(r, c):
                        m = M0[r] + c
                        if c < NCH[r] and m % 2 == 0:
                            dve.wait_ge(t_mm, CPH * h + m + 1)
                            w = 4 if NCH[r] == 3 else 2
                            dve.tensor_copy(probT[r % 2][:, 4 * c:4 * c + w, :].rearrange("p a b -> p (a b)"),
                                            ps[:, 6, 0:w * P]).then_inc(pt_dve, 1)

                    queries_out(2, 0)
                    queries_out(0, 1)
                    chunk_max(0, 0)
                    neg_max(0)
                    for r in range(QB):
                        ahead = NCH[r + 1] if r + 1 < QB else 0
                        for c in range(min(ahead, 2)):
                            chunk_max(r + 1, c)
                        if ahead == 1:
                            neg_max(r + 1)
                        turned_out(r, 0)
                        if r == 0:
                            queries_out(1, 2)
                        if ahead == 3:
                            chunk_max(r + 1, 2)
                            neg_max(r + 1)
                        turned_out(r, 1)
                        turned_out(r, 2)
                        dve.wait_ge(pv_mm, QB * h + r + 1)
                        vo, so = VD * s, VD * (1 - s)
                        ch.link(dve.reciprocal(rin[vo:vo + VD, :], ps[so:so + VD, 5, 0:P]))
                        dve.tensor_tensor(om[vo:vo + VD, bass.ds(i * TOK + ORDER[r] * P, P)],
                                          ps[vo:vo + VD, 5, 0:P], rin[vo:vo + VD, :], ALU.mult).then_inc(o_ev, 1)
            ch.leave(HEADS // 2)

            dve.sem_inc(am_rd, 2)
            dve.sem_inc(u_free, 2)
            dve.sem_inc(oh_rd, 3)
            dve.sem_inc(mg_ev, 2)
            with dve.Fori(0, HG) as h:
                ch.enter(h, HLINKS)
                for d in range(2):
                    step = slice(None) if d == 0 else slice(None, None, -1)
                    dve.wait_ge(ln_rd, 2 * h + d + 1)
                    if d == 0:
                        dve.wait_ge(vx_rd, 4 * h + 4)
                    dve.tensor_tensor_scan(bd[d][:, step], reset, bd[d][:, step], 0.0,
                                           op0=ALU.mult, op1=ALU.add).then_inc(cs_rd, 1)
                    ch.link(dve.tensor_scalar(kd[d], kd[d], noml[:, d, bass.ds(h, 1)], oml[:, d, bass.ds(h, 1)],
                                              ALU.mult, ALU.add))
                    dve.wait_ge(e_rd, 4 * h + 2 * d + 2)
                    edge = CHUNK - 1 if d == 0 else 0
                    ch.link(dve.tensor_copy(dec[:, d, :], ed[d][:, edge:TOK:CHUNK]))
                    ch.link(dve.tensor_tensor(kd[d], kd[d], bd[d], ALU.mult))
                    ch.link(dve.tensor_tensor(
                        ke[d].rearrange("p (c t) -> p c t", t=CHUNK), kd[d].rearrange("p (c t) -> p c t", t=CHUNK),
                        dec[:, d, :].rearrange("p (c a) -> p c a", a=1).to_broadcast([P, TOK // CHUNK, CHUNK]),
                        ALU.mult))
                dve.wait_ge(hp_act, 15 * h + 12)
                for d in range(2):
                    dve.tensor_tensor(ed[d], ed[d], hq, ALU.mult).then_inc(hg_rd, 1)

                def scores_masked(s):
                    dve.wait_ge(a_mm, NS * h + s + 1)
                    if s >= 2:
                        dve.wait_ge(oo_mm, NS * h + s - 1)
                    dve.tensor_tensor(am[s % 4], ps[:, 1 + s % 2, 0:P], masks[:, SEQ[s][0], :],
                                      ALU.mult).then_inc(am_rd, 1)

                def add_backward(s):
                    b = SEQ[s][1]
                    dve.wait_ge(oo_mm, NS * h + s + 3)
                    dve.tensor_tensor(ot[:, b, :], ps[:, 0 if s % 2 else 5, 0:P], ot[:, b, :], ALU.add).then_inc(ob_ev, 1)

                scores_masked(0)
                dve.wait_ge(st_in, 16 * h + 16)
                for s in range(NS):
                    d, b = SEQ[s]
                    if s % BLK == 0:
                        dve.tensor_copy(sring[4 * s % 16], st0[:, d, :]).then_inc(s_init, 1)
                        dve.wait_ge(s_init, 2 * h + d + 1)
                    if s + 1 < NS:
                        scores_masked(s + 1)
                    dve.wait_ge(u_mm, NS * h + s + 1)
                    if s % BLK == BLK - 1:
                        dve.wait_ge(fin_out, 16 * h + 16)
                    for p in range(CPB):
                        cc = p if d == 0 else CPB - 1 - p
                        cur = sring[(4 * s + p) % 16]
                        nxt = sring[(4 * s + p + 1) % 16]
                        if p == CPB - 1 and s % BLK == LBLK - 1:
                            ins = dve.memset(nxt, 0.0)
                        else:
                            if p == CPB - 1 and s % BLK == BLK - 1:
                                nxt = fin[:, d, :]
                            ins = dve.scalar_tensor_tensor(
                                nxt, cur, dec[:, d, b * CPB + cc:b * CPB + cc + 1],
                                ps[:, 3 + s % 2, cc * P:(cc + 1) * P], op0=ALU.mult, op1=ALU.add)
                        if p == CPB - 2:
                            ins.then_inc(st_rd, 1)
                            dve.wait_ge(st_rd, NS * h + s + 1)
                        elif p == CPB - 1:
                            ins.then_inc(u_free, 1)
                            dve.wait_ge(u_free, NS * h + s + 3)
                        else:
                            ch.link(ins)
                    if s % BLK == BLK - 1:
                        dve.sem_inc(fin_rd, 1)
                    if s == BLK:
                        dve.wait_ge(of_ev, BLK * h + BLK)
                    if s > BLK:
                        add_backward(s - 1)
                add_backward(NS - 1)
                dve.wait_ge(rms_rd, h + 1)
                ch.link(dve.reciprocal(orr, orm))
                dve.tensor_tensor(ot, ot, orr.rearrange("p (b a) -> p b a", a=1).to_broadcast([P, BLK, P]),
                                  ALU.mult).then_inc(sq_rd, 1)
                for n in range(3):
                    dve.wait_ge(ot_mm, 3 * h + n + 1)
                    dve.scalar_tensor_tensor(oh[:, bass.ds(h * TOK + TCH[n][0], TCH[n][1])],
                                             ps[:, (6, 7, 5)[n], 0:TCH[n][1]], vcol[:, R_HN:R_HN + 1],
                                             chunk(hgate, n), op0=ALU.mult, op1=ALU.mult).then_inc(oh_rd, 1)
            ch.leave(HG)


            dve.wait_ge(oh_rd, 3 * HG + 3)
            with dve.Fori(0, DK // 2) as i:
                ch.enter(i, 12)
                for s in range(2):
                    for n in range(3):
                        u = 3 * s + n
                        w, bank = TCH[n][1], 4 * (u % 2)
                        dve.wait_ge(mg_sig, 12 * i + 2 * u + 2)
                        ga, gb = gate_a[u % 2][:, 0:w], gate_b[u % 2][:, 0:w]
                        ch.link(dve.tensor_tensor(ga, ps[:, bank + 2, 0:w], ga, ALU.mult))
                        ch.link(dve.tensor_tensor(gb, ps[:, bank + 3, 0:w], gb, ALU.mult))
                        dve.tensor_tensor(mt[:, bass.ds((2 * i + s) * TOK + TCH[n][0], w)], ga, gb,
                                          ALU.add).then_inc(mg_ev, 1)
            ch.leave(DK // 2)

            dve.wait_ge(bc_in, 16 * 11)
            dve.wait_ge(pads, 4)

            def aff_row(b):
                if b < SPLIT:
                    return 64, b * P
                return (0, (b - SPLIT) * P) if b < LBLK else (32, (b - LBLK) * P)

            def softmax(b):
                dve.wait_ge(lg_mm, b + 1)
                ch.link(dve.reduce_max(st5[:, 40:41], ps[:, 6, 0:EXPERTS], AX.X))
                dve.tensor_scalar_mul(st5[:, 41:42], st5[:, 40:41], -1.0).then_inc(lmax_rd, 1)
                if b >= BLK - 2:
                    first_rounds(2)
                dve.wait_ge(lexp_rd, b + 1)
                ch.link(dve.reciprocal(st5[:, 43:44], st5[:, 42:43]))
                c = aff_row(b)[0]
                if b >= 2:
                    dve.wait_ge(af_mm, b - 1)
                dve.tensor_scalar(affp[b % 2][:, c:c + EXPERTS], ex5, st5[:, 43:44], None,
                                  ALU.mult).then_inc(af_rd, 1)

            def rows_out(b):
                dve.wait_ge(af_mm, b + 1)
                r, c = aff_row(b)
                dve.tensor_copy(aff[0][r:r + EXPERTS, c:c + P], ps[r:r + EXPERTS, 7, 0:P]).then_inc(af_ev, 1)

            def top_round(lo, hi, w, r):
                v8, a = topv[lo:hi, 8 * r:8 * r + 8], aff[r % 2][lo:hi, 0:w]
                ch.link(dve.max(v8, a))
                if r + 1 < CAPL // 8:
                    ch.mark(dve.match_replace(aff[1 - r % 2][lo:hi, 0:w], v8, a, -2.0))
                ch.mark(dve.max_index(topi[lo:hi, 8 * r:8 * r + 8].bitcast(U32), v8, a))
                if r + 1 < CAPL // 8:
                    ch.meet(1)

            rounds = iter(range(CAPL // 8))

            def first_rounds(n):
                dve.wait_ge(af_ev, SPLIT)
                for _, r in zip(range(n), rounds):
                    top_round(64, RQ, SPLIT * P, r)

            for b in range(BLK + 3):
                if SPLIT + 3 <= b < BLK:
                    first_rounds(2)
                if b < BLK:
                    g, q = (0 if b < LBLK else 1), b % 2
                    dve.wait_ge(wo_mm, b + 1)
                    z = zt[q]
                    dve.tensor_tensor(z, ps[:, 2 * q:2 * q + 2, :].rearrange("p a b -> p (a b)"), g1b[g],
                                      ALU.mult).then_inc(z_rd, 1)
                    dve.wait_ge(z_rd, b + 1)
                    dve.wait_ge(x_in[q], XIN0 + 16 * (b // 2 + 1))
                    dve.scalar_tensor_tensor(z, xt[q], ALPHA, z, op0=ALU.mult, op1=ALU.add).then_inc(z_sum, 1)
                    dve.wait_ge(z_sum, b + 1)
                    for n in range(2):
                        last = dve.bn_stats(st5[:, 6 * n:6 * n + 6], z[:, n * 512:(n + 1) * 512])
                    ch.link(last)
                    dve.bn_aggr(st5[:, 12:14], st5[:, 0:12]).then_inc(var_rd, 1)
                    dve.wait_ge(sd_rd, b + 1)
                    ch.link(dve.reciprocal(st5[:, 15:16], st5[:, 14:15]))
                    dve.scalar_tensor_tensor(st5[:, 16:17], st5[:, 12:13], -1.0, st5[:, 15:16],
                                             op0=ALU.mult, op1=ALU.mult).then_inc(nm_rd, 1)
                    if b >= SPLIT + 3:
                        first_rounds(1)
                    dve.wait_ge(zn_rd, b + 1)
                    dve.tensor_tensor(zn[q], zn[q], ln1gb, ALU.mult).then_inc(zg_rd, 1)
                    if b >= SPLIT + 3:
                        first_rounds(1)
                    if b == BLK - 1:
                        dve.wait_ge(zg_rd, b + 1)
                        dve.tensor_tensor(zn[q], zn[q], ln1bb, ALU.add).then_inc(x1_rd, 1)
                    dve.wait_ge(x1_rd, b + 1)
                    if b >= 2:
                        dve.wait_ge(h2_out[q], 16 * (b // 2))
                        dve.wait_ge(ht_mm, b - 1)
                    dve.scalar_tensor_tensor(h2[q], scb[g], 1.0, zn[q], op0=ALU.add, op1=ALU.mult)\
                        .then_inc(hs_rd, 1)
                    if b == BLK - 1:
                        dve.wait_ge(hs_rd, b + 1)
                        dve.wait_ge(h2_rd, b)
                        dve.tensor_tensor(h2[q], h2[q], shb[g], ALU.add).then_inc(h2_rd, 1)
                if 2 <= b <= BLK + 1:
                    softmax(b - 2)
                if b >= 3:
                    rows_out(b - 3)

            first_rounds(CAPL // 8)
            dve.wait_ge(af_ev, BLK)
            for r in range(CAPL // 8):
                top_round(0, 64, (LBLK - SPLIT) * P, r)
            ch.meet()
            ch.link(dve.tensor_copy(topf[0:64, :], topi[0:64, :].bitcast(U32)))
            ch.link(dve.tensor_copy(topf[64:RQ, :], topi[64:RQ, :].bitcast(U32)))
            dve.tensor_scalar_add(topf[32:48, :], topf[32:48, :], float(LAT))
            dve.tensor_copy(topr[0:16, 0, :], topv[0:16, ::-1])
            ch.link(dve.tensor_scalar_add(topr[0:16, 1, :], topf[0:16, ::-1], float(SPLIT * P)))
            dve.tensor_copy(topv[0:16, :], topr[0:16, 0, :])
            dve.tensor_copy(topf[0:16, :], topr[0:16, 1, :]).then_inc(top_rd, 1)
            dve.wait_ge(top_mm, 3)
            dve.tensor_copy(modv[:, :, 40:48], ps[:, 2, 0:16].rearrange("p (g k) -> p g k", k=DK))
            dve.tensor_copy(gates[:, 32:48], ps[:, 0, 32:48])
            dve.tensor_copy(rowi[:, 32:48].bitcast(U32), ps[:, 1, 32:48])
            for n, (bank, c) in enumerate(((0, 64), (0, 0), (1, 64), (1, 0))):
                last = dve.tensor_copy(tsel[:, n, :], ps[:, bank, c:c + EXPERTS])
            ch.link(last)
            dve.tensor_tensor(gates[:, 0:16], tsel[:, 0, :], tsel[:, 1, :], ALU.max).then_inc(top_ev, 1)
            dve.tensor_tensor(tsel[:, 4, :], tsel[:, 0, :], tsel[:, 1, :], ALU.is_ge)
            ch.link(dve.tensor_tensor(tsel[:, 5, :], tsel[:, 2, :], tsel[:, 3, :], ALU.subtract))
            ch.link(dve.tensor_tensor(tsel[:, 5, :], tsel[:, 5, :], tsel[:, 4, :], ALU.mult))
            dve.tensor_tensor(rowi[:, 0:16].bitcast(U32), tsel[:, 5, :], tsel[:, 3, :], ALU.add).then_inc(top_ev, 1)
            dve.wait_ge(top_ev, 2)

            def take_index(e):
                ch.link(dve.tensor_copy(idx_g[:, 0:1].bitcast(U32), rowi[:, bass.ds(e, 1)].bitcast(U32)))
                dve.tensor_copy(idx_g[0:CAPC, 1:2].bitcast(U32),
                                rowi[0:CAPC, bass.ds(e + 32, 1)].bitcast(U32)).then_inc(ix_rd, 1)

            def expert(e, more):
                if more:
                    dve.wait_ge(xg_in, 32 * e + 32)
                    take_index(e + 1)
                for f in range(DK):
                    dve.wait_ge(sl_rd, 8 * e + f + 1)
                    dve.tensor_tensor(hid[:, f, :], ps[:, 2 * (f % 2) + 1, 0:CAP], slu[f % 2],
                                      ALU.mult).then_inc(hid_ev, 1)
                if not isinstance(e, int) or e:
                    dve.wait_ge(sc_out, 32 * e)
                ch.link(dve.tensor_copy(idx_s[:, 0:1].bitcast(U32), rowi[:, bass.ds(e, 1)].bitcast(U32)))
                ch.link(dve.tensor_copy(idx_s[0:CAPC, 1:2].bitcast(U32),
                                        rowi[0:CAPC, bass.ds(e + 32, 1)].bitcast(U32)))
                ch.link(dve.tensor_copy(gate_s[:, 0:1], gates[:, bass.ds(e, 1)]))
                dve.tensor_copy(gate_s[0:CAPC, 1:2], gates[0:CAPC, bass.ds(e + 32, 1)]).then_inc(gs_rd, 1)
                dve.wait_ge(gs_rd, e + 1)
                for d in range(1, DK, 2):
                    dve.wait_ge(dn_mm, 8 * e + d + 1)
                    dve.tensor_scalar(yt[:, d, 0:CAPL], ps[:, d % 4, 0:CAPL], modv[:, 0, 40 + d:41 + d], None,
                                      ALU.mult)
                    dve.tensor_scalar(yt[:, d, CAPL:CAP], ps[:, d % 4, CAPL:CAP], modv[:, 1, 40 + d:41 + d],
                                      None, ALU.mult).then_inc(yt_dve, 1)
                    if d % 4 == 1 and d > 1 or d == DK - 1:
                        half = 0 if d < DK - 1 else 1
                        dve.wait_ge(yb_mm, 2 * e + half + 1)
                        dve.tensor_scalar(yl[:, half * 512:(half + 1) * 512], ps[:, 4 + half, :],
                                          gate_s[:, 0:1], None, ALU.mult).then_inc(yl_rd, 1)

            dve.sem_inc(hid_ev, 2)
            dve.sem_inc(yt_dve, 1)
            dve.sem_inc(yl_rd, 1)
            take_index(0)
            expert(0, True)
            with dve.Fori(1, EXPERTS - 1) as e:
                ch.enter(e, 4, 1)
                expert(e, True)
            ch.leave(EXPERTS - 1)
            expert(EXPERTS - 1, False)

            def stats(b):
                o = 18 * b
                dve.wait_ge(rows_in(b)[0], rows_in(b)[1] + 16)
                for n in range(2):
                    last = dve.bn_stats(st8[:, o + 6 * n:o + 6 * n + 6], rows8[b][:, n * 512:(n + 1) * 512])
                ch.link(last)
                dve.bn_aggr(st8[:, o + 12:o + 14], st8[:, o:o + 12]).then_inc(var_rd, 1)

            def scales(b):
                o = 18 * b
                dve.wait_ge(sd_rd, BLK + b + 1)
                ch.link(dve.reciprocal(st8[:, o + 15:o + 16], st8[:, o + 14:o + 15]))
                dve.scalar_tensor_tensor(st8[:, o + 16:o + 17], st8[:, o + 12:o + 13], -1.0,
                                         st8[:, o + 15:o + 16], op0=ALU.mult, op1=ALU.mult).then_inc(nm_rd, 1)

            dve.wait_ge(ln2_in, 32)
            stats(0)
            for b in range(BLK):
                scales(b)
                if b + 1 < BLK:
                    stats(b + 1)
                dve.wait_ge(zn_rd, BLK + b + 1)
                dve.tensor_tensor(zt8[b], zt8[b], ln2gb, ALU.mult).then_inc(zg_rd, 1)

        @block.scalar
        def _(act):
            ch = Chain(act, act_chain)
            act.wait_ge(vcol_rd, 1)
            ch.link(act.activation(scond[:, :, 0], vcol[:, R_C:R_C + 8], ACT.Silu))
            act.activation(scond[:, :, 1], vcol[:, R_C + 8:R_C + 16], ACT.Silu).then_inc(scond_rd, 1)
            act.wait_ge(vcol_rd, 2)
            act.activation(small[:, 16:24], small[:, 8:16], ACT.Exp).then_inc(scond_rd, 1)
            act.wait_ge(mod_rd, 1)
            for b in range(BLK):
                gr = 0 if b < LBLK else 1
                act.wait_ge(xt_done, 2 * b + 2)
                for q in range(4):
                    k = 4 + q
                    last = act.activation(hT[:, k, b * P:(b + 1) * P],
                                          ps[:, 2 + 2 * (b % 2), q * P:(q + 1) * P], ACT.Identity,
                                          bias=modv[:, gr, k:k + 1], scale=modv[:, gr, 8 + k:9 + k])
                last.then_inc(h_act, 1)

            act.wait_ge(memsets, 2)
            def root_mean(dst, first, size):
                for n in range(3):
                    act.wait_ge(ssq_mm, first + n)
                    act.activation(chunk(dst, n), ps[:, 5 + n, 0:TCH[n][1]], ACT.Sqrt, bias=eps,
                                   scale=1.0 / size).then_inc(rs_read, 1)

            for pos, o in enumerate(FIRST):
                if o is None:
                    root_mean(rsk, 3 * KT_ - 2, KVL)
                    continue
                for n in range(3):
                    q = squares(pos) + n
                    act.wait_ge(pr_dve, 3 * pos + n + 1)
                    if q >= 3:
                        act.wait_ge(ssq_mm, q - 2)
                    act.activation(sqr[q % 3][:, 0:TCH[n][1]], ps[:, (3 * pos + n) % 5, 0:TCH[n][1]],
                                   ACT.Square).then_inc(pr_act, 1)
            root_mean(qm, 3 * (QT_ + KT_) - 2, QL)
            act.wait_ge(qm_rd, 1)
            act.activation(kT[1][NOPE:P, :], kT[0][NOPE:P, :], ACT.Copy).then_inc(qm_rd, 1)

            act.sem_inc(pt_act, 1)
            act.wait_ge(vo_rd, 2)
            with act.Fori(0, HEADS // 2) as i:
                for n in range(4):
                    act.wait_ge(v_mm, 4 * i + n + 1)
                    w = 4 if n < 3 else 2
                    for s in range(2):
                        src = ps[:, n, 0:w * P].rearrange("p (a b) -> p a b", b=P)[:, :, s * VD:(s + 1) * VD]
                        last = act.activation(vhead[s][:, 4 * n:4 * n + w, s * VD:(s + 1) * VD], src, ACT.Copy)
                    last.then_inc(v_ev, 1)
                for bank, lo, src in ((3, LAT + PAST, slice(256, 512)), (4, 0, slice(0, 512))):
                    if bank == 4:
                        act.wait_ge(k_mm, 3 * i + 1)
                    for s in range(2):
                        last = act.activation(kT[s][0:NOPE, lo:lo + src.stop - src.start],
                                              ps[s * NOPE:(s + 1) * NOPE, bank, src], ACT.Copy)
                    last.then_inc(k_act, 1)
                for s in range(2):
                    h = 2 * i + s
                    def probs(r):
                        o = 8 * (r % 2)
                        act.wait_ge(nb_rd, QB * h + r + 1)
                        for c in range(NCH[r]):
                            w = 512 if NCH[r] == 3 else CTX
                            act.activation(prob[r % 2][:, c * 512:c * 512 + w], ps[:, (M0[r] + c) % 5, 0:w],
                                           ACT.Exp, bias=att[:, o + 4:o + 5], scale=SCALE).then_inc(p_rd, 1)

                    probs(0)
                    act.wait_ge(au_mm, h + 1)
                    act.wait_ge(ar_out, 32 * h + 16)
                    for a in range(4):
                        last = act.activation(arow[32 * a:32 * a + 2, :], ps[32 * a:32 * a + 2, 5, 0:P], ACT.Copy)
                    last.then_inc(au_ev, 1)
                    for r in range(QB):
                        for c in range(NCH[r]):
                            m = M0[r] + c
                            if m % 2:
                                act.wait_ge(t_mm, CPH * h + m + 1)
                                w = 4 if NCH[r] == 3 else 2
                                act.activation(probT[r % 2][:, 4 * c:4 * c + w, :].rearrange("p a b -> p (a b)"),
                                               ps[:, 7, 0:w * P], ACT.Copy).then_inc(pt_act, 1)
                        if r + 1 < QB:
                            probs(r + 1)

            act.sem_inc(ket_rd, 2)
            with act.Fori(0, HG) as h:
                ch.enter(h, 1)
                def proj(m, dst, func):
                    banks = (1, 2, 0) if m == 0 else range(3 * (m % 2), 3 * (m % 2) + 3)
                    for n in range(3):
                        act.wait_ge(hp_mm, 15 * h + 3 * m + n + 1)
                        act.activation(chunk(dst, n), ps[:, banks[n], 0:TCH[n][1]], func).then_inc(hp_act, 1)

                def decays(d):
                    act.wait_ge(cs_rd, 2 * h + d + 1)
                    act.activation(ed[d], bd[d], ACT.Exp).then_inc(e_rd, 1)
                    act.activation(bd[d], bd[d], ACT.Exp, scale=-1.0).then_inc(e_rd, 1)

                def log_f(d):
                    act.wait_ge(hp_act, 15 * h + 6 + 3 * d)
                    act.activation(bd[d], kd[d], ACT.Ln, bias=lb[:, d, bass.ds(h, 1)],
                                   scale=oml[:, d, bass.ds(h, 1)]).then_inc(ln_rd, 1)

                proj(0, vh.rearrange("p b v -> p (b v)"), ACT.Copy)
                proj(1, kd[0], ACT.Sigmoid)
                log_f(0)
                decays(0)
                proj(2, kd[1], ACT.Sigmoid)
                log_f(1)
                decays(1)
                proj(3, hq, ACT.Silu)
                act.wait_ge(oh_rd, 3 * h + 3)
                proj(4, hgate, ACT.Silu)

                def keys_out(s):
                    act.wait_ge(kt_mm, NS * h + s + 1)
                    if s >= 2:
                        act.wait_ge(u_mm, NS * h + s - 1)
                    act.activation(ket[s % 2], ps[:, 6 + s % 2, 0:P], ACT.Copy).then_inc(ket_rd, 1)

                def out_forward(s):
                    act.wait_ge(oo_mm, NS * h + s + 3)
                    act.activation(ot[:, SEQ[s][1], :], ps[:, 0 if s % 2 else 5, 0:P], ACT.Copy).then_inc(of_ev, 1)

                def squares_summed(s):
                    b = SEQ[s][1]
                    act.wait_ge(ob_ev, BLK * h + s - BLK + 1)
                    return act.activation(osq[:, b, :], ot[:, b, :], ACT.Square, accum_out=oss[:, b:b + 1])

                keys_out(0)
                for s in range(NS):
                    if s + 1 < NS:
                        keys_out(s + 1)
                    if 1 <= s <= BLK:
                        out_forward(s - 1)
                    if s > BLK:
                        squares_summed(s - 1)
                ch.link(squares_summed(NS - 1))
                act.activation(orm, oss, ACT.Sqrt, bias=eps, scale=1.0 / P).then_inc(rms_rd, 1)
            ch.leave(HG)

            with act.Fori(0, DK // 2) as i:
                for u in range(6):
                    w, bank = TCH[u % 3][1], 4 * (u % 2)
                    act.wait_ge(mg_mm, 6 * i + u + 1)
                    act.activation(gate_a[u % 2][:, 0:w], ps[:, bank, 0:w], ACT.Sigmoid).then_inc(mg_sig, 1)
                    act.activation(gate_b[u % 2][:, 0:w], ps[:, bank + 1, 0:w], ACT.Sigmoid).then_inc(mg_sig, 1)

            for b in range(BLK + 3):
                if 2 <= b <= BLK + 1:
                    act.wait_ge(lt_mm, b - 1)
                    act.activation(lgt[b % 2], ps[:, 6, P:2 * P], ACT.Copy).then_inc(lt_rd, 1)
                if b < BLK:
                    q = b % 2
                    act.wait_ge(var_rd, b + 1)
                    act.activation(st5[:, 14:15], st5[:, 13:14], ACT.Sqrt, bias=eps).then_inc(sd_rd, 1)
                    act.wait_ge(nm_rd, b + 1)
                    if b >= 2:
                        act.wait_ge(hs_rd, b - 1)
                        act.wait_ge(xa_rd, b - 1)
                    act.activation(zn[q], zt[q], ACT.Identity, bias=st5[:, 16:17],
                                   scale=st5[:, 15:16]).then_inc(zn_rd, 1)
                if 1 <= b <= BLK:
                    act.wait_ge(ht_mm, b)
                    act.activation(h2T[(b - 1) % 2].rearrange("p a b -> p (a b)"),
                                   ps[:, 4:6, :].rearrange("p a b -> p (a b)"), ACT.Copy).then_inc(ht_ev, 1)
                if 2 <= b <= BLK + 1:
                    act.wait_ge(lmax_rd, b - 1)
                    if b >= 3:
                        act.wait_ge(af_rd, b - 2)
                    act.activation(ex5, ps[:, 6, 0:EXPERTS], ACT.Exp, bias=st5[:, 41:42],
                                   accum_out=st5[:, 42:43]).then_inc(lexp_rd, 1)

            def tokens_in(e):
                for n in range(3):
                    act.wait_ge(xe_mm, 3 * e + n + 1)
                    w = 3 if n < 2 else 2
                    act.activation(xeT[:, 3 * n:3 * n + w, :].rearrange("p a b -> p (a b)"),
                                   ps[:, 4 + n, 0:w * CAP], ACT.Copy).then_inc(xe_ev, 1)

            def expert(e, more):
                for f in range(DK):
                    act.wait_ge(up_mm, 8 * e + f + 1)
                    act.activation(slu[f % 2], ps[:, 2 * (f % 2), 0:CAP], ACT.Silu).then_inc(sl_rd, 1)
                if more:
                    tokens_in(e + 1)
                act.wait_ge(gs_rd, e + 1)
                for d in range(0, DK, 2):
                    act.wait_ge(dn_mm, 8 * e + d + 1)
                    act.activation(yt[:, d, 0:CAPL], ps[:, d % 4, 0:CAPL], ACT.Copy,
                                   scale=modv[:, 0, 40 + d:41 + d])
                    act.activation(yt[:, d, CAPL:CAP], ps[:, d % 4, CAPL:CAP], ACT.Copy,
                                   scale=modv[:, 1, 40 + d:41 + d]).then_inc(yt_act, 1)
                for half in range(2):
                    act.wait_ge(yb_mm, 2 * e + half + 1)
                    act.activation(yc[0:CAPC, half * 512:(half + 1) * 512], ps[0:CAPC, 6 + half, :], ACT.Copy,
                                   scale=gate_s[0:CAPC, 1:2]).then_inc(yc_rd, 1)

            act.sem_inc(yt_act, 1)
            act.sem_inc(yc_rd, 1)
            tokens_in(0)
            with act.Fori(0, EXPERTS - 1) as e:
                expert(e, True)
            expert(EXPERTS - 1, False)

            for b in range(BLK):
                o = 18 * b
                act.wait_ge(var_rd, BLK + b + 1)
                act.activation(st8[:, o + 14:o + 15], st8[:, o + 13:o + 14], ACT.Sqrt, bias=eps).then_inc(sd_rd, 1)
                act.wait_ge(nm_rd, BLK + b + 1)
                act.activation(zt8[b], rows8[b], ACT.Identity, bias=st8[:, o + 16:o + 17],
                               scale=st8[:, o + 15:o + 16]).then_inc(zn_rd, 1)

        @block.gpsimd
        def _(pool):
            pool.memset(arow1, 0.0).then_inc(pads, 1)
            pool.memset(ones, 1.0).then_inc(memsets, 1)
            pool.memset(eps, EPS).then_inc(memsets, 1)
            pool.memset(ckpe_t, 0.0).then_inc(memsets, 1)
            pool.wait_ge(memsets, 3)
            pool.sem_inc(memsets, 1)


            pool.wait_ge(pr_mm, 9)
            pool.memset(vhead[0][:, :, VD:P], 1.0).then_inc(vo_rd, 1)
            pool.memset(vhead[1][:, :, 0:VD], 1.0).then_inc(vo_rd, 1)
            with pool.Fori(0, HEADS) as h:
                pool.wait_ge(wq_in, 16 * h + 16)
                after_loop_wait(pool)
                for n in range(2):
                    last = pool.tensor_copy(wuq[:, :, QKD + n:P:2], wuq[:, :, NOPE + 1 - n:QKD:2])
                last.then_inc(wsw_rd, 1)

            pool.wait_ge(o_ev, QB * HEADS + 1)
            pool.wait_ge(ar_out, 32 * HEADS + 16)
            pool.memset(vx, 0.0).then_inc(pool_chain, 1)
            pool.memset(reset, 1.0).then_inc(pool_chain, 1)
            pool.wait_ge(pool_chain, 2)
            pool.memset(reset[:, 0:TOK:CHUNK], 0.0).then_inc(pool_chain, 1)
            pool.wait_ge(pool_chain, 3)
            with pool.Fori(0, HG) as h:
                pool.wait_ge(hp_act, 15 * h + 3)
                after_loop_wait(pool)
                for cc in range(CPB):
                    rows = slice(cc * CHUNK, (cc + 1) * CHUNK)
                    pool.tensor_copy(vx[rows, :, cc, :], vh[rows]).then_inc(vx_rd, 1)

            pool.wait_ge(mg_ev, 26)
            pool.memset(aff[0], -1.0).then_inc(pads, 1)
            for q in range(2):
                pool.memset(affp[q], 0.0).then_inc(pads, 1)
            pool.memset(wrt, 0.0).then_inc(pads, 1)
            pool.tensor_tensor(stack, ident[:, 0:EXPERTS], ident[:, 32:32 + EXPERTS], ALU.add).then_inc(pool_chain, 1)
            for j in (2, 3):
                pool.wait_ge(pool_chain, 2 + j)
                pool.tensor_tensor(stack, stack, ident[:, 32 * j:32 * j + EXPERTS], ALU.add)\
                    .then_inc(pads if j == 3 else pool_chain, 1)
            pool.wait_ge(bc_in, 16 * 11)
            for b in range(BLK):
                g, q = (0 if b < LBLK else 1), b % 2
                if b < BLK - 1:
                    pool.wait_ge(zg_rd, b + 1)
                    pool.tensor_tensor(zn[q], zn[q], ln1bb, ALU.add).then_inc(x1_rd, 1)
                    pool.wait_ge(hs_rd, b + 1)
                    pool.tensor_tensor(h2[q], h2[q], shb[g], ALU.add).then_inc(h2_rd, 1)
                pool.wait_ge(x1_rd, b + 1)
                if b >= 2:
                    pool.wait_ge(acc_out[q], 16 * (b // 2))
                pool.tensor_scalar_mul(xa[q], zn[q], ALPHA).then_inc(xa_rd, 1)

            for n in range(2):
                pool.wait_ge(h2_out[n], 16 * (BLK // 2))
                pool.wait_ge(acc_out[n], 16 * (BLK // 2))

            def gather(e):
                pool.wait_ge(ix_rd, e + 1)
                after_loop_wait(pool)
                pool.indirect_dma_start(xl, None, h2_rows, bass.IndirectOffsetOnAxis(
                    ap=idx_g[:, 0:1].bitcast(U32), axis=0)).then_inc(xg_in, 16)
                pool.indirect_dma_start(xc[0:CAPC, :], None, h2_rows, bass.IndirectOffsetOnAxis(
                    ap=idx_g[0:CAPC, 1:2].bitcast(U32), axis=0)).then_inc(xg_in, 16)

            def scatter(e):
                pool.wait_ge(gs_rd, e + 1)
                pool.wait_ge(yl_rd, 2 * e + 3)
                after_loop_wait(pool)
                pool.indirect_dma_start(acc_rows, bass.IndirectOffsetOnAxis(
                    ap=idx_s[:, 0:1].bitcast(U32), axis=0), yl, None, compute_op=ALU.add).then_inc(sc_out, 16)
                pool.wait_ge(yc_rd, 2 * e + 3)
                after_loop_wait(pool)
                pool.indirect_dma_start(acc_rows, bass.IndirectOffsetOnAxis(
                    ap=idx_s[0:CAPC, 1:2].bitcast(U32), axis=0), yc[0:CAPC, :], None,
                    compute_op=ALU.add).then_inc(sc_out, 16)

            gather(0)
            with pool.Fori(0, EXPERTS - 1) as e:
                pool.wait_ge(xe_mm, 3 * e + 3)
                gather(e + 1)
                scatter(e)
            scatter(EXPERTS - 1)

            for b in range(BLK):
                pool.wait_ge(zg_rd, BLK + b + 1)
                pool.tensor_tensor(zt8[b], zt8[b], ln2bb, ALU.add).then_inc(x1_rd, 1)


def shape_tables():
    import numpy as np
    p = np.arange(P)
    same = p[:, None] // CHUNK == p[None] // CHUNK
    masks = [(same & (p[:, None] <= p[None])), (same & (p[:, None] >= p[None]))]
    tables = np.concatenate([np.eye(P)] + masks, axis=1).astype(np.float32)
    nf = ROPE // 4
    inv = (np.float32(10000.0) ** (-np.arange(nf, dtype=np.float32) / np.float32(nf))).astype(np.float32)
    t = np.arange(LAT)
    ang = np.concatenate([(t // GRID_W).astype(np.float32)[:, None] * inv,
                          (t % GRID_W).astype(np.float32)[:, None] * inv], axis=-1)
    cos, sin = np.repeat(np.cos(ang), 2, axis=1), np.repeat(np.sin(ang), 2, axis=1)
    sin[:, 0::2] *= -1
    return tables, np.ascontiguousarray(np.stack([cos.T, sin.T], axis=1), dtype=np.float32)


_INS = ['x_prompt', 'x_sample', 'c', 'cache_ckv', 'cache_kpe', 'state_hgrn', 'c_ctx', 'w_ada', 'b_ada', 'w_in',
        'mla_q_norm', 'mla_w_uq', 'mla_kv_norm', 'mla_w_ukv', 'mla_w_o', 'hgrn_gamma', 'hgrn_norm', 'hgrn_w_o',
        'w_out', 'ln1_g', 'ln1_b', 'moe_w_router', 'moe_w1', 'moe_w3', 'moe_w2', 'ln2_g', 'ln2_b']
_OUTS = [(1, CTX, D), (1, LAT, D), (1, 1, CTX, KVL), (1, 1, CTX, ROPE), (1, 1, 2, HG, P, P)]


def kernel(**inputs):
    import numpy as _np
    import concourse.bacc as _bacc
    from concourse import mybir as _mybir
    from concourse.bass_utils import run_bass_kernel_spmd as _run

    nc = _bacc.Bacc("TRN2", target_bir_lowering=False, num_devices=1)
    arrays, args = {}, []
    tables, rope = shape_tables()
    for name, a in [(n, inputs[n]) for n in _INS] + [("tables", tables), ("rope", rope)]:
        a = _np.ascontiguousarray(a)
        arrays[f"in_{name}_dram"] = a
        args.append(nc.dram_tensor(f"in_{name}_dram", a.shape, _mybir.dt.from_np(a.dtype), kind="ExternalInput").ap())
    for i, shape in enumerate(_OUTS):
        args.append(nc.dram_tensor(f"out_{i}_dram", shape, _mybir.dt.float32, kind="ExternalOutput").ap())
    flow_step(nc, *args)
    r = _run(nc, [arrays], core_ids=[0])
    return tuple(r.results[0][f"out_{i}_dram"] for i in range(len(_OUTS)))
```
